# Optimizing a Trainium2 kernel written in Bass

```python
import math
import jax, jax.numpy as jnp
from jax import lax
import numpy as np

D_MODEL = 1024
BATCH = 1
SEQ = 256
DEPTH = 2

HEAD_DIM_A = 64
HEADS_PER_GROUP_A = 4
DIL_GROUPS = ((128, 1), (512, 4), (2048, 16))
N_HEADS_A = HEADS_PER_GROUP_A * len(DIL_GROUPS)
DA = N_HEADS_A * HEAD_DIM_A
DA_OUT = HEADS_PER_GROUP_A * HEAD_DIM_A
POOL_WINDOWS = (2, 4, 8, 16)
POOL_GROUP_DIM = 128
DB = POOL_GROUP_DIM * len(POOL_WINDOWS)
N_HEADS_C = 8
QK_NOPE = 64
QK_ROPE = 32
V_DIM = 64
Q_LORA = 384
KV_LORA = 256
DC = N_HEADS_C * V_DIM
ROPE_THETA = 10000.0
N_EXPERTS = 64
TOP_K = 8
N_GROUPS = 8
TOPK_GROUPS = 4
EXPERT_FF = 256
SHARED_FF = 256
ROUTED_SCALE = 2.5
MOE_BLOCK = 128
Q_BLOCK = 128
EPS = 1e-6
NEG = -1e30
N_IN = 3 * DA + DB + Q_LORA + KV_LORA + QK_ROPE + 3 * D_MODEL

kernel_name = 'hybrid_dilated_pool_mla_moe_adaln'

def rmsnorm(x, g):
    xf = x.astype(jnp.float32)
    y = xf * lax.rsqrt(jnp.mean(xf * xf, axis=-1, keepdims=True) + EPS)
    return (y * g.astype(jnp.float32)).astype(x.dtype)

def adaln(c, w, b):
    m = jax.nn.silu(c) @ w + b
    shift, scale, gate = jnp.split(m, 3, axis=-1)
    return shift[:, None, :], scale[:, None, :], gate[:, None, :]

def rope(x, positions):
    r = x.shape[-1]
    freqs = ROPE_THETA ** (-jnp.arange(0, r, 2, dtype=jnp.float32) / r)
    ang = positions.astype(jnp.float32)[..., None] * freqs
    if x.ndim == 4:
        ang = ang[:, :, None, :]
    cos, sin = jnp.cos(ang), jnp.sin(ang)
    xf = x.astype(jnp.float32)
    x1, x2 = xf[..., : r // 2], xf[..., r // 2:]
    return jnp.concatenate([x1 * cos - x2 * sin, x2 * cos + x1 * sin], axis=-1).astype(x.dtype)

def dilated_attention(q, k, v, dilation, n_back):
    B, S, H, Dh = q.shape
    L = S // dilation
    qb_len = math.gcd(L, Q_BLOCK)
    nb = L // qb_len
    kw_len = qb_len + n_back

    def by_residue(t):
        return t.reshape(B, L, dilation, H, Dh).transpose(0, 2, 1, 3, 4)

    qr, kr, vr = by_residue(q), by_residue(k), by_residue(v)
    pad = ((0, 0), (0, 0), (n_back, 0), (0, 0), (0, 0))
    win = jnp.arange(nb)[:, None] * qb_len + jnp.arange(kw_len)[None, :]
    kw = jnp.pad(kr, pad)[:, :, win]
    vw = jnp.pad(vr, pad)[:, :, win]
    qb = qr.reshape(B, dilation, nb, qb_len, H, Dh)
    s = jnp.einsum('brnqhe,brnkhe->brnhqk', qb, kw).astype(jnp.float32) * (Dh ** -0.5)
    dist = jnp.arange(qb_len)[:, None] + n_back - jnp.arange(kw_len)[None, :]
    kpos = (jnp.arange(nb) * qb_len)[:, None, None] + jnp.arange(kw_len)[None, None, :] - n_back
    valid = ((dist >= 0) & (dist <= n_back))[None] & (kpos >= 0)
    s = jnp.where(valid[None, None, :, None], s, NEG)
    m = jnp.max(s, axis=-1, keepdims=True)
    p = jnp.exp(s - m)
    den = jnp.sum(p, axis=-1, keepdims=True)
    o = jnp.einsum('brnhqk,brnkhe->brnqhe', (p / den).astype(v.dtype), vw)
    lse = (m + jnp.log(den))[..., 0]
    o = o.reshape(B, dilation, L, H, Dh).transpose(0, 2, 1, 3, 4).reshape(B, S, H, Dh)
    lse = lse.transpose(0, 1, 2, 4, 3).reshape(B, dilation, L, H).transpose(0, 2, 1, 3).reshape(B, S, H)
    return o, lse

def pool_mixer(u, pool_w, pool_scale):
    B, S, _ = u.shape
    ug = u.reshape(B, S, len(POOL_WINDOWS), POOL_GROUP_DIM).astype(jnp.float32)
    cs = jnp.cumsum(ug, axis=1)
    t = jnp.arange(S)
    outs = []
    for gi, w in enumerate(POOL_WINDOWS):
        csg = cs[:, :, gi]
        lag = jnp.pad(csg, ((0, 0), (w, 0), (0, 0)))[:, :S]
        cnt = jnp.minimum(t + 1, w).astype(jnp.float32)[None, :, None]
        outs.append((csg - lag) / cnt - ug[:, :, gi])
    pooled = jnp.stack(outs, axis=2).astype(u.dtype)
    mixed = jnp.einsum('bsgc,gcd->bsgd', pooled, pool_w).reshape(B, S, DB)
    return mixed * pool_scale

def mla(cq, ckv, kr, positions, cq_g, ckv_g, w_uq, w_ukv):
    B, S, _ = cq.shape
    q = (rmsnorm(cq, cq_g) @ w_uq).reshape(B, S, N_HEADS_C, QK_NOPE + QK_ROPE)
    qn, qr = q[..., :QK_NOPE], rope(q[..., QK_NOPE:], positions)
    kv = (rmsnorm(ckv, ckv_g) @ w_ukv).reshape(B, S, N_HEADS_C, QK_NOPE + V_DIM)
    kn, v = kv[..., :QK_NOPE], kv[..., QK_NOPE:]
    krr = rope(kr, positions)
    nb = S // Q_BLOCK
    scale = (QK_NOPE + QK_ROPE) ** -0.5
    kpos = jnp.arange(S)

    def blocks(t):
        return t.reshape(B, nb, Q_BLOCK, *t.shape[2:]).swapaxes(0, 1)

    def attend(args):
        i, qn_b, qr_b = args
        s = (jnp.einsum('bqhe,bkhe->bhqk', qn_b, kn) + jnp.einsum('bqhr,bkr->bhqk', qr_b, krr)).astype(jnp.float32) * scale
        qpos = i * Q_BLOCK + jnp.arange(Q_BLOCK)
        s = jnp.where(kpos[None, :] <= qpos[:, None], s, NEG)
        p = jax.nn.softmax(s, axis=-1).astype(v.dtype)
        return jnp.einsum('bhqk,bkhe->bqhe', p, v)

    o = lax.map(attend, (jnp.arange(nb), blocks(qn), blocks(qr)))
    return o.swapaxes(0, 1).reshape(B, S, DC)

def token_mixer(h, positions, w_in, pool_w, pool_scale, cq_g, ckv_g, w_uq, w_ukv, w_oa, w_ob, w_oc, w_out):
    B, S, _ = h.shape
    sizes = (DA, DA, DA, DB, Q_LORA, KV_LORA, QK_ROPE, D_MODEL, D_MODEL, D_MODEL)
    points = [int(p) for p in np.cumsum(sizes)[:-1]]
    qa, ka, va, ub, cq, ckv, kr, ga, gb, gc = jnp.split(h @ w_in, points, axis=-1)
    qa, ka, va = (t.reshape(B, S, N_HEADS_A, HEAD_DIM_A) for t in (qa, ka, va))
    outs, lses = [], []
    for g, (window, dil) in enumerate(DIL_GROUPS):
        sl = slice(g * HEADS_PER_GROUP_A, (g + 1) * HEADS_PER_GROUP_A)
        o, l = dilated_attention(qa[:, :, sl], ka[:, :, sl], va[:, :, sl], dil, window // dil)
        outs.append(o)
        lses.append(l)
    wts = jax.nn.softmax(jnp.stack(lses), axis=0)
    ya = jnp.einsum('gbsh,gbshe->bshe', wts, jnp.stack(outs).astype(jnp.float32)).reshape(B, S, DA_OUT).astype(h.dtype)
    yb = pool_mixer(ub, pool_w, pool_scale)
    yc = mla(cq, ckv, kr, positions, cq_g, ckv_g, w_uq, w_ukv)
    mix = jax.nn.sigmoid(ga) * (ya @ w_oa) + jax.nn.sigmoid(gb) * (yb @ w_ob) + jax.nn.sigmoid(gc) * (yc @ w_oc)
    return mix @ w_out

def routed_experts(h2, router_w, router_bias, w1, w3, w2):
    N, D = h2.shape
    scores = jax.nn.sigmoid((h2 @ router_w).astype(jnp.float32))
    sel = scores + router_bias.astype(jnp.float32)
    grp = sel.reshape(N, N_GROUPS, N_EXPERTS // N_GROUPS)
    grp_score = lax.top_k(grp, 2)[0].sum(-1)
    top_g = lax.top_k(grp_score, TOPK_GROUPS)[1]
    gmask = jax.nn.one_hot(top_g, N_GROUPS, dtype=jnp.float32).sum(1) > 0
    emask = jnp.repeat(gmask, N_EXPERTS // N_GROUPS, axis=1)
    _, idx = lax.top_k(jnp.where(emask, sel, NEG), TOP_K)
    wk = jnp.take_along_axis(scores, idx, axis=1)
    wk = wk / jnp.sum(wk, axis=-1, keepdims=True) * ROUTED_SCALE
    M = N * TOP_K
    flat_e = idx.reshape(-1).astype(jnp.int32)
    flat_tok = jnp.arange(M, dtype=jnp.int32) // TOP_K
    flat_w = wk.reshape(-1)
    order = jnp.argsort(flat_e)
    se = flat_e[order]
    counts = jnp.bincount(flat_e, length=N_EXPERTS)
    padded = (counts + MOE_BLOCK - 1) // MOE_BLOCK * MOE_BLOCK
    start = jnp.cumsum(counts) - counts
    pend = jnp.cumsum(padded)
    pstart = pend - padded
    dest = jnp.arange(M, dtype=jnp.int32) - start[se] + pstart[se]
    P = (M + MOE_BLOCK - 1) // MOE_BLOCK * MOE_BLOCK + N_EXPERTS * MOE_BLOCK
    nblk = P // MOE_BLOCK
    slot_tok = jnp.full((P,), N, jnp.int32).at[dest].set(flat_tok[order])
    slot_w = jnp.zeros((P,), h2.dtype).at[dest].set(flat_w[order].astype(h2.dtype))
    blk_e = jnp.minimum(jnp.searchsorted(pend, jnp.arange(nblk) * MOE_BLOCK, side='right'), N_EXPERTS - 1)
    x_pad = jnp.concatenate([h2, jnp.zeros((1, D), h2.dtype)], axis=0)

    def run(args):
        e, tok, w = args
        xb = x_pad[tok]
        y = (jax.nn.silu(xb @ w1[e]) * (xb @ w3[e])) @ w2[e]
        return y * w[:, None]

    ys = lax.map(run, (blk_e, slot_tok.reshape(nblk, MOE_BLOCK), slot_w.reshape(nblk, MOE_BLOCK)))
    out = jnp.zeros((N + 1, D), h2.dtype).at[slot_tok].add(ys.reshape(P, D))
    return out[:N]

def channel_mixer(h, router_w, router_bias, w1, w3, w2, sh_w1, sh_w3, sh_w2):
    B, S, D = h.shape
    h2 = h.reshape(B * S, D)
    shared = (jax.nn.silu(h2 @ sh_w1) * (h2 @ sh_w3)) @ sh_w2
    return (shared + routed_experts(h2, router_w, router_bias, w1, w3, w2)).reshape(B, S, D)

def setup_inputs(seed: int = 0) -> dict:
    key = jax.random.key(seed)
    ks = jax.random.split(key, 32)
    f32 = jnp.float32
    L = DEPTH

    def nrm(k, shape, fan_in, scale=1.0):
        return jax.random.normal(k, shape, f32) * (scale * fan_in ** -0.5)

    def gain(k, shape):
        return 1.0 + 0.05 * jax.random.normal(k, shape, f32)

    x = jax.random.normal(ks[0], (BATCH, SEQ, D_MODEL), f32)
    c = jax.random.normal(ks[1], (BATCH, D_MODEL), f32)
    positions = (jnp.arange(SEQ, dtype=jnp.int32)[None, :] + jax.random.randint(ks[2], (BATCH, 1), 0, 4096)).astype(jnp.int32)
    return {
        'x': x,
        'c': c,
        'positions': positions,
        'ada_mix_w': nrm(ks[3], (L, D_MODEL, 3 * D_MODEL), D_MODEL, 0.5),
        'ada_mix_b': 0.02 * jax.random.normal(ks[4], (L, 3 * D_MODEL), f32),
        'norm_mix_g': gain(ks[5], (L, D_MODEL)),
        'w_in': nrm(ks[6], (L, D_MODEL, N_IN), D_MODEL),
        'pool_w': nrm(ks[7], (L, len(POOL_WINDOWS), POOL_GROUP_DIM, POOL_GROUP_DIM), POOL_GROUP_DIM),
        'pool_scale': gain(ks[8], (L, DB)),
        'cq_norm_g': gain(ks[9], (L, Q_LORA)),
        'ckv_norm_g': gain(ks[10], (L, KV_LORA)),
        'w_uq': nrm(ks[11], (L, Q_LORA, N_HEADS_C * (QK_NOPE + QK_ROPE)), Q_LORA),
        'w_ukv': nrm(ks[12], (L, KV_LORA, N_HEADS_C * (QK_NOPE + V_DIM)), KV_LORA),
        'w_oa': nrm(ks[13], (L, DA_OUT, D_MODEL), DA_OUT),
        'w_ob': nrm(ks[14], (L, DB, D_MODEL), DB),
        'w_oc': nrm(ks[15], (L, DC, D_MODEL), DC),
        'w_out': nrm(ks[16], (L, D_MODEL, D_MODEL), D_MODEL),
        'ada_ffn_w': nrm(ks[17], (L, D_MODEL, 3 * D_MODEL), D_MODEL, 0.5),
        'ada_ffn_b': 0.02 * jax.random.normal(ks[18], (L, 3 * D_MODEL), f32),
        'norm_ffn_g': gain(ks[19], (L, D_MODEL)),
        'router_w': nrm(ks[20], (L, D_MODEL, N_EXPERTS), D_MODEL),
        'router_bias': 0.01 * jax.random.normal(ks[21], (L, N_EXPERTS), f32),
        'exp_w1': nrm(ks[22], (L, N_EXPERTS, D_MODEL, EXPERT_FF), D_MODEL),
        'exp_w3': nrm(ks[23], (L, N_EXPERTS, D_MODEL, EXPERT_FF), D_MODEL),
        'exp_w2': nrm(ks[24], (L, N_EXPERTS, EXPERT_FF, D_MODEL), EXPERT_FF),
        'sh_w1': nrm(ks[25], (L, D_MODEL, SHARED_FF), D_MODEL),
        'sh_w3': nrm(ks[26], (L, D_MODEL, SHARED_FF), D_MODEL),
        'sh_w2': nrm(ks[27], (L, SHARED_FF, D_MODEL), SHARED_FF),
        'final_g': gain(ks[28], (D_MODEL,)),
    }

def reference(x, c, positions, ada_mix_w, ada_mix_b, norm_mix_g, w_in, pool_w, pool_scale, cq_norm_g, ckv_norm_g, w_uq, w_ukv, w_oa, w_ob, w_oc, w_out, ada_ffn_w, ada_ffn_b, norm_ffn_g, router_w, router_bias, exp_w1, exp_w3, exp_w2, sh_w1, sh_w3, sh_w2, final_g):
    for l in range(DEPTH):
        shift, scale, gate = adaln(c, ada_mix_w[l], ada_mix_b[l])
        h = rmsnorm(x, norm_mix_g[l]) * (1.0 + scale) + shift
        x = x + gate * token_mixer(h, positions, w_in[l], pool_w[l], pool_scale[l], cq_norm_g[l], ckv_norm_g[l], w_uq[l], w_ukv[l], w_oa[l], w_ob[l], w_oc[l], w_out[l])
        shift, scale, gate = adaln(c, ada_ffn_w[l], ada_ffn_b[l])
        h = rmsnorm(x, norm_ffn_g[l]) * (1.0 + scale) + shift
        x = x + gate * channel_mixer(h, router_w[l], router_bias[l], exp_w1[l], exp_w3[l], exp_w2[l], sh_w1[l], sh_w3[l], sh_w2[l])
    return rmsnorm(x, final_g)


_drawn_inputs = setup_inputs


def setup_inputs(seed=0):
    import zlib

    import numpy as np

    out = dict(_drawn_inputs(seed))
    spreads = {}
    factors = {'cq_norm_g': 4.77, 'ckv_norm_g': 2.894}
    for name, (base, spread) in spreads.items():
        noise = np.random.default_rng([zlib.crc32(name.encode()), seed]).standard_normal(out[name].shape)
        drawn = base * np.exp(spread * noise) if base else spread * noise
        out[name] = __import__('jax').numpy.asarray(drawn.astype(out[name].dtype))
    for name, factor in factors.items():
        out[name] = (out[name] * factor).astype(out[name].dtype)
    return out
```

```python
from contextlib import ExitStack
import math

import numpy as np
import concourse.bass as bass
import concourse.mybir as mybir

F32 = mybir.dt.float32
F32R = mybir.dt.float32r
BF16 = mybir.dt.bfloat16
I32 = mybir.dt.int32
ALU = mybir.AluOpType
ACT = mybir.ActivationFunctionType
AX_X = mybir.AxisListType.X

P = 128
D = 1024
KD = D // P
T = 256
TB = T // P
DEPTH = 2
DH = 64
HEADS_A = 12
DILATIONS = (1, 4, 16)
N_BACK = 128
DA = HEADS_A * DH
DB = 512
WINDOWS = (2, 4, 8, 16)
HEADS_C = 8
NOPE, ROPE = 64, 32
QK = NOPE + ROPE
Q_LORA, KV_LORA = 384, 256
JQ, JKV = Q_LORA // P, KV_LORA // P
DC = HEADS_C * DH
HEADS = HEADS_A + HEADS_C
NE = 64
FF = 256
GROUP = 8
TOPK_GROUPS = 4
ROUTED_SCALE = 2.5
EPS = 1e-6
NEG = -1e30
TAKEN = -3e38
SLOTS = 64
BATCH_ITEMS = 4
MAX_EXTRA = 40
ITEMS = NE + MAX_EXTRA
NOT_HERE = 512.0
NO_ITEM = 1024.0
W_SLOTS = 2
ADA_SLOTS = 2
RAW = 6

COL_QK, COL_V = 0, 2 * DA
COL_U = 3 * DA
COL_C = COL_U + DB
COL_KR = COL_C + Q_LORA + KV_LORA
COL_G = COL_KR + ROPE
N_IN = COL_G + 3 * D

W_LOADS = [("w_in", COL_U, 512), ("w_in", COL_C, 512), ("w_in", COL_C + 512, 160)]
W_LOADS += [("w_in", COL_QK + 512 * i, 512) for i in range(3)]
W_LOADS += [("w_in", COL_V, 512), ("w_in", COL_V + 512, 256), ("w_uq", 0, 0), ("w_ukv", 0, 0)]
W_LOADS += [("w_in", COL_G + 512 * i, 512) for i in range(6)]
W_LOADS += [("w_o", 0, 512), ("w_o", 512, 512), ("w_out", 0, 512), ("w_out", 512, 512)]
W_BRANCH_ROWS = (("w_oa", 0, 2), ("w_ob", 2, 4), ("w_oc", 6, 4))
W_AT = {}
for _n, _load in enumerate(W_LOADS):
    W_AT.setdefault(_load[:2], _n)
W_LANDED = []
for _n, _load in enumerate(W_LOADS):
    W_LANDED.append((W_LANDED[_n - W_SLOTS] if _n >= W_SLOTS else 0) + (48 if _load[0] == "w_o" else 16))

UNITS = [(pair, qb) for pair in range(HEADS // 2) for qb in range(TB)]
GATE_GROUPS = [(c, blk) for c in range(6) for blk in range(TB)]


class Count:

    def __init__(self, eng, sem):
        self.eng, self.sem, self.n = eng, sem, 0

    def inc(self, ins):
        self.n += 1
        ins.then_inc(self.sem, 1)

    def wait(self):
        self.eng.wait_ge(self.sem, self.n)

    def step(self, ins):
        self.inc(ins)
        self.wait()


def hybrid_trunk(nc, t, out):
    stack = ExitStack()
    with stack:
        def sb(name, shape, dt=F32, where=stack):
            return where.enter_context(nc.sbuf_tensor(name, shape, dt))

        def sem(name):
            return stack.enter_context(nc.semaphore(name))

        bank = [stack.enter_context(nc.psum_tensor(f"bank{i}", [P, 512], F32)) for i in range(8)]

        x = sb("x", [P, TB, D])
        ident = sb("ident", [P, P])
        ones = sb("ones", [P, T])
        mask = sb("mask", [P, 3, TB, T], BF16)
        rcount = sb("rcount", [P, len(WINDOWS), 16])
        cos_sin = sb("cos_sin", [P, TB, 2, ROPE // 2])
        silu_c = sb("silu_c", [P, KD])
        mod_a = sb("mod_a", [P, 2, KD])
        mod_b = sb("mod_b", [P, 2, KD])
        gate_ffn = sb("gate_ffn", [P, D])
        small = sb("small", [P, 16])
        item_scratch = nc.dram_tensor("item_scratch", [ITEMS, T], BF16, kind="Internal").ap()

        s_first = sem("s_first")
        setup_dma = sem("setup_dma")
        pool_setup = sem("pool_setup")
        act_setup = sem("act_setup")
        dve_setup = sem("dve_setup")
        s_last = setup_dma

        with ExitStack() as scope, nc.Block() as block:
            diff = sb("diff", [P, TB, T], I32, scope)
            low = sb("low", [P, TB, T], I32, scope)
            dist = sb("dist", [P, TB, T], F32, scope)
            ok = sb("ok", [P, TB, T], F32, scope)
            ok2 = sb("ok2", [P, TB, T], F32, scope)
            tok = sb("tok", [P, 16], I32, scope)
            tokf = sb("tokf", [P, 16], F32, scope)
            pos_i = sb("pos_i", [P, TB], I32, scope)
            pos_f = sb("pos_f", [P, TB], F32, scope)
            ang = sb("ang", [P, TB, 2, ROPE // 2], F32, scope)
            turns = sb("turns", [P, TB, 2, ROPE // 2], F32, scope)
            c_col = sb("c_col", [P, KD], F32, scope)

            @block.sync
            def _(sp):
                sp.dma_start(x[:], t["x"][0].rearrange("(b p) d -> p b d", p=P)).then_inc(setup_dma, 16)
                sp.dma_start(c_col[:], t["c"][0].rearrange("(p k) -> p k", k=KD)).then_inc(setup_dma, 16)
                sp.dma_start(pos_i[:], t["positions"][0].rearrange("(b p) -> p b", p=P),
                             allow_slow_non_contiguous=True).then_inc(setup_dma, 16)
                sp.wait_ge(setup_dma, 48)

            @block.gpsimd
            def _(pool):
                pool.memset(ident[:], 0.0).then_inc(pool_setup, 1)
                pool.memset(ones[:], 1.0).then_inc(pool_setup, 1)
                pool.iota(diff[:], [[P, TB], [-1, T]], base=0, channel_multiplier=1).then_inc(pool_setup, 1)
                pool.iota(tok[:], [[1, 16]], base=1, channel_multiplier=0).then_inc(pool_setup, 1)
                pool.wait_ge(pool_setup, 4)
                pool.affine_select(out=ident[:], in_=ident[:], compare_op=ALU.not_equal, fill=1.0, base=0,
                                   pattern=[[-1, P]], channel_multiplier=1).then_inc(pool_setup, 1)

            @block.scalar
            def _(act):
                act.wait_ge(setup_dma, 48)
                act.activation(silu_c[:], c_col[:], ACT.Silu).then_inc(act_setup, 1)
                act.wait_ge(dve_setup, 1)
                act.activation(cos_sin[:], ang[:], ACT.Sin).then_inc(act_setup, 1)

            @block.vector
            def _(dve):
                own = Count(dve, s_first)
                dve.wait_ge(setup_dma, 48)
                own.step(dve.tensor_copy(pos_f[:], pos_i[:]))
                freqs = (np.float32(10000.0) ** (-np.arange(0, ROPE, 2, dtype=np.float32) / np.float32(ROPE)))
                for blk in range(TB):
                    for i, f in enumerate(freqs):
                        for part in range(2):
                            own.inc(dve.tensor_scalar(ang[:, blk, part, i:i + 1], pos_f[:, blk:blk + 1],
                                                      float(f), None, ALU.mult))
                own.wait()
                for part, quarter in ((0, 0.25), (1, 0.0)):
                    own.inc(dve.tensor_scalar(turns[:, :, part], ang[:, :, part], 1 / (2 * math.pi), quarter,
                                              ALU.mult, ALU.add))
                own.wait()
                magic = 1.5 * 2 ** 23
                own.step(dve.tensor_scalar(turns[:], turns[:], magic, None, ALU.add))
                own.step(dve.tensor_scalar(turns[:], turns[:], magic, None, ALU.subtract))
                first = 6.28125
                second = float(np.float32(math.floor((2 * math.pi - first) * 2 ** 20) / 2 ** 20))
                third = 2 * math.pi - first - second
                for piece in (first, second, third):
                    own.step(dve.scalar_tensor_tensor(ang[:], turns[:], -piece, ang[:], ALU.mult, ALU.add))
                own.step(dve.tensor_scalar(ang[:, :, 0], ang[:, :, 0], math.pi / 2, None, ALU.add))
                dve.tensor_scalar(ang[:], ang[:], 3.1415925, -3.1415925, ALU.min, ALU.max).then_inc(dve_setup, 1)
                dve.wait_ge(pool_setup, 5)
                own.step(dve.tensor_copy(dist[:], diff[:]))
                for g, dil in enumerate(DILATIONS):
                    own.step(dve.tensor_scalar(low[:], diff[:], dil - 1, None, ALU.bitwise_and))
                    own.step(dve.tensor_copy(ok[:], low[:]))
                    own.step(dve.tensor_scalar(ok[:], ok[:], 0.0, None, ALU.is_equal))
                    own.step(dve.tensor_scalar(ok2[:], dist[:], 0.0, None, ALU.is_ge))
                    own.step(dve.tensor_tensor(ok[:], ok[:], ok2[:], ALU.mult))
                    own.step(dve.tensor_scalar(ok2[:], dist[:], float(N_BACK * dil), None, ALU.is_le))
                    own.step(dve.tensor_tensor(ok[:], ok[:], ok2[:], ALU.mult))
                    own.step(dve.tensor_scalar(mask[:, g], ok[:], 1.0, -NEG, ALU.subtract, ALU.mult))
                own.step(dve.tensor_copy(tokf[:], tok[:]))
                for g, w in enumerate(WINDOWS):
                    own.inc(dve.tensor_scalar(rcount[:, g], tokf[:], float(w), None, ALU.min))
                own.wait()
                own.step(dve.reciprocal(rcount[:], rcount[:]))

        nc.all_engine_barrier(sems_to_clear=range(s_first.num, dve_setup.num + 1))

        names = """norm_act norm_dve norm_ready turned_ready act_own dve_own pool_own w_used ada_used ada_summed
            ada_bcast mod_ready consts_in hT_ready proj_ready proj_taken sums_ready rstd_sq latent_ready
            rope_ready qt_ready qt_taken pooled_ready mixed_ready mixed_taken s_ready s_taken max_ready
            p_ready pt_ready pt_taken o_ready o_taken coef_in coef_out y_ready yt_ready yt_taken
            branch_ready branch_taken mix_ready mixt_ready mixt_taken res_ready router_in logits_ready
            sig_ready sel_ready selt_ready tables_ready table_psum small_psum small_taken scratch_written
            extra_in shared_up shared_act shared_g shared_gt shared_gt_taken shared_used hi_done lo_done
            a_free b_free added silu_done mul_done gt_ready gt_hi gt_lo down_done y_hi y_lo s_made
            gather_ready gather_taken onehot_made wslot_ready wslot_made wslot_moved xg_hi xg_lo
            scatter_done t_done pos_in acc_ready out_done final_in""".split()
        S = {}
        for n in names:
            S[n] = sem(n)
        w_loaded = [sem(f"w_loaded{i}") for i in range(W_SLOTS)]
        ada_loaded = [sem(f"ada_loaded{i}") for i in range(ADA_SLOTS)]
        raw_loaded = [sem(f"raw_loaded{i}") for i in range(RAW)]
        block_sems = range(S[names[0]].num, raw_loaded[-1].num + 1)

        def norm_act(act, own, squares):
            for blk in range(TB):
                own.inc(act.activation(squares, x[:, blk], ACT.Square, accum_out=small[:, blk:blk + 1]))
                own.wait()
            act.nop().then_inc(S["norm_act"], 1)
            act.wait_ge(S["norm_dve"], 1)
            act.activation(small[:, 4:6], small[:, 2:4], ACT.Sqrt).then_inc(S["norm_act"], 1)

        def norm_dve(dve, own):
            dve.wait_ge(S["norm_act"], 1)
            own.step(dve.tensor_scalar(small[:, 6:8], small[:, 0:2], 1.0 / D, EPS, ALU.mult, ALU.add))
            dve.reciprocal(small[:, 2:4], small[:, 6:8]).then_inc(S["norm_dve"], 1)
            dve.wait_ge(S["norm_act"], 2)
            own.step(dve.tensor_tensor(small[:, 8:10], small[:, 4:6], small[:, 4:6], ALU.mult))
            own.step(dve.tensor_tensor(small[:, 8:10], small[:, 8:10], small[:, 6:8], ALU.mult))
            own.step(dve.tensor_scalar(small[:, 8:10], small[:, 8:10], -0.5, 1.5, ALU.mult, ALU.add))
            own.step(dve.tensor_tensor(small[:, 4:6], small[:, 4:6], small[:, 8:10], ALU.mult))

        def turn_pe(pe, xn, banks):
            for k in range(KD):
                for blk in range(TB):
                    mm = pe.transpose(banks[k // 2][:, (k % 2) * T + blk * P:(k % 2) * T + blk * P + P],
                                      xn[:, blk, k::KD], ident[:])
                if k % 2:
                    mm.then_inc(S["turned_ready"], 1)

        def modulate_act(act, hT, banks, which):
            for k in range(KD):
                if k % 2 == 0:
                    act.wait_ge(S["turned_ready"], k // 2 + 1)
                mm = act.activation(hT[:, k], banks[k // 2][:, (k % 2) * T:(k % 2 + 1) * T], ACT.Identity,
                                    bias=mod_b[:, which, k:k + 1], scale=mod_a[:, which, k:k + 1])
            mm.then_inc(S["hT_ready"], 1)

        stages = dict(locals())
        with nc.Fori(0, DEPTH) as layer:
            with ExitStack() as scope, nc.Block() as block:
                mixer_block(nc, t, layer, stages, lambda n, s, d=F32: sb(n, s, d, scope), block)
            nc.all_engine_barrier(sems_to_clear=block_sems)
            with ExitStack() as scope, nc.Block() as block:
                experts_block(nc, t, layer, stages, lambda n, s, d=F32: sb(n, s, d, scope), block)
            nc.all_engine_barrier(sems_to_clear=block_sems)

        with ExitStack() as scope, nc.Block() as block:
            squares = sb("squares", [P, D], F32, scope)
            final_g = sb("final_g_row", [P, D], F32, scope)
            y = sb("y_out", [P, TB, D], F32, scope)

            @block.sync
            def _(sp):
                sp.dma_start(final_g[:], t["final_g"].rearrange("(a d) -> a d", a=1).to_broadcast([P, D])
                             ).then_inc(S["final_in"], 16)
                for blk in range(TB):
                    sp.wait_ge(S["norm_ready"], blk + 1)
                    sp.dma_start(out[0, blk * P:(blk + 1) * P, :], y[:, blk]).then_inc(S["out_done"], 16)
                sp.wait_ge(S["out_done"], 16 * TB)

            @block.scalar
            def _(act):
                norm_act(act, Count(act, S["act_own"]), squares[:])

            @block.vector
            def _(dve):
                norm_dve(dve, Count(dve, S["dve_own"]))
                dve.wait_ge(S["final_in"], 16)
                for blk in range(TB):
                    dve.scalar_tensor_tensor(y[:, blk], x[:, blk], small[:, 4 + blk:5 + blk], final_g[:],
                                             ALU.mult, ALU.mult).then_inc(S["norm_ready"], 1)


def mixer_block(nc, t, layer, g, sb, block):
    S, bank, x, ident, ones = g["S"], g["bank"], g["x"], g["ident"], g["ones"]
    mask, rcount, cos_sin, silu_c = g["mask"], g["rcount"], g["cos_sin"], g["silu_c"]
    mod_a, mod_b, gate_ffn, small = g["mod_a"], g["mod_b"], g["gate_ffn"], g["small"]
    w_loaded, ada_loaded = g["w_loaded"], g["ada_loaded"]

    hT = sb("m_hT", [P, KD, T])
    xn_o = sb("xn_o", [P, TB * HEADS * DH])
    xn = xn_o[:, 0:TB * D].rearrange("p (b d) -> p b d", b=TB)
    heads_o = xn_o[:, :].rearrange("p (b h e) -> p b h e", b=TB, h=HEADS)
    qk_t = sb("qk_t", [P, 12 * T])
    qkT = qk_t[:, :].rearrange("p (j t) -> p j t", j=12)
    yT = qk_t[:, 0:6 * T].rearrange("p (j t) -> p j t", j=6)
    va = sb("va", [P, TB, DA])
    uT = sb("uT", [P, 4, T])
    ybT = uT
    latent = sb("latent", [P, 5, T])
    tanh_g = sb("tanh_g", [P, TB, 3 * D])
    q_y = sb("q_y", [P, TB, (HEADS_C + 1) * QK])
    y_nat = q_y[:, :, 0:768]
    qT_mix = sb("qT_mix", [P, 8 * T])
    qcT = qT_mix[0:QK, :].rearrange("p (h t) -> p h t", h=8)
    raw_c = qT_mix[:, 0:5 * T].rearrange("p (j t) -> p j t", j=5)
    mix = qT_mix[:, :].rearrange("p (b d) -> p b d", b=TB)
    kT_mixT = sb("kT_mixT", [P, 8 * T])
    kcT = kT_mixT[0:QK, :].rearrange("p (h t) -> p h t", h=8)
    sq_c = kT_mixT[:, 0:5 * T].rearrange("p (j t) -> p j t", j=5)
    mixT = kT_mixT[:, :].rearrange("p (k t) -> p k t", k=KD)
    vc = sb("vc", [P, TB, DC])
    att = sb("att", [P, 3, 2, 2, T])
    s_sb, p_sb, pt_sb = att[:, 0], att[:, 1], att[:, 2]
    flat = att[:, :, :, :, :].rearrange("p a b c t -> p (a b c t)")
    pooled = flat[:, 0:4 * T].rearrange("p (g t) -> p g t", g=4)
    cs = flat[:, 4 * T:4 * T + 4 * (16 + T)].rearrange("p (g t) -> p g t", g=4)
    squares = flat[:, 0:D]
    rope_t = sb("rope_t", [P, 4, HEADS_C + 1, ROPE // 2])
    neg_max = sb("neg_max", [P, TB, HEADS])
    den = sb("den", [P, TB, HEADS])
    fac = sb("fac", [P, 4, HEADS_A])
    gate_mix = sb("gate_mix", [P, D])
    scaled = sb("scaled", [P, 3, 512])
    rstd = scaled[:, 0:2].rearrange("p a (b t) -> p a b t", b=2)
    wring = sb("wring", [P, W_SLOTS, 5120])
    ada_ring = sb("ada_ring", [P, ADA_SLOTS, 1536])
    ada_acc = sb("ada_acc", [P, 3 * D])
    pool_w = sb("pool_w_sb", [P, 4, P])
    cols = sb("cols", [P, 64])
    g_col = [cols[:, 0:8], cols[:, 8:16]]
    shift_col = [cols[:, 16:24], cols[:, 24:32]]
    scale_col = [cols[:, 32:40], cols[:, 40:48]]
    pscale = cols[:, 48:52]
    lat_g = cols[:, 52:57]
    gates_row = (gate_mix, gate_ffn)
    N_SMALL = 12

    def w_view(n, rows, width):
        return wring[:, n % W_SLOTS, 0:rows * width].rearrange("p (r n) -> p r n", r=rows)

    first = [("T", W_AT["w_in", COL_U], 0, 2, uT[:, 0:2]), ("T", W_AT["w_in", COL_U], 256, 2, uT[:, 2:4]),
             ("C", W_AT["w_in", COL_C], 0, 2, 0), ("C", W_AT["w_in", COL_C], 256, 2, 2),
             ("C", W_AT["w_in", COL_C + 512], 0, 1, 4),
             ("N2", W_AT["w_in", COL_C + 512], 128, ROPE, q_y[:, :, HEADS_C * QK + NOPE:])]
    second = []
    for i in range(3):
        for half in range(2):
            second.append(("T", W_AT["w_in", COL_QK + 512 * i], 256 * half, 2,
                           qkT[:, 4 * i + 2 * half:4 * i + 2 * half + 2]))
    second += [("N", W_AT["w_in", COL_V], 0, (blk, 512), va[:, blk, 0:512]) for blk in range(TB)]
    second += [("N2", W_AT["w_in", COL_V + 512], 0, 256, va[:, :, 512:768])]
    second += [("Q", W_AT["w_uq", 0], 0, (blk, 512), q_y[:, blk, 0:512]) for blk in range(TB)]
    second += [("Q2", W_AT["w_uq", 0], 512, 256, q_y[:, :, 512:768])]
    second += [("K", W_AT["w_ukv", 0], 2 * h, 2, kcT[0:NOPE, 2 * h:2 * h + 2]) for h in range(4)]
    second += [("V", W_AT["w_ukv", 0], 0, blk, vc[:, blk]) for blk in range(TB)]
    gates = [("G", W_AT["w_in", COL_G + 512 * c], 0, (blk, 512), tanh_g[:, blk, 512 * c:512 * c + 512])
             for c, blk in GATE_GROUPS]
    projections = first + second + gates
    last_of_load = {p[1]: n for n, p in enumerate(projections)}

    def gates_at(u):
        n = len(GATE_GROUPS)
        return range(u * n // 20, (u + 1) * n // 20) if u < 20 else range(0)

    def scales(pair):
        return DH ** -0.5 if pair < 6 else QK ** -0.5

    @block.sync
    def _(sp):
        for n, (src, col, width) in enumerate(W_LOADS):
            if n >= W_SLOTS:
                sp.wait_ge(S["w_used"], n - W_SLOTS + 1)
            if src == "w_o":
                for name, row, rows in W_BRANCH_ROWS:
                    sp.dma_start(w_view(n, 10, 512)[:, row:row + rows],
                                 t[name][layer][:, col:col + 512].rearrange("(j p) n -> p j n", p=P)
                                 ).then_inc(w_loaded[n % W_SLOTS], 16)
                continue
            w = t[src][layer]
            if src in ("w_in", "w_out"):
                dst = w_view(n, KD, width)
                sp.dma_start(dst, w[:, col:col + width].rearrange("(p k) n -> p k n", k=KD)
                             ).then_inc(w_loaded[n % W_SLOTS], 16)
            else:
                rows, width = w.shape[0] // P, w.shape[1]
                sp.dma_start(w_view(n, rows, width), w.rearrange("(j p) n -> p j n", p=P)
                             ).then_inc(w_loaded[n % W_SLOTS], 16)

    @block.scalar
    def _(act):
        own = Count(act, S["act_own"])
        loads = [(pool_w[:], t["pool_w"][layer].rearrange("g c d -> c g d")),
                 (pscale, t["pool_scale"][layer].rearrange("(g p) -> p g", p=P)),
                 (lat_g[:, 0:JQ], t["cq_norm_g"][layer].rearrange("(j p) -> p j", p=P)),
                 (lat_g[:, JQ:5], t["ckv_norm_g"][layer].rearrange("(j p) -> p j", p=P))]
        for i, kind in enumerate(("mix", "ffn")):
            bias = t[f"ada_{kind}_b"][layer]
            loads += [(g_col[i], t[f"norm_{kind}_g"][layer].rearrange("(p k) -> p k", k=KD)),
                      (shift_col[i], bias[0:D].rearrange("(p k) -> p k", k=KD)),
                      (scale_col[i], bias[D:2 * D].rearrange("(p k) -> p k", k=KD)),
                      (gates_row[i][0:1], bias[2 * D:3 * D].rearrange("(a d) -> a d", a=1))]
        assert len(loads) == N_SMALL

        def load_ada(n):
            src = t["ada_mix_w" if n < 2 * KD else "ada_ffn_w"][layer].rearrange("(p k) n -> p k n", k=KD)
            k, half = (n // 2) % KD, n % 2
            if n >= ADA_SLOTS:
                act.wait_ge(S["ada_used"], n - ADA_SLOTS + 1)
            act.dma_start(ada_ring[:, n % ADA_SLOTS], src[:, k, 1536 * half:1536 * (half + 1)]
                          ).then_inc(ada_loaded[n % ADA_SLOTS], 16)

        for n in range(ADA_SLOTS):
            load_ada(n)
        for dst, src in loads:
            act.dma_start(dst, src, allow_slow_non_contiguous=True).then_inc(S["consts_in"], 16)
        for n in range(ADA_SLOTS, 4):
            load_ada(n)
        g["norm_act"](act, own, squares)
        for n in range(4, 2 * KD + ADA_SLOTS):
            load_ada(n)
        act.wait_ge(S["mod_ready"], 1)
        g["modulate_act"](act, hT, bank[2:6], 0)

        def take_projection(n):
            kind, load, col, size, dst = projections[n]
            act.wait_ge(S["proj_ready"], n + 1)
            ps = bank[n % 2]
            if kind in ("T", "K"):
                rows = P if kind == "T" else NOPE
                ins = act.activation(dst, ps[0:rows, 0:size * T].rearrange("p (j t) -> p j t", j=size), ACT.Copy)
            elif kind == "C":
                src = ps[:, 0:size * T].rearrange("p (j t) -> p j t", j=size)
                act.activation(raw_c[:, dst:dst + size], src, ACT.Copy)
                ins = act.activation(sq_c[:, dst:dst + size], src, ACT.Square)
            elif kind in ("N2", "Q2"):
                ins = act.activation(dst, ps[:, 0:TB * size].rearrange("p (b n) -> p b n", b=TB), ACT.Copy)
            elif kind == "G":
                ins = act.activation(dst, ps[:], ACT.Tanh, scale=0.5)
            else:
                ins = act.activation(dst, ps[:], ACT.Copy)
            ins.then_inc(S["proj_taken"], 1)

        for n in range(len(first)):
            take_projection(n)
        act.wait_ge(S["rstd_sq"], 1)
        act.activation(rstd[:, :, 0], rstd[:, :, 1], ACT.Sqrt).then_inc(S["rstd_sq"], 1)
        for n in range(len(first), len(first) + len(second)):
            if n == len(first) + 12:
                act.wait_ge(S["sums_ready"], 1)
            take_projection(n)
        for i in range(2):
            act.wait_ge(S["mixed_ready"], i + 1)
            for j in range(2):
                ins = act.activation(ybT[:, 2 * i + j], bank[6 + i][:, j * T:(j + 1) * T], ACT.Copy,
                                     scale=pscale[:, 2 * i + j:2 * i + j + 1])
            ins.then_inc(S["mixed_taken"], 1)
        for i in range(5):
            act.wait_ge(S["qt_ready"], i + 1)
            src = bank[2 + i % 2][0:QK, :].rearrange("p (j t) -> p j t", j=2)
            if i < 4:
                ins = act.activation(qcT[:, 2 * i:2 * i + 2], src, ACT.Copy)
            else:
                ins = act.activation(kcT[NOPE:QK], src[NOPE:QK, 0:1].to_broadcast([ROPE, HEADS_C, T]), ACT.Copy)
            ins.then_inc(S["qt_taken"], 1)

        gate_n = len(first) + len(second)
        for u in range(len(UNITS) + 2):
            if u < len(UNITS):
                pair, qb = UNITS[u]
                act.wait_ge(S["max_ready"], u + 1)
                if u >= 2:
                    act.wait_ge(S["pt_ready"], u - 1)
                for h in range(2):
                    ins = act.activation(p_sb[:, u % 2, h, 0:P * (qb + 1)], s_sb[:, u % 2, h, 0:P * (qb + 1)],
                                         ACT.Exp, bias=neg_max[:, qb, 2 * pair + h:2 * pair + h + 1],
                                         accum_out=den[:, qb, 2 * pair + h:2 * pair + h + 1])
                ins.then_inc(S["p_ready"], 1)
            if 1 <= u and u + 1 < 2 * KD:
                load_ada(2 * KD + u + 1)
            for n in gates_at(u):
                take_projection(gate_n + n)
            if u >= 2:
                pair, qb = UNITS[u - 2]
                act.wait_ge(S["o_ready"], u - 1)
                act.activation(heads_o[:, qb, 2 * pair:2 * pair + 2],
                               bank[7][:, 0:2 * DH].rearrange("p (h e) -> p h e", h=2),
                               ACT.Copy).then_inc(S["o_taken"], 1)
        for qb in range(TB):
            act.wait_ge(S["coef_in"], qb + 1)
            act.activation(fac[:, 2 * qb], fac[:, 2 * qb], ACT.Exp).then_inc(S["coef_out"], 1)
        for i in range(3):
            act.wait_ge(S["yt_ready"], i + 1)
            act.activation(yT[:, 2 * i:2 * i + 2], bank[2 + i][:].rearrange("p (j t) -> p j t", j=2),
                           ACT.Copy).then_inc(S["yt_taken"], 1)
        for i in range(4):
            act.wait_ge(S["mixt_ready"], i + 1)
            act.activation(mixT[:, 2 * i:2 * i + 2], bank[6 + i % 2][:].rearrange("p (j t) -> p j t", j=2),
                           ACT.Copy, scale=0.5).then_inc(S["mixt_taken"], 1)

    @block.vector
    def _(dve):
        own = Count(dve, S["dve_own"])

        def ada_step(n):
            k, half = (n // 2) % KD, n % 2
            dve.wait_ge(ada_loaded[n % ADA_SLOTS], 16 * (n // ADA_SLOTS + 1))
            acc = ada_acc[:, 1536 * half:1536 * (half + 1)]
            if k == 0:
                ins = dve.tensor_scalar(acc, ada_ring[:, n % ADA_SLOTS], silu_c[:, 0:1], None, ALU.mult)
            else:
                dve.wait_ge(S["ada_used"], n - 1)
                ins = dve.scalar_tensor_tensor(acc, ada_ring[:, n % ADA_SLOTS], silu_c[:, k:k + 1], acc,
                                               ALU.mult, ALU.add)
            ins.then_inc(S["ada_used"], 1)

        def take_sums(which, gate):
            dve.wait_ge(S["ada_summed"], which + 1)
            dve.wait_ge(S["consts_in"], 16 * N_SMALL)
            own.inc(dve.tensor_tensor(mod_b[:, which], bank[0][:, 0:KD], shift_col[which], ALU.add))
            own.step(dve.tensor_tensor(mod_a[:, which], bank[0][:, KD:2 * KD], scale_col[which], ALU.add))
            dve.scalar_tensor_tensor(mod_a[:, which], mod_a[:, which], 1.0, g_col[which], ALU.add,
                                     ALU.mult).then_inc(S["mod_ready"], 1)
            for half in range(2):
                ins = dve.tensor_copy(gate[:, 512 * half:512 * (half + 1)], bank[6 + half][:])
            ins.then_inc(S["ada_bcast"], 1)

        for n in range(4):
            ada_step(n)
        g["norm_dve"](dve, own)
        for blk in range(TB):
            dve.tensor_scalar(xn[:, blk], x[:, blk], small[:, 4 + blk:5 + blk], None,
                              ALU.mult).then_inc(S["norm_ready"], 1)
        for n in range(4, 2 * KD):
            ada_step(n)
        take_sums(0, gate_mix)

        own.inc(dve.memset(cs[:, :, 0:16], 0.0))
        for grp in range(4):
            dve.wait_ge(S["proj_taken"], grp // 2 + 1)
            own.inc(dve.tensor_tensor_scan(cs[:, grp, 16:], ones[:], uT[:, grp], 0.0, ALU.mult, ALU.add))
        own.wait()
        for grp, w in enumerate(WINDOWS):
            own.inc(dve.tensor_tensor(pooled[:, grp], cs[:, grp, 16:], cs[:, grp, 16 - w:16 - w + T], ALU.subtract))
        own.wait()
        for grp, w in enumerate(WINDOWS):
            own.inc(dve.tensor_tensor(pooled[:, grp, 0:16], pooled[:, grp, 0:16], rcount[:, grp], ALU.mult))
        own.wait()
        for grp, w in enumerate(WINDOWS):
            own.inc(dve.tensor_tensor(pooled[:, grp, 0:16], pooled[:, grp, 0:16], uT[:, grp, 0:16], ALU.subtract))
            own.inc(dve.scalar_tensor_tensor(pooled[:, grp, 16:], pooled[:, grp, 16:], 1.0 / w, uT[:, grp, 16:],
                                             ALU.mult, ALU.subtract))
        own.wait()
        dve.nop().then_inc(S["pooled_ready"], 1)

        dve.wait_ge(S["sums_ready"], 1)
        for i, n in enumerate((Q_LORA, KV_LORA)):
            own.inc(dve.tensor_scalar(cs[:, i, 0:T], bank[2][:, i * T:(i + 1) * T], 1.0 / n, EPS, ALU.mult, ALU.add))
        own.wait()
        ms = cs[:, 0:2, 0:T]
        dve.reciprocal(rstd[:, :, 1], ms).then_inc(S["rstd_sq"], 1)
        dve.wait_ge(S["rstd_sq"], 2)
        own.step(dve.tensor_tensor(rstd[:, :, 1], rstd[:, :, 0], rstd[:, :, 0], ALU.mult))
        own.step(dve.tensor_tensor(rstd[:, :, 1], rstd[:, :, 1], ms, ALU.mult))
        own.step(dve.tensor_scalar(rstd[:, :, 1], rstd[:, :, 1], -0.5, 1.5, ALU.mult, ALU.add))
        own.step(dve.tensor_tensor(rstd[:, :, 0], rstd[:, :, 0], rstd[:, :, 1], ALU.mult))
        for j in range(5):
            ins = dve.scalar_tensor_tensor(latent[:, j], raw_c[:, j], lat_g[:, j:j + 1],
                                           rstd[:, 0 if j < JQ else 1, 0], ALU.mult, ALU.mult)
        ins.then_inc(S["latent_ready"], 1)

        own.inc(dve.memset(q_y[:, :, HEADS_C * QK:HEADS_C * QK + NOPE], 0.0))
        dve.wait_ge(S["proj_taken"], len(first) + 12)
        for blk in range(TB):
            heads = q_y[:, blk].rearrange("p (h e) -> p h e", e=QK)
            x1, x2 = heads[:, :, NOPE:NOPE + ROPE // 2], heads[:, :, NOPE + ROPE // 2:QK]
            cos, sin = (cos_sin[:, blk, i:i + 1].to_broadcast([P, HEADS_C + 1, ROPE // 2]) for i in range(2))
            own.inc(dve.tensor_tensor(rope_t[:, 0], x1, cos, ALU.mult))
            own.inc(dve.tensor_tensor(rope_t[:, 1], x2, sin, ALU.mult))
            own.inc(dve.tensor_tensor(rope_t[:, 2], x2, cos, ALU.mult))
            own.step(dve.tensor_tensor(rope_t[:, 3], x1, sin, ALU.mult))
            own.inc(dve.tensor_tensor(x1, rope_t[:, 0], rope_t[:, 1], ALU.subtract))
            own.step(dve.tensor_tensor(x2, rope_t[:, 2], rope_t[:, 3], ALU.add))
        dve.nop().then_inc(S["rope_ready"], 1)

        for u in range(len(UNITS) + 1):
            if u < len(UNITS):
                pair, qb = UNITS[u]
                nk = P * (qb + 1)
                dve.wait_ge(S["s_ready"], u + 1)
                if u >= 2:
                    dve.wait_ge(S["p_ready"], u - 1)
                ps = [bank[2 + 2 * (u % 2) + h][:, 0:nk] for h in range(2)]
                grp = pair // 2 if pair < 6 else 0
                for h in range(2):
                    if pair < 6:
                        dve.scalar_tensor_tensor(s_sb[:, u % 2, h, 0:nk], ps[h], scales(pair),
                                                 mask[:, grp, qb, 0:nk], ALU.mult, ALU.add
                                                 ).then_inc(S["s_taken"], 1)
                    else:
                        if qb:
                            dve.tensor_scalar(s_sb[:, u % 2, h, 0:P], ps[h][:, 0:P], scales(pair), None, ALU.mult)
                        dve.scalar_tensor_tensor(s_sb[:, u % 2, h, nk - P:nk], ps[h][:, nk - P:nk], scales(pair),
                                                 mask[:, 0, 0, 0:P], ALU.mult, ALU.add).then_inc(S["s_taken"], 1)
                dve.wait_ge(S["s_taken"], 2 * u + 2)
                own.step(dve.tensor_reduce(neg_max[:, qb, 2 * pair:2 * pair + 2], s_sb[:, u % 2, :, 0:nk], AX_X, ALU.max))
                dve.tensor_scalar(neg_max[:, qb, 2 * pair:2 * pair + 2], neg_max[:, qb, 2 * pair:2 * pair + 2], -1.0,
                                  None, ALU.mult).then_inc(S["max_ready"], 1)
            if u >= 1:
                pair, qb = UNITS[u - 1]
                nk = P * (qb + 1)
                dve.wait_ge(S["pt_ready"], u)
                if u >= 3:
                    dve.wait_ge(S["o_ready"], u - 2)
                dve.tensor_copy(pt_sb[:, (u - 1) % 2, :, 0:nk],
                                bank[6][:].rearrange("p (h k) -> p h k", h=2)[:, :, 0:nk]
                                ).then_inc(S["pt_taken"], 1)
            if u < 2 * KD:
                ada_step(2 * KD + u)
        dve.wait_ge(S["o_taken"], len(UNITS))
        for qb in range(TB):
            nm = neg_max[:, qb, 0:HEADS_A].rearrange("p (g h) -> p g h", g=3)
            f = fac[:, 2 * qb].rearrange("p (g h) -> p g h", g=3)
            w = fac[:, 2 * qb + 1].rearrange("p (g h) -> p g h", g=3)
            own.step(dve.tensor_tensor(w[:, 0], nm[:, 0], nm[:, 1], ALU.min))
            own.step(dve.tensor_tensor(w[:, 0], w[:, 0], nm[:, 2], ALU.min))
            for grp in range(3):
                own.inc(dve.tensor_tensor(f[:, grp], w[:, 0], nm[:, grp], ALU.subtract))
            own.wait()
            dve.nop().then_inc(S["coef_in"], 1)
        for qb in range(TB):
            f = fac[:, 2 * qb].rearrange("p (g h) -> p g h", g=3)
            w = fac[:, 2 * qb + 1].rearrange("p (g h) -> p g h", g=3)
            dve.wait_ge(S["coef_out"], qb + 1)
            own.step(dve.tensor_tensor(w, f, den[:, qb, 0:HEADS_A].rearrange("p (g h) -> p g h", g=3), ALU.mult))
            own.step(dve.tensor_tensor(w[:, 0], w[:, 0], w[:, 1], ALU.add))
            own.step(dve.tensor_tensor(w[:, 0], w[:, 0], w[:, 2], ALU.add))
            own.inc(dve.reciprocal(w[:, 1], w[:, 0]))
            own.step(dve.reciprocal(den[:, qb, HEADS_A:], den[:, qb, HEADS_A:]))
            for grp in range(3):
                own.inc(dve.tensor_tensor(f[:, grp], f[:, grp], w[:, 1], ALU.mult))
            own.wait()
            own.inc(dve.tensor_tensor(heads_o[:, qb, 0:HEADS_A], heads_o[:, qb, 0:HEADS_A],
                                      fac[:, 2 * qb, :, None].to_broadcast([P, HEADS_A, DH]), ALU.mult))
            yc = y_nat[:, qb, 4 * DH:].rearrange("p (h e) -> p h e", e=DH)
            own.inc(dve.tensor_tensor(yc, heads_o[:, qb, HEADS_A:], den[:, qb, HEADS_A:, None].to_broadcast(
                [P, HEADS_C, DH]), ALU.mult))
            own.wait()
            ya = y_nat[:, qb, 0:4 * DH].rearrange("p (h e) -> p h e", e=DH)
            own.step(dve.tensor_tensor(ya, heads_o[:, qb, 0:4], heads_o[:, qb, 4:8], ALU.add))
            dve.tensor_tensor(ya, ya, heads_o[:, qb, 8:12], ALU.add).then_inc(S["y_ready"], 1)
        take_sums(1, gate_ffn)

        for n in range(2 * TB):
            half, blk = n // TB, n % TB
            dve.wait_ge(S["branch_ready"], n + 1)
            for br in range(3):
                own.inc(dve.scalar_tensor_tensor(
                    scaled[:, br], tanh_g[:, blk, D * br + 512 * half:D * br + 512 * (half + 1)], 1.0,
                    bank[3 * (n % 2) + br][:], ALU.add, ALU.mult))
            own.wait()
            dve.nop().then_inc(S["branch_taken"], 1)
            own.step(dve.tensor_tensor(scaled[:, 0], scaled[:, 0], scaled[:, 1], ALU.add))
            dst = mix[:, blk, 512 * half:512 * (half + 1)]
            own.step(dve.tensor_tensor(dst, scaled[:, 0], scaled[:, 2], ALU.add))
        dve.nop().then_inc(S["mix_ready"], 1)

        for n in range(2 * TB):
            half, blk = n // TB, n % TB
            dve.wait_ge(S["res_ready"], n + 1)
            cut = slice(512 * half, 512 * (half + 1))
            own.step(dve.tensor_tensor(scaled[:, 0], gate_mix[:, cut], bank[n][:], ALU.mult))
            own.step(dve.tensor_tensor(x[:, blk, cut], x[:, blk, cut], scaled[:, 0], ALU.add))

    @block.tensor
    def _(pe):
        def sum_ada(which):
            pe.wait_ge(S["ada_used"], 2 * KD * (which + 1))
            for part in range(2):
                for k in range(KD):
                    pe.matmul(bank[0][:, part * KD + k:part * KD + k + 1],
                              ada_acc[:, part * D + k:(part + 1) * D:KD], ones[:, 0:1], start=True, stop=True)
            pe.wait_ge(S["consts_in"], 16 * N_SMALL)
            for half in range(2):
                cut = slice(512 * half, 512 * (half + 1))
                pe.matmul(bank[6 + half][:], ones[:, 0:P], ada_acc[:, 2 * D + 512 * half:2 * D + 512 * (half + 1)],
                          start=True, stop=False)
                mm = pe.matmul(bank[6 + half][:], ones[0:1, 0:P], gates_row[which][0:1, cut], start=False, stop=True)
            mm.then_inc(S["ada_summed"], 1)

        pe.wait_ge(S["norm_ready"], TB)
        g["turn_pe"](pe, xn, bank[2:6])
        sum_ada(0)
        pe.wait_ge(S["hT_ready"], 1)

        def project(n):
            kind, load, col, size, dst = projections[n]
            ps = bank[n % 2]
            pe.wait_ge(w_loaded[load % W_SLOTS], W_LANDED[load])
            if n >= 2:
                pe.wait_ge(S["proj_taken"], n - 1)
            if kind in ("T", "C"):
                w = w_view(load, KD, W_LOADS[load][2])
                for j in range(size):
                    for k in range(KD):
                        mm = pe.matmul(ps[:, j * T:(j + 1) * T], w[:, k, col + P * j:col + P * (j + 1)], hT[:, k],
                                       start=(k == 0), stop=(k == KD - 1))
            elif kind in ("N", "G"):
                w = w_view(load, KD, W_LOADS[load][2])
                blk, width = size
                for k in range(KD):
                    mm = pe.matmul(ps[:, 0:width], hT[:, k, blk * P:(blk + 1) * P], w[:, k, col:col + width],
                                   start=(k == 0), stop=(k == KD - 1))
            elif kind == "N2":
                w = w_view(load, KD, W_LOADS[load][2])
                for blk in range(TB):
                    for k in range(KD):
                        mm = pe.matmul(ps[:, blk * size:(blk + 1) * size], hT[:, k, blk * P:(blk + 1) * P],
                                       w[:, k, col:col + size], start=(k == 0), stop=(k == KD - 1))
            elif kind in ("Q", "Q2"):
                w = w_view(load, JQ, HEADS_C * QK)
                for blk, width, at in ([(size[0], size[1], 0)] if kind == "Q"
                                       else [(b, size, b * size) for b in range(TB)]):
                    for j in range(JQ):
                        mm = pe.matmul(ps[:, at:at + width], latent[:, j, blk * P:(blk + 1) * P],
                                       w[:, j, col:col + width], start=(j == 0), stop=(j == JQ - 1))
            elif kind == "K":
                w = w_view(load, JKV, HEADS_C * P)
                for h in range(size):
                    for j in range(JKV):
                        mm = pe.matmul(ps[0:NOPE, h * T:(h + 1) * T],
                                       w[:, j, (col + h) * P:(col + h) * P + NOPE], latent[:, JQ + j],
                                       start=(j == 0), stop=(j == JKV - 1))
            else:
                w = w_view(load, JKV, HEADS_C * P).rearrange("p j (h e) -> p j h e", e=P)
                for j in range(JKV):
                    mm = pe.matmul(ps[:], latent[:, JQ + j, size * P:(size + 1) * P], w[:, j, :, NOPE:P],
                                   start=(j == 0), stop=(j == JKV - 1))
            mm.then_inc(S["proj_ready"], 1)
            if last_of_load[load] == n:
                pe.wait_ge(S["proj_ready"], n + 1)
                pe.sem_inc(S["w_used"], 1)

        for n in range(len(first)):
            project(n)
        pe.wait_ge(S["proj_taken"], 5)
        for i, tiles in enumerate((range(JQ), range(JQ, 5))):
            for j in tiles:
                mm = pe.matmul(bank[2][:, i * T:(i + 1) * T], ones[:, 0:P], sq_c[:, j],
                               start=(j == tiles[0]), stop=(j == tiles[-1]))
        mm.then_inc(S["sums_ready"], 1)
        for n in range(len(first), len(first) + len(second)):
            if projections[n][0] == "Q":
                pe.wait_ge(S["latent_ready"], 1)
            project(n)
        pe.wait_ge(S["pooled_ready"], 1)
        pe.wait_ge(S["ada_bcast"], 1)
        for i in range(2):
            for j in range(2):
                mm = pe.matmul(bank[6 + i][:, j * T:(j + 1) * T], pool_w[:, 2 * i + j], pooled[:, 2 * i + j],
                               start=True, stop=True)
            mm.then_inc(S["mixed_ready"], 1)
        pe.wait_ge(S["rope_ready"], 1)
        for i in range(5):
            if i >= 2:
                pe.wait_ge(S["qt_taken"], i - 1)
            for j in range(2 if i < 4 else 1):
                for blk in range(TB):
                    slot = 2 * i + j
                    mm = pe.transpose(bank[2 + i % 2][0:QK, j * T + blk * P:j * T + (blk + 1) * P],
                                      q_y[:, blk, slot * QK:(slot + 1) * QK], ident[:])
            mm.then_inc(S["qt_ready"], 1)
        pe.wait_ge(S["qt_taken"], 5)
        pe.wait_ge(S["mixed_taken"], 2)
        gate_n = len(first) + len(second)
        pe.wait_ge(S["proj_taken"], gate_n)
        for u in range(len(UNITS) + 2):
            if u < len(UNITS):
                pair, qb = UNITS[u]
                nk = P * (qb + 1)
                if u >= 2:
                    pe.wait_ge(S["s_taken"], 2 * (u - 1))
                for h in range(2):
                    if pair < 6:
                        q = qkT[DH * h:DH * (h + 1), pair, qb * P:(qb + 1) * P]
                        k = qkT[DH * h:DH * (h + 1), 6 + pair, 0:nk]
                    else:
                        head = 2 * (pair - 6) + h
                        q, k = qcT[:, head, qb * P:(qb + 1) * P], kcT[:, head, 0:nk]
                    mm = pe.matmul(bank[2 + 2 * (u % 2) + h][:, 0:nk], q, k, start=True, stop=True)
                mm.then_inc(S["s_ready"], 1)
            for n in gates_at(u):
                project(gate_n + n)
            if 1 <= u <= len(UNITS):
                pair, qb = UNITS[u - 1]
                pe.wait_ge(S["p_ready"], u)
                if u >= 2:
                    pe.wait_ge(S["pt_taken"], u - 1)
                for h in range(2):
                    for kb in range(qb + 1):
                        cut = slice(h * T + kb * P, h * T + (kb + 1) * P)
                        mm = pe.transpose(bank[6][:, cut], p_sb[:, (u - 1) % 2, h, kb * P:(kb + 1) * P],
                                          ident[:])
                mm.then_inc(S["pt_ready"], 1)
            if u >= 2:
                pair, qb = UNITS[u - 2]
                pe.wait_ge(S["pt_taken"], u - 1)
                if u >= 3:
                    pe.wait_ge(S["o_taken"], u - 2)
                for h in range(2):
                    head = 2 * pair + h
                    for kb in range(qb + 1):
                        v = (va[:, kb, DH * head:DH * (head + 1)] if pair < 6
                             else vc[:, kb, DH * (head - HEADS_A):DH * (head - HEADS_A + 1)])
                        mm = pe.matmul(bank[7][:, h * DH:(h + 1) * DH], pt_sb[:, u % 2, h, kb * P:(kb + 1) * P],
                                       v, start=(kb == 0), stop=(kb == qb))
                mm.then_inc(S["o_ready"], 1)

        pe.wait_ge(S["y_ready"], TB)
        for i in range(3):
            for j in range(2):
                for blk in range(TB):
                    mm = pe.transpose(bank[2 + i][:, j * T + blk * P:j * T + (blk + 1) * P],
                                      y_nat[:, blk, (2 * i + j) * P:(2 * i + j + 1) * P], ident[:])
            mm.then_inc(S["yt_ready"], 1)
        pe.wait_ge(S["proj_taken"], len(projections))
        sum_ada(1)
        pe.wait_ge(S["yt_taken"], 3)
        pe.wait_ge(S["ada_bcast"], 2)
        for n in range(2 * TB):
            half, blk = n // TB, n % TB
            if n >= 2:
                pe.wait_ge(S["branch_taken"], n - 1)
            load = W_AT["w_o", 512 * half]
            pe.wait_ge(w_loaded[load % W_SLOTS], W_LANDED[load])
            w = w_view(load, 10, 512)
            for br, (src, at) in enumerate(((yT, 0), (ybT, 0), (yT, 2))):
                _, row, rows = W_BRANCH_ROWS[br]
                for j in range(rows):
                    mm = pe.matmul(bank[3 * (n % 2) + br][:], src[:, at + j, blk * P:(blk + 1) * P],
                                   w[:, row + j], start=(j == 0), stop=(j == rows - 1))
            mm.then_inc(S["branch_ready"], 1)
            if blk == TB - 1:
                pe.wait_ge(S["branch_ready"], n + 1)
                pe.sem_inc(S["w_used"], 1)
        pe.wait_ge(S["mix_ready"], 1)
        for i in range(4):
            if i >= 2:
                pe.wait_ge(S["mixt_taken"], i - 1)
            for j in range(2):
                for blk in range(TB):
                    mm = pe.transpose(bank[6 + i % 2][:, j * T + blk * P:j * T + (blk + 1) * P],
                                      mix[:, blk, 2 * i + j::KD], ident[:])
            mm.then_inc(S["mixt_ready"], 1)
        pe.wait_ge(S["mixt_taken"], 4)
        for n in range(2 * TB):
            half, blk = n // TB, n % TB
            load = W_AT["w_out", 512 * half]
            pe.wait_ge(w_loaded[load % W_SLOTS], W_LANDED[load])
            w = w_view(load, KD, 512)
            for k in range(KD):
                mm = pe.matmul(bank[n][:], mixT[:, k, blk * P:(blk + 1) * P], w[:, k], start=(k == 0),
                               stop=(k == KD - 1))
            mm.then_inc(S["res_ready"], 1)


def experts_block(nc, t, layer, g, sb, block):
    S, bank, x, ident, ones = g["S"], g["bank"], g["x"], g["ident"], g["ones"]
    gate_ffn, small, raw_loaded = g["gate_ffn"], g["small"], g["raw_loaded"]
    scratch = g["item_scratch"]
    acc = [bank[n] for n in range(4)]
    up_bank, y_bank, gather_bank = bank[4], bank[5:7], bank[7]

    xn_hi = sb("xn_hi", [P, TB, D], F32R)
    xn_lo = sb("xn_lo", [P, TB, D], F32R)
    hT = sb("e_hT", [P, KD, T])
    raw = sb("raw", [P, RAW, 2048])
    w_hi = sb("w_hi", [P, 3, 2048], F32R)
    w_lo = sb("w_lo", [P, 3, 2048], F32R)
    stage = sb("stage", [P, 2, KD, BATCH_ITEMS * SLOTS])
    xn = stage[:, 1].rearrange("p k (a s) -> p (k a s)", a=1).rearrange("p (b d) -> p b d", b=TB)
    squares = stage[:, 0].rearrange("p k s -> p (k s)")[:, 0:D]
    xg = sb("xg", [P, 2, KD, 2 * SLOTS], F32R)
    onehot = sb("onehot", [P, TB, BATCH_ITEMS, 2 * SLOTS], F32R)
    pos_rows = sb("pos_rows", [P, 2, BATCH_ITEMS, T], BF16)
    spread = sb("spread", [P, T], F32R)
    t_half = sb("t_half", [SLOTS, 512])
    up_sum = sb("up_sum", [SLOTS, 512])
    silu_sb = sb("silu_sb", [SLOTS, FF])
    g_sb = sb("g_sb", [SLOTS, FF])
    gT = sb("gT", [P, 2, 2 * SLOTS], F32R)
    y_h = sb("y_h", [P, D], F32R)
    y_l = sb("y_l", [P, D], F32R)
    w_slot = sb("w_slot", [P, 2, BATCH_ITEMS])
    router_w = sb("router_w_sb", [P, KD, NE])
    bias_row = sb("bias_row", [P, NE])
    scores = sb("scores", [P, TB, NE])
    sel = sb("sel", [P, TB, NE])
    chosen = sb("chosen", [P, TB, NE])
    weight = sb("weight", [P, TB, NE])
    top = sb("top", [P, TB, 8, GROUP])
    grp = sb("grp", [P, TB, 8])
    versus = sb("versus", [P, 2, 8, 8])
    earlier = sb("earlier", [P, 8, 8])
    earlier_e = sb("earlier_e", [NE, NE])
    iota_i = sb("iota_i", [P, 2, SLOTS], I32)
    slot_id = sb("slot_id", [P, 2 * SLOTS])
    slot_of_row = sb("slot_of_row", [P, 1])
    e_id = sb("e_id", [NE, 1])
    part_i = sb("part_i", [P, 2], I32)
    sums = sb("sums", [P, TB, 2])
    maskT_wT = sb("maskT_wT", [NE, 2, T])
    posT = sb("posT", [NE, T])
    extra = sb("extra", [NE, 8])
    pick = sb("pick", [NE, ITEMS])
    shift = sb("shift", [NE, ITEMS])
    sel_x = sb("sel_x", [NE, 2, MAX_EXTRA])
    item_pos = sb("item_pos", [P, TB, ITEMS])
    item_w = sb("item_w", [P, TB, ITEMS, 2], F32R)
    item_rows = sb("item_rows", [ITEMS, T], BF16)
    extra_e = sb("extra_e", [1, MAX_EXTRA], I32)
    extra_n = sb("extra_n", [1, 4])
    extra_b = sb("extra_b", [1, 4], I32)
    shared_g = sb("shared_g", [P, TB, FF])
    shared_gT = sb("shared_gT", [P, 2, T])
    scaled = sb("e_scaled", [P, 512])

    scratch_rows = scratch.rearrange("(b i) t -> b (i t)", i=BATCH_ITEMS)

    def piece(c, buf):
        if c < 2:
            return buf.rearrange("p (m k f) -> p m k f", m=2, k=4)
        return buf.rearrange("p (j n) -> p j n", j=2)

    @block.sync
    def _(sp):
        def load_piece(c, slot, w1, w3, w2):
            dst = piece(c, raw[:, slot])
            if c < 2:
                for m, w in enumerate((w1, w3)):
                    sp.dma_start(dst[:, m], w.rearrange("(p k) f -> p k f", k=KD)[:, 4 * c:4 * c + 4]
                                 ).then_inc(raw_loaded[slot], 16)
            else:
                for j in range(2):
                    sp.dma_start(dst[:, j], w2[j * P:(j + 1) * P, :]).then_inc(raw_loaded[slot], 16)

        w1s, w3s, w2s = (t[f"exp_w{i}"].rearrange("l e a b -> (l e) a b") for i in (1, 3, 2))

        def load_item(e, slot0, wait):
            n = layer * NE + e
            for c in range(3):
                wait(c)
                load_piece(c, slot0 + c, w1s[n], w3s[n], w2s[n])

        sp.dma_start(router_w[:], t["router_w"][layer].rearrange("(p k) e -> p k e", k=KD)
                     ).then_inc(S["router_in"], 16)
        sp.dma_start(bias_row[:], t["router_bias"][layer].rearrange("(a e) -> a e", a=1).to_broadcast([P, NE])
                     ).then_inc(S["router_in"], 16)
        for c in range(3):
            load_piece(c, c, t["sh_w1"][layer], t["sh_w3"][layer], t["sh_w2"][layer])
        load_item(0, 3, lambda c: None)
        load_item(1, 0, lambda c: sp.wait_ge(S["shared_used"], c + 1))
        sp.wait_ge(S["tables_ready"], 1)
        sp.dma_start(scratch, item_rows[:]).then_inc(S["scratch_written"], 16)
        sp.wait_ge(S["scratch_written"], 16)
        sp.dma_start(pos_rows[:, 0].rearrange("p i t -> p (i t)"), scratch_rows[0:1].to_broadcast(
            [P, BATCH_ITEMS * T])).then_inc(S["pos_in"], 16)
        with sp.Fori(1, NE // 2) as j:
            for odd in range(2):
                load_item(j * 2 + odd, 3 * (1 - odd),
                          lambda c: sp.wait_ge(S["lo_done"], j * 12 + (6 * odd - 12 + 2 * (c + 1))))
        sp.wait_ge(S["extra_in"], 1)
        batches = sp.value_load(extra_b[0:1, 0:1], min_val=0, max_val=8)
        with sp.If(batches > 0):
            with sp.Fori(0, batches) as xb:
                for u in range(BATCH_ITEMS):
                    e = sp.value_load(extra_e[0:1, bass.ds(xb * BATCH_ITEMS + u, 1)], min_val=0, max_val=NE - 1)
                    load_item(e, 3 * (1 - u % 2),
                              lambda c: sp.wait_ge(S["lo_done"], xb * 24 + (6 * (NE - 2 + u) + 2 * (c + 1))))
        load_item(0, 3, lambda c: sp.wait_ge(S["lo_done"], batches * 24 + (6 * (NE - 2) + 2 * (c + 1))))

    @block.gpsimd
    def _(pool):
        own = Count(pool, S["pool_own"])
        own.inc(pool.iota(iota_i[:], [[0, 2], [1, SLOTS]], base=0, channel_multiplier=0))
        own.inc(pool.iota(part_i[:, 0:1], [[1, 1]], base=0, channel_multiplier=1))
        own.inc(pool.memset(earlier[:], 1.0))
        own.inc(pool.memset(earlier_e[:], 1.0))
        own.wait()
        own.inc(pool.affine_select(out=earlier[:], in_=earlier[:], compare_op=ALU.is_gt, fill=0.0, base=0,
                                   pattern=[[1, 8], [-1, 8]], channel_multiplier=0))
        own.inc(pool.affine_select(out=earlier_e[:], in_=earlier_e[:], compare_op=ALU.is_gt, fill=0.0, base=0,
                                   pattern=[[1, NE]], channel_multiplier=-1))
    @block.scalar
    def _(act):
        own = Count(act, S["act_own"])

        def hi_half(i, c, h):
            if h == 0:
                act.wait_ge(raw_loaded[i.raw_slot(c)], i.uses_val(32))
                if c < 2 and not i.first:
                    act.wait_ge(S["a_free" if c == 0 else "b_free"], i.val(1, 0))
                elif not i.first:
                    act.wait_ge(S["down_done"], i.val(2, 1))
            cut = slice(1024 * h, 1024 * (h + 1))
            act.activation(w_hi[:, c, cut], raw[:, i.raw_slot(c), cut], ACT.Copy).then_inc(S["hi_done"], 1)

        def take_gather(b1, pair, parity):
            waited_apart(act, S["sig_ready"])
            act.wait_ge(S["gather_ready"], b1(4, pair - 3))
            for j in range(2):
                k = 2 * pair + j
                ins = act.activation(parity(stage)[:, k], gather_bank[:, j * 256:(j + 1) * 256].rearrange(
                    "p (a s) -> p a s", a=1), ACT.Identity, bias=g["mod_b"][:, 1, k:k + 1],
                    scale=g["mod_a"][:, 1, k:k + 1])
            ins.then_inc(S["gather_taken"], 1)

        def xg_high(i, src, batch_done):
            waited_apart(act, S["sig_ready"])
            act.wait_ge(S["gather_taken"], batch_done)
            if not i.early:
                act.wait_ge(S["b_free"], i.val(1, -1))
            act.activation(xg[:, i.parity, :, 0:SLOTS], src, ACT.Copy).then_inc(S["xg_hi"], 1)

        def t_and_silu(i):
            act.wait_ge(S["b_free"], i.val(1, 1))
            act.activation(t_half[:], up_bank[SLOTS:P, :], ACT.Copy).then_inc(S["t_done"], 1)
            act.wait_ge(S["added"], i.val(1, 1))
            act.activation(silu_sb[:], up_sum[:, 0:FF], ACT.Silu).then_inc(S["silu_done"], 1)

        g["norm_act"](act, own, squares)
        act.wait_ge(S["norm_ready"], TB)
        for blk in range(TB):
            act.activation(xn_hi[:, blk], xn[:, blk], ACT.Copy).then_inc(S["norm_act"], 1)
        g["modulate_act"](act, hT, bank[4:8], 1)
        item0 = Item(None, 0, first=True)
        for c in range(3):
            for h in range(2):
                hi_half(item0, c, h)
        act.wait_ge(S["logits_ready"], 1)
        act.activation(scores[:], gather_bank[:, 0:TB * NE].rearrange("p (b e) -> p b e", b=TB),
                       ACT.Sigmoid).then_inc(S["sig_ready"], 1)
        for blk in range(TB):
            act.wait_ge(S["shared_up"], blk + 1)
            act.activation(shared_g[:, blk], bank[4 + blk][:, 0:FF], ACT.Silu).then_inc(S["shared_act"], 1)
        act.wait_ge(S["shared_gt"], 1)
        act.activation(shared_gT[:], bank[6][:].rearrange("p (j t) -> p j t", j=2), ACT.Copy
                       ).then_inc(S["shared_gt_taken"], 1)
        for pair in range(4):
            take_gather(lambda a, c: a + c, pair, lambda s: s[:, 0:1].rearrange("p a k s -> p k a s"))
        for n in range(2):
            i = Item(None, n, early=True)
            xg_high(i, stage[:, 0, :, n * SLOTS:(n + 1) * SLOTS], 4)
        t_and_silu(item0)
        act.wait_ge(S["extra_in"], 1)
        batches = act.value_load(extra_b[0:1, 0:1], min_val=0, max_val=8)
        with act.Fori(0, batches + NE // BATCH_ITEMS) as b:
            par = act.snap(b % 2)
            nxt = act.snap(1 - par)
            act.wait_ge(S["pos_in"], b * 16 + 16)
            act.wait_ge(S["s_made"], b * BATCH_ITEMS + 1)
            act.dma_start(pos_rows[:, bass.ds(nxt, 1)].rearrange("p a i t -> p (a i t)"),
                          scratch_rows[bass.ds(b + 1, 1)].to_broadcast([P, BATCH_ITEMS * T])).then_inc(S["pos_in"], 16)
            for u in range(BATCH_ITEMS):
                i = Item(b, u)
                i1 = i.next()
                act.wait_ge(S["gt_ready"], i.val(1, 1))
                act.wait_ge(S["down_done"], i.val(2, 1))
                act.activation(gT[:, :, 0:SLOTS], y_bank[0][:, 0:2 * SLOTS].rearrange("p (j s) -> p j s", j=2),
                               ACT.Copy).then_inc(S["gt_hi"], 1)
                hi_half(i1, 0, 0)
                hi_half(i1, 0, 1)
                hi_half(i1, 1, 0)
                if u < 2:
                    take_gather(lambda a, c: b * a + (2 * a + c), 2 * u,
                                lambda s: s[:, bass.ds(nxt, 1)].rearrange("p a k s -> p k a s"))
                act.wait_ge(S["wslot_moved"], b + 1)
                for half in range(2):
                    act.wait_ge(S["down_done"], i.val(2, half + 2))
                    if half == 0:
                        act.wait_ge(S["scatter_done"], i.val(1, 1))
                    cut = slice(512 * half, 512 * (half + 1))
                    act.activation(y_h[:, cut], y_bank[half][:], ACT.Copy, scale=w_slot[:, 0, u:u + 1]
                                   ).then_inc(S["y_hi"], 1)
                hi_half(i1, 1, 1)
                hi_half(i1, 2, 0)
                hi_half(i1, 2, 1)
                t_and_silu(i1)
                if u < 2:
                    take_gather(lambda a, c: b * a + (2 * a + c), 2 * u + 1,
                                lambda s: s[:, bass.ds(nxt, 1)].rearrange("p a k s -> p k a s"))
                v = (u + 2) % BATCH_ITEMS
                which = par if u < 2 else nxt
                xg_high(i.next(2), stage[:, bass.ds(which, 1), :, v * SLOTS:(v + 1) * SLOTS].rearrange(
                    "p a k s -> p (a k) s"), b * 4 + (8 if u >= 2 else 4))

    @block.vector
    def _(dve):
        own = Count(dve, S["dve_own"])

        def lo_half(i, c, h):
            dve.wait_ge(S["hi_done"], i.val(6, 2 * c + h + 1))
            cut = slice(1024 * h, 1024 * (h + 1))
            dve.tensor_tensor(w_lo[:, c, cut], raw[:, i.raw_slot(c), cut], w_hi[:, c, cut].bitcast(F32),
                              ALU.subtract).then_inc(S["lo_done"], 1)

        def xg_low(i, src):
            dve.wait_ge(S["xg_hi"], i.val(1, 1))
            waited_apart(dve, S["tables_ready"])
            dve.tensor_tensor(xg[:, i.parity, :, SLOTS:], src, xg[:, i.parity, :, 0:SLOTS].bitcast(F32),
                              ALU.subtract).then_inc(S["xg_lo"], 1)

        def add_halves(i):
            dve.wait_ge(S["t_done"], i.val(1, 1))
            if not i.first:
                dve.wait_ge(S["mul_done"], i.val(1, 0))
            dve.tensor_tensor(up_sum[:], up_bank[0:SLOTS, :], t_half[:], ALU.add).then_inc(S["added"], 1)

        def multiply(i):
            dve.wait_ge(S["silu_done"], i.val(1, 1))
            if not i.first:
                dve.wait_ge(S["gt_ready"], i.val(1, 0))
            dve.tensor_tensor(g_sb[:], silu_sb[:], up_sum[:, FF:], ALU.mult).then_inc(S["mul_done"], 1)

        def make_onehots(column):
            for blk in range(TB):
                for it in range(BATCH_ITEMS):
                    ins = dve.tensor_scalar(onehot[:, blk, it], slot_id[:], item_pos[:, blk, column(it)], None,
                                            ALU.is_equal)
            ins.then_inc(S["onehot_made"], 1)

        def take_wslot(b1):
            dve.wait_ge(S["wslot_ready"], b1)
            dve.tensor_reduce(w_slot[:, 1], gather_bank[:, 0:2 * BATCH_ITEMS].rearrange("p (i c) -> p i c", c=2),
                              AX_X, ALU.add).then_inc(S["wslot_made"], 1)

        def move_wslot(b1):
            dve.wait_ge(S["wslot_made"], b1)
            dve.tensor_copy(w_slot[:, 0], w_slot[:, 1]).then_inc(S["wslot_moved"], 1)

        dve.nop().then_inc(S["s_made"], 1)
        g["norm_dve"](dve, own)
        for blk in range(TB):
            dve.tensor_scalar(xn[:, blk], x[:, blk], small[:, 4 + blk:5 + blk], None,
                              ALU.mult).then_inc(S["norm_ready"], 1)
        for blk in range(TB):
            dve.wait_ge(S["norm_act"], 3 + blk)
            dve.tensor_tensor(xn_lo[:, blk], xn[:, blk], xn_hi[:, blk].bitcast(F32), ALU.subtract
                              ).then_inc(S["norm_dve"], 1)
        dve.wait_ge(S["pool_own"], 6)
        own.inc(dve.tensor_copy(slot_id[:], iota_i[:].rearrange("p a s -> p (a s)")))
        own.inc(dve.tensor_copy(e_id[:], part_i[0:NE, 0:1]))
        own.step(dve.tensor_scalar(part_i[:, 1:2], part_i[:, 0:1], SLOTS - 1, None, ALU.bitwise_and))
        own.step(dve.tensor_copy(slot_of_row[:], part_i[:, 1:2]))
        item0 = Item(None, 0, first=True)
        for c in range(3):
            for h in range(2):
                lo_half(item0, c, h)

        dve.wait_ge(S["router_in"], 32)
        dve.wait_ge(S["sig_ready"], 1)
        own.step(dve.tensor_tensor(sel[:], scores[:], bias_row[:, None, :].to_broadcast([P, TB, NE]), ALU.add))
        for blk in range(TB):
            for gr in range(8):
                own.inc(dve.max(top[:, blk, gr], sel[:, blk, gr * GROUP:(gr + 1) * GROUP]))
        own.wait()
        own.step(dve.tensor_tensor(grp[:], top[:, :, :, 0], top[:, :, :, 1], ALU.add))
        for blk in range(TB):
            other = grp[:, blk, None, :].to_broadcast([P, 8, 8])
            this = grp[:, blk, :, None].to_broadcast([P, 8, 8])
            own.inc(dve.tensor_tensor(versus[:, 0], other, this, ALU.is_gt))
            own.step(dve.tensor_tensor(versus[:, 1], other, this, ALU.is_equal))
            own.step(dve.tensor_tensor(versus[:, 1], versus[:, 1], earlier[:], ALU.mult))
            own.step(dve.tensor_tensor(versus[:, 0], versus[:, 0], versus[:, 1], ALU.add))
            own.step(dve.tensor_reduce(grp[:, blk], versus[:, 0], AX_X, ALU.add))
            own.step(dve.tensor_scalar(grp[:, blk], grp[:, blk], float(TOPK_GROUPS), NEG, ALU.is_ge, ALU.mult))
            own.step(dve.tensor_tensor(sel[:, blk].rearrange("p (g e) -> p g e", g=8),
                                       sel[:, blk].rearrange("p (g e) -> p g e", g=8),
                                       grp[:, blk, :, None].to_broadcast([P, 8, GROUP]), ALU.add))
            own.step(dve.max(top[:, blk, 0], sel[:, blk]))
            own.step(dve.match_replace(chosen[:, blk], top[:, blk, 0], sel[:, blk], TAKEN))
            own.step(dve.tensor_scalar(chosen[:, blk], chosen[:, blk], 0.5 * TAKEN, None, ALU.is_le))
            own.step(dve.tensor_tensor(weight[:, blk], chosen[:, blk], scores[:, blk], ALU.mult))
            own.step(dve.tensor_reduce(sums[:, blk, 0:1], weight[:, blk], AX_X, ALU.add))
            own.step(dve.reciprocal(sums[:, blk, 1:2], sums[:, blk, 0:1]))
            own.step(dve.tensor_scalar(weight[:, blk], weight[:, blk], sums[:, blk, 1:2], ROUTED_SCALE,
                                       ALU.mult, ALU.mult))
        dve.nop().then_inc(S["sel_ready"], 1)

        dve.wait_ge(S["selt_ready"], 1)
        own.step(dve.tensor_copy(maskT_wT[:], bank[7][0:NE, :].rearrange("p (m t) -> p m t", m=2)))
        own.step(dve.tensor_tensor_scan(posT[:], ones[0:NE, :], maskT_wT[:, 0], 0.0, ALU.mult, ALU.add))
        count = posT[:, T - 1:T]
        for n in range(3):
            own.inc(dve.tensor_scalar(extra[:, n:n + 1], count, float(SLOTS * (n + 1)), None, ALU.is_gt))
        own.wait()
        own.step(dve.tensor_tensor(extra[:, 0:1], extra[:, 0:1], extra[:, 1:2], ALU.add))
        own.step(dve.tensor_tensor(extra[:, 0:1], extra[:, 0:1], extra[:, 2:3], ALU.add))
        own.step(dve.scalar_tensor_tensor(posT[:], posT[:], -1.0 - NOT_HERE, maskT_wT[:, 0], ALU.add, ALU.mult))
        own.step(dve.tensor_scalar(posT[:], posT[:], NOT_HERE - NO_ITEM, None, ALU.add))
        own.inc(dve.tensor_copy(pick[:, 0:NE], ident[0:NE, 0:NE]))
        own.step(dve.memset(shift[:, 0:NE], 0.0))
        dve.nop().then_inc(S["small_psum"], 1)
        for blk in range(TB):
            dve.wait_ge(S["shared_act"], blk + 1)
            dve.tensor_tensor(shared_g[:, blk], shared_g[:, blk], bank[4 + blk][:, FF:], ALU.mult
                              ).then_inc(S["shared_g"], 1)
        dve.wait_ge(S["small_taken"], 1)
        own.step(dve.tensor_copy(extra[:, 3:4], bank[7][0:NE, 0:1]))
        own.inc(dve.tensor_copy(extra_n[0:1, 0:1], bank[7][0:1, 1:2]))
        own.step(dve.tensor_tensor(extra[:, 4:5], extra[:, 3:4], extra[:, 0:1], ALU.add))
        ids = slot_id[0:NE, 0:MAX_EXTRA]
        own.inc(dve.tensor_scalar(sel_x[:, 0], ids, extra[:, 3:4], None, ALU.is_ge))
        own.step(dve.tensor_scalar(sel_x[:, 1], ids, extra[:, 4:5], None, ALU.is_lt))
        own.step(dve.tensor_tensor(pick[:, NE:], sel_x[:, 0], sel_x[:, 1], ALU.mult))
        own.step(dve.tensor_scalar(sel_x[:, 0], ids, extra[:, 3:4], None, ALU.subtract))
        own.step(dve.tensor_scalar(sel_x[:, 0], sel_x[:, 0], -float(SLOTS), -float(SLOTS), ALU.mult, ALU.add))
        own.step(dve.tensor_tensor(shift[:, NE:], sel_x[:, 0], pick[:, NE:], ALU.mult))
        own.step(dve.tensor_scalar(extra_n[0:1, 0:1], extra_n[0:1, 0:1], float(BATCH_ITEMS - 1), None, ALU.add))
        own.step(dve.tensor_copy(extra_b[0:1, 1:2], extra_n[0:1, 0:1]))
        own.step(dve.tensor_scalar(extra_b[0:1, 0:1], extra_b[0:1, 1:2], 2, None, ALU.arith_shift_right))
        dve.nop().then_inc(S["small_psum"], 1)
        dve.wait_ge(S["table_psum"], 1)
        own.inc(dve.tensor_copy(extra_e[:], bank[7][0:1, 0:MAX_EXTRA]))
        own.wait()
        dve.nop().then_inc(S["extra_in"], 1)
        pos = up_bank[:, 0:TB * P].rearrange("p (b i) -> p b i", b=TB)[:, :, 0:ITEMS]
        wts = up_bank[:, TB * P:2 * TB * P].rearrange("p (b i) -> p b i", b=TB)[:, :, 0:ITEMS]
        own.inc(dve.tensor_scalar(item_pos[:], pos, NO_ITEM, None, ALU.add))
        own.step(dve.tensor_copy(item_w[:, :, :, 0], wts))
        own.inc(dve.tensor_tensor(item_w[:, :, :, 1], wts, item_w[:, :, :, 0].bitcast(F32), ALU.subtract))
        own.step(dve.tensor_scalar(item_rows[:], y_bank[0][0:ITEMS, 0:T], NO_ITEM, 256.0, ALU.add, ALU.min))
        dve.nop().then_inc(S["tables_ready"], 1)
        make_onehots(lambda it: slice(it, it + 1))

        take_wslot(1)
        move_wslot(1)
        make_onehots(lambda it: slice(BATCH_ITEMS + it, BATCH_ITEMS + it + 1))
        for n in range(2):
            xg_low(Item(None, n), stage[:, 0, :, n * SLOTS:(n + 1) * SLOTS])
        add_halves(item0)
        multiply(item0)
        dve.wait_ge(own.sem, own.n)
        batches = dve.value_load(extra_b[0:1, 0:1], min_val=0, max_val=8)
        with dve.Fori(0, batches + NE // BATCH_ITEMS) as b:
            par = dve.snap(b % 2)
            nxt = dve.snap((b + 1) % 2)
            for u in range(BATCH_ITEMS):
                i = Item(b, u)
                i1 = i.next()
                lo_half(i1, 0, 0)
                dve.wait_ge(S["gt_hi"], i.val(1, 1))
                dve.tensor_tensor(gT[:, :, SLOTS:], y_bank[0][:, 0:2 * SLOTS].rearrange("p (j s) -> p j s", j=2),
                                  gT[:, :, 0:SLOTS].bitcast(F32), ALU.subtract).then_inc(S["gt_lo"], 1)
                lo_half(i1, 0, 1)
                if u == 0:
                    dve.wait_ge(S["pos_in"], b * 16 + 16)
                dve.wait_ge(S["scatter_done"], i.val(1, 1))
                dve.tensor_scalar(spread[:], pos_rows[:, bass.ds(par, 1), u].rearrange("p a t -> p (a t)"),
                                  slot_of_row[:], None, ALU.is_equal).then_inc(S["s_made"], 1)
                lo_half(i1, 1, 0)
                for half in range(2):
                    cut = slice(512 * half, 512 * (half + 1))
                    dve.wait_ge(S["y_hi"], i.val(2, half + 1))
                    dve.scalar_tensor_tensor(y_l[:, cut], y_bank[half][:], w_slot[:, 0, u:u + 1],
                                             y_h[:, cut].bitcast(F32), ALU.mult, ALU.subtract
                                             ).then_inc(S["y_lo"], 1)
                lo_half(i1, 1, 1)
                lo_half(i1, 2, 0)
                if u == 3:
                    take_wslot(b + 2)
                    move_wslot(b + 2)
                    make_onehots(lambda it: bass.ds(b * 4 + (8 + it), 1))
                lo_half(i1, 2, 1)
                add_halves(i1)
                v = (u + 2) % BATCH_ITEMS
                which = par if u < 2 else nxt
                multiply(i1)
                xg_low(i.next(2), stage[:, bass.ds(which, 1), :, v * SLOTS:(v + 1) * SLOTS].rearrange(
                    "p a k s -> p (a k) s"))
        dve.wait_ge(S["pos_in"], batches * 16 + (NE // BATCH_ITEMS + 1) * 16)
        dve.wait_ge(S["acc_ready"], 1)
        for blk in range(TB):
            for half in range(2):
                cut = slice(512 * half, 512 * (half + 1))
                own.step(dve.tensor_tensor(scaled[:], gate_ffn[:, cut], acc[2 * blk + half][:], ALU.mult))
                own.step(dve.tensor_tensor(x[:, blk, cut], x[:, blk, cut], scaled[:], ALU.add))

    @block.tensor
    def _(pe):
        def up(i, c):
            pe.wait_ge(S["lo_done"], i.val(6, 2 * c + 2))
            if c == 0:
                pe.wait_ge(S["xg_lo"], i.val(1, 1))
                if not i.first:
                    pe.wait_ge(S["added"], i.val(1, 0))
            for kk in range(4):
                k = 4 * c + kk
                for w in (w_hi, w_lo):
                    mm = pe.matmul(up_bank[:], xg[:, i.parity, k], piece(c, w[:, c])[:, :, kk],
                                   start=(k == 0 and w is w_hi), stop=(k == KD - 1 and w is w_lo))
            mm.then_inc(S["a_free" if c == 0 else "b_free"], 1)

        def down(i):
            pe.wait_ge(S["gt_lo"], i.val(1, 1))
            pe.wait_ge(S["lo_done"], i.val(6, 6))
            for half in range(2):
                for j in range(2):
                    for w in (w_hi, w_lo):
                        mm = pe.matmul(y_bank[half][:], gT[:, j], piece(2, w[:, 2])[:, j, 512 * half:512 * half + 512],
                                       start=(j == 0 and w is w_hi), stop=(j == 1 and w is w_lo))
                mm.then_inc(S["down_done"], 1)

        def scatter(i):
            pe.wait_ge(S["s_made"], i.val(1, 2))
            pe.wait_ge(S["y_lo"], i.val(2, 2))
            for blk in range(TB):
                for half in range(2):
                    for y in (y_h, y_l):
                        mm = pe.matmul(acc[2 * blk + half][:], spread[:, blk * P:(blk + 1) * P],
                                       y[:, 512 * half:512 * half + 512], start=False, stop=False,
                                       skip_group_check=True)
            mm.then_inc(S["scatter_done"], 1)

        def turn_g(i):
            waited_apart(pe, S["logits_ready"])
            pe.wait_ge(S["mul_done"], i.val(1, 1))
            for j in range(2):
                mm = pe.transpose(y_bank[0][:, j * SLOTS:(j + 1) * SLOTS], g_sb[:, j * P:(j + 1) * P],
                                  ident[0:SLOTS, 0:SLOTS])
            mm.then_inc(S["gt_ready"], 1)

        def gather(pair, waits):
            for sem_name, value in waits:
                pe.wait_ge(S[sem_name], value)
            for j in range(2):
                k = 2 * pair + j
                for blk in range(TB):
                    for xs in (xn_hi, xn_lo):
                        mm = pe.matmul(gather_bank[:, 256 * j:256 * (j + 1)], xs[:, blk, k::KD],
                                       onehot[:, blk, :, 0:SLOTS],
                                       start=(blk == 0 and xs is xn_hi), stop=(blk == TB - 1 and xs is xn_lo))
            mm.then_inc(S["gather_ready"], 1)

        def slot_weights(taken, column):
            pe.wait_ge(S["gather_taken"], taken)
            for it in range(BATCH_ITEMS):
                for blk in range(TB):
                    mm = pe.matmul(gather_bank[:, 2 * it:2 * it + 2],
                                   onehot[:, blk, it], item_w[:, blk, column(it)],
                                   start=(blk == 0), stop=(blk == TB - 1))
            mm.then_inc(S["wslot_ready"], 1)

        pe.nop().then_inc(S["down_done"], 1)
        pe.nop().then_inc(S["scatter_done"], 1)
        pe.wait_ge(S["norm_ready"], TB)
        g["turn_pe"](pe, xn, bank[4:8])
        pe.wait_ge(S["hT_ready"], 1)
        pe.wait_ge(S["router_in"], 32)
        for blk in range(TB):
            for k in range(KD):
                mm = pe.matmul(bank[7][:, blk * NE:(blk + 1) * NE], hT[:, k, blk * P:(blk + 1) * P], router_w[:, k],
                               start=(k == 0), stop=(k == KD - 1))
        mm.then_inc(S["logits_ready"], 1)
        for blk in range(TB):
            for c in range(2):
                pe.wait_ge(raw_loaded[c], 32)
                for kk in range(4):
                    k = 4 * c + kk
                    mm = pe.matmul(bank[4 + blk][:], hT[:, k, blk * P:(blk + 1) * P], piece(c, raw[:, c])[:, :, kk],
                                   start=(k == 0), stop=(k == KD - 1))
            mm.then_inc(S["shared_up"], 1)
        pe.wait_ge(S["shared_up"], 2)
        pe.sem_inc(S["shared_used"], 2)
        pe.wait_ge(S["sel_ready"], 1)
        for m, src in enumerate((chosen, weight)):
            for blk in range(TB):
                mm = pe.transpose(bank[7][0:NE, m * T + blk * P:m * T + (blk + 1) * P], src[:, blk], ident[:])
        mm.then_inc(S["selt_ready"], 1)
        for blk in range(TB):
            pe.wait_ge(S["shared_g"], blk + 1)
            for j in range(2):
                mm = pe.transpose(bank[6][:, j * T + blk * P:j * T + (blk + 1) * P], shared_g[:, blk, j * P:(j + 1) * P],
                                  ident[:])
        mm.then_inc(S["shared_gt"], 1)
        pe.wait_ge(S["small_psum"], 1)
        pe.matmul(bank[7][0:NE, 0:1], earlier_e[:], extra[:, 0:1], start=True, stop=True)
        pe.matmul(bank[7][:, 1:2], ones[0:NE, 0:P], extra[:, 0:1], start=True, stop=True).then_inc(S["small_taken"], 1)
        pe.wait_ge(S["shared_gt_taken"], 1)
        pe.wait_ge(raw_loaded[2], 32)
        for blk in range(TB):
            for half in range(2):
                for j in range(2):
                    mm = pe.matmul(acc[2 * blk + half][:], shared_gT[:, j, blk * P:(blk + 1) * P],
                                   piece(2, raw[:, 2])[:, j, 512 * half:512 * half + 512], start=(j == 0), stop=False,
                                   skip_group_check=True)
        mm.then_inc(S["shared_used"], 1)
        pe.wait_ge(S["small_psum"], 2)
        for blk in range(TB):
            cut = slice(blk * P, blk * P + ITEMS)
            pe.matmul(up_bank[:, cut], posT[:, blk * P:(blk + 1) * P], pick[:], start=True, stop=False)
            pe.matmul(up_bank[:, cut], ones[0:NE, 0:P], shift[:], start=False, stop=True)
        for blk in range(TB):
            cut = slice((TB + blk) * P, (TB + blk) * P + ITEMS)
            pe.matmul(up_bank[:, cut], maskT_wT[:, 1, blk * P:(blk + 1) * P], pick[:], start=True, stop=True)
        pe.matmul(y_bank[0][0:ITEMS, 0:T], pick[:], posT[:], start=True, stop=False)
        pe.matmul(y_bank[0][0:ITEMS, 0:T], shift[:], ones[0:NE, :], start=False, stop=True)
        pe.matmul(bank[7][0:1, 0:MAX_EXTRA], e_id[:], pick[:, NE:], start=True, stop=True
                  ).then_inc(S["table_psum"], 1)
        pe.wait_ge(S["norm_dve"], 1 + TB)
        for pair in range(4):
            gather(pair, [("onehot_made", 1)] + ([("gather_taken", pair)] if pair else []))
        slot_weights(4, lambda it: it)
        item0 = Item(None, 0, first=True)
        up(item0, 0)
        up(item0, 1)
        turn_g(item0)
        pe.wait_ge(S["extra_in"], 1)
        batches = pe.value_load(extra_b[0:1, 0:1], min_val=0, max_val=8)
        with pe.Fori(0, batches + NE // BATCH_ITEMS) as b:
            for u in range(BATCH_ITEMS):
                i = Item(b, u)
                i1 = i.next()
                down(i)
                up(i1, 0)
                if u < 2:
                    gather(2 * u, [("onehot_made", b + 2), ("wslot_made", b + 1)]
                           + [("gather_taken", b * 4 + (4 + 2 * u))])
                up(i1, 1)
                scatter(i)
                turn_g(i1)
                if u < 2:
                    gather(2 * u + 1, [("gather_taken", b * 4 + (5 + 2 * u))])
                if u == 2:
                    slot_weights(b * 4 + 8, lambda it: pe.snap(b * 4 + (4 + it)))
        pe.wait_ge(S["scatter_done"], batches * 4 + (NE + 1))
        pe.nop().then_inc(S["acc_ready"], 1)


def waited_apart(eng, sem):
    eng.wait_ge(sem, 1)


class Item:

    def __init__(self, b, off, first=False, early=False):
        self.b, self.off, self.first, self.early = b, off, first, early

    def val(self, a, c):
        return a * self.off + c if self.b is None else self.b * (4 * a) + (a * self.off + c)

    def next(self, n=1):
        return Item(self.b, self.off + n)

    @property
    def parity(self):
        return self.off % 2

    def raw_slot(self, c):
        return 3 * (1 - self.parity) + c

    def uses_val(self, a):
        n = self.off // 2 + 1 + self.parity
        return a * n if self.b is None else self.b * (2 * a) + a * n


_INS = ["x", "c", "positions", "ada_mix_w", "ada_mix_b", "norm_mix_g", "w_in", "pool_w", "pool_scale",
        "cq_norm_g", "ckv_norm_g", "w_uq", "w_ukv", "w_oa", "w_ob", "w_oc", "w_out", "ada_ffn_w", "ada_ffn_b",
        "norm_ffn_g", "router_w", "router_bias", "exp_w1", "exp_w3", "exp_w2", "sh_w1", "sh_w3", "sh_w2",
        "final_g"]


def kernel(**inputs):
    import concourse.bacc as bacc
    from concourse.bass_utils import run_bass_kernel_spmd

    nc = bacc.Bacc("TRN2", target_bir_lowering=False, num_devices=1)
    arrays, tensors = {}, {}
    for name in _INS:
        a = np.ascontiguousarray(inputs[name])
        arrays[f"in_{name}"] = a
        tensors[name] = nc.dram_tensor(f"in_{name}", a.shape, mybir.dt.from_np(a.dtype), kind="ExternalInput").ap()
    out = nc.dram_tensor("out_y", (1, T, D), F32, kind="ExternalOutput").ap()
    hybrid_trunk(nc, tensors, out)
    r = run_bass_kernel_spmd(nc, [arrays], core_ids=[0])
    return r.results[0]["out_y"]
```

```python
from contextlib import ExitStack
import math

import numpy as np
import concourse.bass as bass
import concourse.mybir as mybir

F32 = mybir.dt.float32
F32R = mybir.dt.float32r
BF16 = mybir.dt.bfloat16
I32 = mybir.dt.int32
ALU = mybir.AluOpType
ACT = mybir.ActivationFunctionType
AX_X = mybir.AxisListType.X

P = 128
D = 1024
KD = D // P
T = 256
TB = T // P
DEPTH = 2
DH = 64
HEADS_A = 12
DILATIONS = (1, 4, 16)
N_BACK = 128
DA = HEADS_A * DH
DB = 512
WINDOWS = (2, 4, 8, 16)
HEADS_C = 8
NOPE, ROPE = 64, 32
QK = NOPE + ROPE
Q_LORA, KV_LORA = 384, 256
JQ, JKV = Q_LORA // P, KV_LORA // P
DC = HEADS_C * DH
HEADS = HEADS_A + HEADS_C
NE = 64
FF = 256
GROUP = 8
TOPK_GROUPS = 4
ROUTED_SCALE = 2.5
EPS = 1e-6
NEG = -1e30
TAKEN = -3e38
SLOTS = 64
BATCH_ITEMS = 4
MAX_EXTRA = 40
ITEMS = NE + MAX_EXTRA
NOT_HERE = 512.0
NO_ITEM = 1024.0
W_SLOTS = 2
ADA_SLOTS = 2
RAW = 6

HI = ("hi_a", "hi_b", "hi_c")
LO = ("lo_a", "lo_b", "lo_c")

COL_QK, COL_V = 0, 2 * DA
COL_U = 3 * DA
COL_C = COL_U + DB
COL_KR = COL_C + Q_LORA + KV_LORA
COL_G = COL_KR + ROPE
N_IN = COL_G + 3 * D

W_LOADS = [("w_in", COL_U, 512), ("w_in", COL_C, 512), ("w_in", COL_C + 512, 160)]
W_LOADS += [("w_in", COL_QK + 512 * i, 512) for i in range(3)]
W_LOADS += [("w_in", COL_V, 512), ("w_in", COL_V + 512, 256), ("w_uq", 0, 0), ("w_ukv", 0, 0)]
W_LOADS += [("w_in", COL_G + 512 * i, 512) for i in range(6)]
W_LOADS += [("w_o", 0, 512), ("w_o", 512, 512), ("w_out", 0, 512), ("w_out", 512, 512)]
W_BRANCH_ROWS = (("w_oa", 0, 2), ("w_ob", 2, 4), ("w_oc", 6, 4))
W_AT = {}
for _n, _load in enumerate(W_LOADS):
    W_AT.setdefault(_load[:2], _n)
W_LANDED = []
for _n, _load in enumerate(W_LOADS):
    W_LANDED.append((W_LANDED[_n - W_SLOTS] if _n >= W_SLOTS else 0) + (48 if _load[0] == "w_o" else 16))

UNITS = [(pair, qb) for pair in range(HEADS // 2) for qb in range(TB)]
GATE_GROUPS = [(c, blk) for c in range(6) for blk in range(TB)]


class Count:

    def __init__(self, eng, sem):
        self.eng, self.sem, self.n = eng, sem, 0

    def inc(self, ins):
        self.n += 1
        ins.then_inc(self.sem, 1)

    def wait(self):
        self.eng.wait_ge(self.sem, self.n)

    def step(self, ins):
        self.inc(ins)
        self.wait()


def hybrid_trunk(nc, t, out):
    stack = ExitStack()
    with stack:
        def sb(name, shape, dt=F32, where=stack):
            return where.enter_context(nc.sbuf_tensor(name, shape, dt))

        def sem(name):
            return stack.enter_context(nc.semaphore(name))

        bank = [stack.enter_context(nc.psum_tensor(f"bank{i}", [P, 512], F32)) for i in range(8)]

        x = sb("x", [P, TB, D])
        ident = sb("ident", [P, P])
        ones = sb("ones", [P, T])
        mask = sb("mask", [P, 3, TB, T], BF16)
        rcount = sb("rcount", [P, len(WINDOWS), 16])
        cos_sin = sb("cos_sin", [P, TB, 2, ROPE // 2])
        silu_c = sb("silu_c", [P, KD])
        mod_a = sb("mod_a", [P, 2, KD])
        mod_b = sb("mod_b", [P, 2, KD])
        gate_ffn = sb("gate_ffn", [P, D])
        small = sb("small", [P, 16])
        item_scratch = nc.dram_tensor("item_scratch", [ITEMS, T], BF16, kind="Internal").ap()

        s_first = sem("s_first")
        setup_dma = sem("setup_dma")
        pool_setup = sem("pool_setup")
        act_setup = sem("act_setup")
        dve_setup = sem("dve_setup")
        s_last = setup_dma

        with ExitStack() as scope, nc.Block() as block:
            diff = sb("diff", [P, TB, T], I32, scope)
            low = sb("low", [P, TB, T], I32, scope)
            dist = sb("dist", [P, TB, T], F32, scope)
            ok = sb("ok", [P, TB, T], F32, scope)
            ok2 = sb("ok2", [P, TB, T], F32, scope)
            tok = sb("tok", [P, 16], I32, scope)
            tokf = sb("tokf", [P, 16], F32, scope)
            pos_i = sb("pos_i", [P, TB], I32, scope)
            pos_f = sb("pos_f", [P, TB], F32, scope)
            ang = sb("ang", [P, TB, 2, ROPE // 2], F32, scope)
            turns = sb("turns", [P, TB, 2, ROPE // 2], F32, scope)
            c_col = sb("c_col", [P, KD], F32, scope)

            @block.sync
            def _(sp):
                sp.dma_start(x[:], t["x"][0].rearrange("(b p) d -> p b d", p=P)).then_inc(setup_dma, 16)
                sp.dma_start(c_col[:], t["c"][0].rearrange("(p k) -> p k", k=KD)).then_inc(setup_dma, 16)
                sp.dma_start(pos_i[:], t["positions"][0].rearrange("(b p) -> p b", p=P),
                             allow_slow_non_contiguous=True).then_inc(setup_dma, 16)
                sp.wait_ge(setup_dma, 48)

            @block.gpsimd
            def _(pool):
                pool.memset(ident[:], 0.0).then_inc(pool_setup, 1)
                pool.memset(ones[:], 1.0).then_inc(pool_setup, 1)
                pool.iota(diff[:], [[P, TB], [-1, T]], base=0, channel_multiplier=1).then_inc(pool_setup, 1)
                pool.iota(tok[:], [[1, 16]], base=1, channel_multiplier=0).then_inc(pool_setup, 1)
                pool.wait_ge(pool_setup, 4)
                pool.affine_select(out=ident[:], in_=ident[:], compare_op=ALU.not_equal, fill=1.0, base=0,
                                   pattern=[[-1, P]], channel_multiplier=1).then_inc(pool_setup, 1)

            @block.scalar
            def _(act):
                act.wait_ge(setup_dma, 48)
                act.activation(silu_c[:], c_col[:], ACT.Silu).then_inc(act_setup, 1)
                act.wait_ge(dve_setup, 1)
                act.activation(cos_sin[:], ang[:], ACT.Sin).then_inc(act_setup, 1)

            @block.vector
            def _(dve):
                own = Count(dve, s_first)
                dve.wait_ge(setup_dma, 48)
                own.step(dve.tensor_copy(pos_f[:], pos_i[:]))
                freqs = (np.float32(10000.0) ** (-np.arange(0, ROPE, 2, dtype=np.float32) / np.float32(ROPE)))
                for blk in range(TB):
                    for i, f in enumerate(freqs):
                        for part in range(2):
                            own.inc(dve.tensor_scalar(ang[:, blk, part, i:i + 1], pos_f[:, blk:blk + 1],
                                                      float(f), None, ALU.mult))
                own.wait()
                for part, quarter in ((0, 0.25), (1, 0.0)):
                    own.inc(dve.tensor_scalar(turns[:, :, part], ang[:, :, part], 1 / (2 * math.pi), quarter,
                                              ALU.mult, ALU.add))
                own.wait()
                magic = 1.5 * 2 ** 23
                own.step(dve.tensor_scalar(turns[:], turns[:], magic, None, ALU.add))
                own.step(dve.tensor_scalar(turns[:], turns[:], magic, None, ALU.subtract))
                first = 6.28125
                second = float(np.float32(math.floor((2 * math.pi - first) * 2 ** 20) / 2 ** 20))
                third = 2 * math.pi - first - second
                for piece in (first, second, third):
                    own.step(dve.scalar_tensor_tensor(ang[:], turns[:], -piece, ang[:], ALU.mult, ALU.add))
                own.step(dve.tensor_scalar(ang[:, :, 0], ang[:, :, 0], math.pi / 2, None, ALU.add))
                dve.tensor_scalar(ang[:], ang[:], 3.1415925, -3.1415925, ALU.min, ALU.max).then_inc(dve_setup, 1)
                dve.wait_ge(pool_setup, 5)
                own.step(dve.tensor_copy(dist[:], diff[:]))
                for g, dil in enumerate(DILATIONS):
                    own.step(dve.tensor_scalar(low[:], diff[:], dil - 1, None, ALU.bitwise_and))
                    own.step(dve.tensor_copy(ok[:], low[:]))
                    own.step(dve.tensor_scalar(ok[:], ok[:], 0.0, None, ALU.is_equal))
                    own.step(dve.tensor_scalar(ok2[:], dist[:], 0.0, None, ALU.is_ge))
                    own.step(dve.tensor_tensor(ok[:], ok[:], ok2[:], ALU.mult))
                    own.step(dve.tensor_scalar(ok2[:], dist[:], float(N_BACK * dil), None, ALU.is_le))
                    own.step(dve.tensor_tensor(ok[:], ok[:], ok2[:], ALU.mult))
                    own.step(dve.tensor_scalar(mask[:, g], ok[:], 1.0, -NEG, ALU.subtract, ALU.mult))
                own.step(dve.tensor_copy(tokf[:], tok[:]))
                for g, w in enumerate(WINDOWS):
                    own.inc(dve.tensor_scalar(rcount[:, g], tokf[:], float(w), None, ALU.min))
                own.wait()
                own.step(dve.reciprocal(rcount[:], rcount[:]))

        nc.all_engine_barrier(sems_to_clear=range(s_first.num, dve_setup.num + 1))

        names = """norm_act norm_dve norm_ready turned_ready act_own dve_own pool_own w_used ada_used ada_summed
            ada_bcast mod_ready consts_in hT_ready proj_ready proj_taken sums_ready rstd_sq latent_ready
            rope_ready qt_ready qt_taken pooled_ready mixed_ready mixed_taken s_ready s_taken max_ready
            p_ready pt_ready pt_taken o_ready o_taken coef_in coef_out y_ready yt_ready yt_taken
            branch_ready branch_taken mix_ready mixt_ready mixt_taken res_ready router_in logits_ready
            sig_ready sel_ready selt_ready tables_ready table_psum small_psum small_taken scratch_written
            extra_in shared_up shared_act shared_g shared_gt shared_gt_taken shared_used hi_a hi_b hi_c lo_a lo_b lo_c
            a_free b_free added silu_done mul_done gt_ready gt_hi gt_lo down_done y_hi y_lo s_made
            gather_ready gather_taken onehot_made wslot_ready wslot_made wslot_moved xg_hi xg_lo
            scatter_done t_done pos_in acc_ready out_done final_in""".split()
        S = {}
        for n in names:
            S[n] = sem(n)
        w_loaded = [sem(f"w_loaded{i}") for i in range(W_SLOTS)]
        ada_loaded = [sem(f"ada_loaded{i}") for i in range(ADA_SLOTS)]
        raw_loaded = [sem(f"raw_loaded{i}") for i in range(RAW)]
        block_sems = range(S[names[0]].num, raw_loaded[-1].num + 1)

        def norm_act(act, own, squares):
            for blk in range(TB):
                own.inc(act.activation(squares, x[:, blk], ACT.Square, accum_out=small[:, blk:blk + 1]))
                own.wait()
            act.nop().then_inc(S["norm_act"], 1)
            act.wait_ge(S["norm_dve"], 1)
            act.activation(small[:, 4:6], small[:, 2:4], ACT.Sqrt).then_inc(S["norm_act"], 1)

        def norm_dve(dve, own):
            dve.wait_ge(S["norm_act"], 1)
            own.step(dve.tensor_scalar(small[:, 6:8], small[:, 0:2], 1.0 / D, EPS, ALU.mult, ALU.add))
            dve.reciprocal(small[:, 2:4], small[:, 6:8]).then_inc(S["norm_dve"], 1)
            dve.wait_ge(S["norm_act"], 2)
            own.step(dve.tensor_tensor(small[:, 8:10], small[:, 4:6], small[:, 4:6], ALU.mult))
            own.step(dve.tensor_tensor(small[:, 8:10], small[:, 8:10], small[:, 6:8], ALU.mult))
            own.step(dve.tensor_scalar(small[:, 8:10], small[:, 8:10], -0.5, 1.5, ALU.mult, ALU.add))
            own.step(dve.tensor_tensor(small[:, 4:6], small[:, 4:6], small[:, 8:10], ALU.mult))

        def turn_pe(pe, xn, banks):
            for k in range(KD):
                for blk in range(TB):
                    mm = pe.transpose(banks[k // 2][:, (k % 2) * T + blk * P:(k % 2) * T + blk * P + P],
                                      xn[:, blk, k::KD], ident[:])
                if k % 2:
                    mm.then_inc(S["turned_ready"], 1)

        def modulate_act(act, hT, banks, which):
            for k in range(KD):
                if k % 2 == 0:
                    act.wait_ge(S["turned_ready"], k // 2 + 1)
                mm = act.activation(hT[:, k], banks[k // 2][:, (k % 2) * T:(k % 2 + 1) * T], ACT.Identity,
                                    bias=mod_b[:, which, k:k + 1], scale=mod_a[:, which, k:k + 1])
            mm.then_inc(S["hT_ready"], 1)

        stages = dict(locals())
        with nc.Fori(0, DEPTH) as layer:
            with ExitStack() as scope, nc.Block() as block:
                mixer_block(nc, t, layer, stages, lambda n, s, d=F32: sb(n, s, d, scope), block)
            nc.all_engine_barrier(sems_to_clear=block_sems)
            with ExitStack() as scope, nc.Block() as block:
                experts_block(nc, t, layer, stages, lambda n, s, d=F32: sb(n, s, d, scope), block)
            nc.all_engine_barrier(sems_to_clear=block_sems)

        with ExitStack() as scope, nc.Block() as block:
            squares = sb("squares", [P, D], F32, scope)
            final_g = sb("final_g_row", [P, D], F32, scope)
            y = sb("y_out", [P, TB, D], F32, scope)

            @block.sync
            def _(sp):
                sp.dma_start(final_g[:], t["final_g"].rearrange("(a d) -> a d", a=1).to_broadcast([P, D])
                             ).then_inc(S["final_in"], 16)
                for blk in range(TB):
                    sp.wait_ge(S["norm_ready"], blk + 1)
                    sp.dma_start(out[0, blk * P:(blk + 1) * P, :], y[:, blk]).then_inc(S["out_done"], 16)
                sp.wait_ge(S["out_done"], 16 * TB)

            @block.scalar
            def _(act):
                norm_act(act, Count(act, S["act_own"]), squares[:])

            @block.vector
            def _(dve):
                norm_dve(dve, Count(dve, S["dve_own"]))
                dve.wait_ge(S["final_in"], 16)
                for blk in range(TB):
                    dve.scalar_tensor_tensor(y[:, blk], x[:, blk], small[:, 4 + blk:5 + blk], final_g[:],
                                             ALU.mult, ALU.mult).then_inc(S["norm_ready"], 1)


def mixer_block(nc, t, layer, g, sb, block):
    S, bank, x, ident, ones = g["S"], g["bank"], g["x"], g["ident"], g["ones"]
    mask, rcount, cos_sin, silu_c = g["mask"], g["rcount"], g["cos_sin"], g["silu_c"]
    mod_a, mod_b, gate_ffn, small = g["mod_a"], g["mod_b"], g["gate_ffn"], g["small"]
    w_loaded, ada_loaded = g["w_loaded"], g["ada_loaded"]

    hT = sb("m_hT", [P, KD, T])
    xn_o = sb("xn_o", [P, TB * HEADS * DH])
    xn = xn_o[:, 0:TB * D].rearrange("p (b d) -> p b d", b=TB)
    heads_o = xn_o[:, :].rearrange("p (b h e) -> p b h e", b=TB, h=HEADS)
    qk_t = sb("qk_t", [P, 12 * T])
    qkT = qk_t[:, :].rearrange("p (j t) -> p j t", j=12)
    yT = qk_t[:, 0:6 * T].rearrange("p (j t) -> p j t", j=6)
    va = sb("va", [P, TB, DA])
    uT = sb("uT", [P, 4, T])
    ybT = uT
    latent = sb("latent", [P, 5, T])
    tanh_g = sb("tanh_g", [P, TB, 3 * D])
    q_y = sb("q_y", [P, TB, (HEADS_C + 1) * QK])
    y_nat = q_y[:, :, 0:768]
    qT_mix = sb("qT_mix", [P, 8 * T])
    qcT = qT_mix[0:QK, :].rearrange("p (h t) -> p h t", h=8)
    raw_c = qT_mix[:, 0:5 * T].rearrange("p (j t) -> p j t", j=5)
    mix = qT_mix[:, :].rearrange("p (b d) -> p b d", b=TB)
    kT_mixT = sb("kT_mixT", [P, 8 * T])
    kcT = kT_mixT[0:QK, :].rearrange("p (h t) -> p h t", h=8)
    sq_c = kT_mixT[:, 0:5 * T].rearrange("p (j t) -> p j t", j=5)
    mixT = kT_mixT[:, :].rearrange("p (k t) -> p k t", k=KD)
    vc = sb("vc", [P, TB, DC])
    att = sb("att", [P, 3, 2, 2, T])
    s_sb, p_sb, pt_sb = att[:, 0], att[:, 1], att[:, 2]
    flat = att[:, :, :, :, :].rearrange("p a b c t -> p (a b c t)")
    pooled = flat[:, 0:4 * T].rearrange("p (g t) -> p g t", g=4)
    cs = flat[:, 4 * T:4 * T + 4 * (16 + T)].rearrange("p (g t) -> p g t", g=4)
    squares = flat[:, 0:D]
    rope_t = sb("rope_t", [P, 4, HEADS_C + 1, ROPE // 2])
    neg_max = sb("neg_max", [P, TB, HEADS])
    den = sb("den", [P, TB, HEADS])
    fac = sb("fac", [P, 4, HEADS_A])
    gate_mix = sb("gate_mix", [P, D])
    scaled = sb("scaled", [P, 3, 512])
    rstd = scaled[:, 0:2].rearrange("p a (b t) -> p a b t", b=2)
    wring = sb("wring", [P, W_SLOTS, 5120])
    ada_ring = sb("ada_ring", [P, ADA_SLOTS, 1536])
    ada_acc = sb("ada_acc", [P, 3 * D])
    pool_w = sb("pool_w_sb", [P, 4, P])
    cols = sb("cols", [P, 64])
    g_col = [cols[:, 0:8], cols[:, 8:16]]
    shift_col = [cols[:, 16:24], cols[:, 24:32]]
    scale_col = [cols[:, 32:40], cols[:, 40:48]]
    pscale = cols[:, 48:52]
    lat_g = cols[:, 52:57]
    gates_row = (gate_mix, gate_ffn)
    N_SMALL = 12

    def w_view(n, rows, width):
        return wring[:, n % W_SLOTS, 0:rows * width].rearrange("p (r n) -> p r n", r=rows)

    first = [("T", W_AT["w_in", COL_U], 0, 2, uT[:, 0:2]), ("T", W_AT["w_in", COL_U], 256, 2, uT[:, 2:4]),
             ("C", W_AT["w_in", COL_C], 0, 2, 0), ("C", W_AT["w_in", COL_C], 256, 2, 2),
             ("C", W_AT["w_in", COL_C + 512], 0, 1, 4),
             ("N2", W_AT["w_in", COL_C + 512], 128, ROPE, q_y[:, :, HEADS_C * QK + NOPE:])]
    second = []
    for i in range(3):
        for half in range(2):
            second.append(("T", W_AT["w_in", COL_QK + 512 * i], 256 * half, 2,
                           qkT[:, 4 * i + 2 * half:4 * i + 2 * half + 2]))
    second += [("N", W_AT["w_in", COL_V], 0, (blk, 512), va[:, blk, 0:512]) for blk in range(TB)]
    second += [("N2", W_AT["w_in", COL_V + 512], 0, 256, va[:, :, 512:768])]
    second += [("Q", W_AT["w_uq", 0], 0, (blk, 512), q_y[:, blk, 0:512]) for blk in range(TB)]
    second += [("Q2", W_AT["w_uq", 0], 512, 256, q_y[:, :, 512:768])]
    second += [("K", W_AT["w_ukv", 0], 2 * h, 2, kcT[0:NOPE, 2 * h:2 * h + 2]) for h in range(4)]
    second += [("V", W_AT["w_ukv", 0], 0, blk, vc[:, blk]) for blk in range(TB)]
    gates = [("G", W_AT["w_in", COL_G + 512 * c], 0, (blk, 512), tanh_g[:, blk, 512 * c:512 * c + 512])
             for c, blk in GATE_GROUPS]
    projections = first + second + gates
    last_of_load = {p[1]: n for n, p in enumerate(projections)}

    def gates_at(u):
        n = len(GATE_GROUPS)
        return range(u * n // 20, (u + 1) * n // 20) if u < 20 else range(0)

    def scales(pair):
        return DH ** -0.5 if pair < 6 else QK ** -0.5

    @block.sync
    def _(sp):
        for n, (src, col, width) in enumerate(W_LOADS):
            if n >= W_SLOTS:
                sp.wait_ge(S["w_used"], n - W_SLOTS + 1)
            if src == "w_o":
                for name, row, rows in W_BRANCH_ROWS:
                    sp.dma_start(w_view(n, 10, 512)[:, row:row + rows],
                                 t[name][layer][:, col:col + 512].rearrange("(j p) n -> p j n", p=P)
                                 ).then_inc(w_loaded[n % W_SLOTS], 16)
                continue
            w = t[src][layer]
            if src in ("w_in", "w_out"):
                dst = w_view(n, KD, width)
                sp.dma_start(dst, w[:, col:col + width].rearrange("(p k) n -> p k n", k=KD)
                             ).then_inc(w_loaded[n % W_SLOTS], 16)
            else:
                rows, width = w.shape[0] // P, w.shape[1]
                sp.dma_start(w_view(n, rows, width), w.rearrange("(j p) n -> p j n", p=P)
                             ).then_inc(w_loaded[n % W_SLOTS], 16)

    @block.scalar
    def _(act):
        own = Count(act, S["act_own"])
        loads = [(pool_w[:], t["pool_w"][layer].rearrange("g c d -> c g d")),
                 (pscale, t["pool_scale"][layer].rearrange("(g p) -> p g", p=P)),
                 (lat_g[:, 0:JQ], t["cq_norm_g"][layer].rearrange("(j p) -> p j", p=P)),
                 (lat_g[:, JQ:5], t["ckv_norm_g"][layer].rearrange("(j p) -> p j", p=P))]
        for i, kind in enumerate(("mix", "ffn")):
            bias = t[f"ada_{kind}_b"][layer]
            loads += [(g_col[i], t[f"norm_{kind}_g"][layer].rearrange("(p k) -> p k", k=KD)),
                      (shift_col[i], bias[0:D].rearrange("(p k) -> p k", k=KD)),
                      (scale_col[i], bias[D:2 * D].rearrange("(p k) -> p k", k=KD)),
                      (gates_row[i][0:1], bias[2 * D:3 * D].rearrange("(a d) -> a d", a=1))]
        assert len(loads) == N_SMALL

        def load_ada(n):
            src = t["ada_mix_w" if n < 2 * KD else "ada_ffn_w"][layer].rearrange("(p k) n -> p k n", k=KD)
            k, half = (n // 2) % KD, n % 2
            if n >= ADA_SLOTS:
                act.wait_ge(S["ada_used"], n - ADA_SLOTS + 1)
            act.dma_start(ada_ring[:, n % ADA_SLOTS], src[:, k, 1536 * half:1536 * (half + 1)]
                          ).then_inc(ada_loaded[n % ADA_SLOTS], 16)

        for n in range(ADA_SLOTS):
            load_ada(n)
        for dst, src in loads:
            act.dma_start(dst, src, allow_slow_non_contiguous=True).then_inc(S["consts_in"], 16)
        for n in range(ADA_SLOTS, 4):
            load_ada(n)
        g["norm_act"](act, own, squares)
        for n in range(4, 2 * KD + ADA_SLOTS):
            load_ada(n)
        act.wait_ge(S["mod_ready"], 1)
        g["modulate_act"](act, hT, bank[2:6], 0)

        def take_projection(n):
            kind, load, col, size, dst = projections[n]
            act.wait_ge(S["proj_ready"], n + 1)
            ps = bank[n % 2]
            if kind in ("T", "K"):
                rows = P if kind == "T" else NOPE
                ins = act.activation(dst, ps[0:rows, 0:size * T].rearrange("p (j t) -> p j t", j=size), ACT.Copy)
            elif kind == "C":
                src = ps[:, 0:size * T].rearrange("p (j t) -> p j t", j=size)
                act.activation(raw_c[:, dst:dst + size], src, ACT.Copy)
                ins = act.activation(sq_c[:, dst:dst + size], src, ACT.Square)
            elif kind in ("N2", "Q2"):
                ins = act.activation(dst, ps[:, 0:TB * size].rearrange("p (b n) -> p b n", b=TB), ACT.Copy)
            elif kind == "G":
                ins = act.activation(dst, ps[:], ACT.Tanh, scale=0.5)
            else:
                ins = act.activation(dst, ps[:], ACT.Copy)
            ins.then_inc(S["proj_taken"], 1)

        for n in range(len(first)):
            take_projection(n)
        act.wait_ge(S["rstd_sq"], 1)
        act.activation(rstd[:, :, 0], rstd[:, :, 1], ACT.Sqrt).then_inc(S["rstd_sq"], 1)
        for n in range(len(first), len(first) + len(second)):
            if n == len(first) + 12:
                act.wait_ge(S["sums_ready"], 1)
            take_projection(n)
        for i in range(2):
            act.wait_ge(S["mixed_ready"], i + 1)
            for j in range(2):
                ins = act.activation(ybT[:, 2 * i + j], bank[6 + i][:, j * T:(j + 1) * T], ACT.Copy,
                                     scale=pscale[:, 2 * i + j:2 * i + j + 1])
            ins.then_inc(S["mixed_taken"], 1)
        for i in range(5):
            act.wait_ge(S["qt_ready"], i + 1)
            src = bank[2 + i % 2][0:QK, :].rearrange("p (j t) -> p j t", j=2)
            if i < 4:
                ins = act.activation(qcT[:, 2 * i:2 * i + 2], src, ACT.Copy)
            else:
                ins = act.activation(kcT[NOPE:QK], src[NOPE:QK, 0:1].to_broadcast([ROPE, HEADS_C, T]), ACT.Copy)
            ins.then_inc(S["qt_taken"], 1)

        gate_n = len(first) + len(second)
        for u in range(len(UNITS) + 2):
            if u < len(UNITS):
                pair, qb = UNITS[u]
                act.wait_ge(S["max_ready"], u + 1)
                if u >= 2:
                    act.wait_ge(S["pt_ready"], u - 1)
                for h in range(2):
                    ins = act.activation(p_sb[:, u % 2, h, 0:P * (qb + 1)], s_sb[:, u % 2, h, 0:P * (qb + 1)],
                                         ACT.Exp, bias=neg_max[:, qb, 2 * pair + h:2 * pair + h + 1],
                                         accum_out=den[:, qb, 2 * pair + h:2 * pair + h + 1])
                ins.then_inc(S["p_ready"], 1)
            if 1 <= u and u + 1 < 2 * KD:
                load_ada(2 * KD + u + 1)
            for n in gates_at(u):
                take_projection(gate_n + n)
            if u >= 2:
                pair, qb = UNITS[u - 2]
                act.wait_ge(S["o_ready"], u - 1)
                act.activation(heads_o[:, qb, 2 * pair:2 * pair + 2],
                               bank[7][:, 0:2 * DH].rearrange("p (h e) -> p h e", h=2),
                               ACT.Copy).then_inc(S["o_taken"], 1)
        for qb in range(TB):
            act.wait_ge(S["coef_in"], qb + 1)
            act.activation(fac[:, 2 * qb], fac[:, 2 * qb], ACT.Exp).then_inc(S["coef_out"], 1)
        for i in range(3):
            act.wait_ge(S["yt_ready"], i + 1)
            act.activation(yT[:, 2 * i:2 * i + 2], bank[2 + i][:].rearrange("p (j t) -> p j t", j=2),
                           ACT.Copy).then_inc(S["yt_taken"], 1)
        for i in range(4):
            act.wait_ge(S["mixt_ready"], i + 1)
            act.activation(mixT[:, 2 * i:2 * i + 2], bank[6 + i % 2][:].rearrange("p (j t) -> p j t", j=2),
                           ACT.Copy, scale=0.5).then_inc(S["mixt_taken"], 1)

    @block.vector
    def _(dve):
        own = Count(dve, S["dve_own"])

        def ada_step(n):
            k, half = (n // 2) % KD, n % 2
            dve.wait_ge(ada_loaded[n % ADA_SLOTS], 16 * (n // ADA_SLOTS + 1))
            acc = ada_acc[:, 1536 * half:1536 * (half + 1)]
            if k == 0:
                ins = dve.tensor_scalar(acc, ada_ring[:, n % ADA_SLOTS], silu_c[:, 0:1], None, ALU.mult)
            else:
                dve.wait_ge(S["ada_used"], n - 1)
                ins = dve.scalar_tensor_tensor(acc, ada_ring[:, n % ADA_SLOTS], silu_c[:, k:k + 1], acc,
                                               ALU.mult, ALU.add)
            ins.then_inc(S["ada_used"], 1)

        def take_sums(which, gate):
            dve.wait_ge(S["ada_summed"], which + 1)
            dve.wait_ge(S["consts_in"], 16 * N_SMALL)
            own.inc(dve.tensor_tensor(mod_b[:, which], bank[0][:, 0:KD], shift_col[which], ALU.add))
            own.step(dve.tensor_tensor(mod_a[:, which], bank[0][:, KD:2 * KD], scale_col[which], ALU.add))
            dve.scalar_tensor_tensor(mod_a[:, which], mod_a[:, which], 1.0, g_col[which], ALU.add,
                                     ALU.mult).then_inc(S["mod_ready"], 1)
            for half in range(2):
                ins = dve.tensor_copy(gate[:, 512 * half:512 * (half + 1)], bank[6 + half][:])
            ins.then_inc(S["ada_bcast"], 1)

        for n in range(4):
            ada_step(n)
        g["norm_dve"](dve, own)
        for blk in range(TB):
            dve.tensor_scalar(xn[:, blk], x[:, blk], small[:, 4 + blk:5 + blk], None,
                              ALU.mult).then_inc(S["norm_ready"], 1)
        for n in range(4, 2 * KD):
            ada_step(n)
        take_sums(0, gate_mix)

        own.inc(dve.memset(cs[:, :, 0:16], 0.0))
        for grp in range(4):
            dve.wait_ge(S["proj_taken"], grp // 2 + 1)
            own.inc(dve.tensor_tensor_scan(cs[:, grp, 16:], ones[:], uT[:, grp], 0.0, ALU.mult, ALU.add))
        own.wait()
        for grp, w in enumerate(WINDOWS):
            own.inc(dve.tensor_tensor(pooled[:, grp], cs[:, grp, 16:], cs[:, grp, 16 - w:16 - w + T], ALU.subtract))
        own.wait()
        for grp, w in enumerate(WINDOWS):
            own.inc(dve.tensor_tensor(pooled[:, grp, 0:16], pooled[:, grp, 0:16], rcount[:, grp], ALU.mult))
        own.wait()
        for grp, w in enumerate(WINDOWS):
            own.inc(dve.tensor_tensor(pooled[:, grp, 0:16], pooled[:, grp, 0:16], uT[:, grp, 0:16], ALU.subtract))
            own.inc(dve.scalar_tensor_tensor(pooled[:, grp, 16:], pooled[:, grp, 16:], 1.0 / w, uT[:, grp, 16:],
                                             ALU.mult, ALU.subtract))
        own.wait()
        dve.nop().then_inc(S["pooled_ready"], 1)

        dve.wait_ge(S["sums_ready"], 1)
        for i, n in enumerate((Q_LORA, KV_LORA)):
            own.inc(dve.tensor_scalar(cs[:, i, 0:T], bank[2][:, i * T:(i + 1) * T], 1.0 / n, EPS, ALU.mult, ALU.add))
        own.wait()
        ms = cs[:, 0:2, 0:T]
        dve.reciprocal(rstd[:, :, 1], ms).then_inc(S["rstd_sq"], 1)
        dve.wait_ge(S["rstd_sq"], 2)
        own.step(dve.tensor_tensor(rstd[:, :, 1], rstd[:, :, 0], rstd[:, :, 0], ALU.mult))
        own.step(dve.tensor_tensor(rstd[:, :, 1], rstd[:, :, 1], ms, ALU.mult))
        own.step(dve.tensor_scalar(rstd[:, :, 1], rstd[:, :, 1], -0.5, 1.5, ALU.mult, ALU.add))
        own.step(dve.tensor_tensor(rstd[:, :, 0], rstd[:, :, 0], rstd[:, :, 1], ALU.mult))
        for j in range(5):
            ins = dve.scalar_tensor_tensor(latent[:, j], raw_c[:, j], lat_g[:, j:j + 1],
                                           rstd[:, 0 if j < JQ else 1, 0], ALU.mult, ALU.mult)
        ins.then_inc(S["latent_ready"], 1)

        own.inc(dve.memset(q_y[:, :, HEADS_C * QK:HEADS_C * QK + NOPE], 0.0))
        dve.wait_ge(S["proj_taken"], len(first) + 12)
        for blk in range(TB):
            heads = q_y[:, blk].rearrange("p (h e) -> p h e", e=QK)
            x1, x2 = heads[:, :, NOPE:NOPE + ROPE // 2], heads[:, :, NOPE + ROPE // 2:QK]
            cos, sin = (cos_sin[:, blk, i:i + 1].to_broadcast([P, HEADS_C + 1, ROPE // 2]) for i in range(2))
            own.inc(dve.tensor_tensor(rope_t[:, 0], x1, cos, ALU.mult))
            own.inc(dve.tensor_tensor(rope_t[:, 1], x2, sin, ALU.mult))
            own.inc(dve.tensor_tensor(rope_t[:, 2], x2, cos, ALU.mult))
            own.step(dve.tensor_tensor(rope_t[:, 3], x1, sin, ALU.mult))
            own.inc(dve.tensor_tensor(x1, rope_t[:, 0], rope_t[:, 1], ALU.subtract))
            own.step(dve.tensor_tensor(x2, rope_t[:, 2], rope_t[:, 3], ALU.add))
        dve.nop().then_inc(S["rope_ready"], 1)

        for u in range(len(UNITS) + 1):
            if u < len(UNITS):
                pair, qb = UNITS[u]
                nk = P * (qb + 1)
                dve.wait_ge(S["s_ready"], u + 1)
                if u >= 2:
                    dve.wait_ge(S["p_ready"], u - 1)
                ps = [bank[2 + 2 * (u % 2) + h][:, 0:nk] for h in range(2)]
                grp = pair // 2 if pair < 6 else 0
                for h in range(2):
                    if pair < 6:
                        dve.scalar_tensor_tensor(s_sb[:, u % 2, h, 0:nk], ps[h], scales(pair),
                                                 mask[:, grp, qb, 0:nk], ALU.mult, ALU.add
                                                 ).then_inc(S["s_taken"], 1)
                    else:
                        if qb:
                            dve.tensor_scalar(s_sb[:, u % 2, h, 0:P], ps[h][:, 0:P], scales(pair), None, ALU.mult)
                        dve.scalar_tensor_tensor(s_sb[:, u % 2, h, nk - P:nk], ps[h][:, nk - P:nk], scales(pair),
                                                 mask[:, 0, 0, 0:P], ALU.mult, ALU.add).then_inc(S["s_taken"], 1)
                dve.wait_ge(S["s_taken"], 2 * u + 2)
                own.step(dve.tensor_reduce(neg_max[:, qb, 2 * pair:2 * pair + 2], s_sb[:, u % 2, :, 0:nk], AX_X, ALU.max))
                dve.tensor_scalar(neg_max[:, qb, 2 * pair:2 * pair + 2], neg_max[:, qb, 2 * pair:2 * pair + 2], -1.0,
                                  None, ALU.mult).then_inc(S["max_ready"], 1)
            if u >= 1:
                pair, qb = UNITS[u - 1]
                nk = P * (qb + 1)
                dve.wait_ge(S["pt_ready"], u)
                if u >= 3:
                    dve.wait_ge(S["o_ready"], u - 2)
                dve.tensor_copy(pt_sb[:, (u - 1) % 2, :, 0:nk],
                                bank[6][:].rearrange("p (h k) -> p h k", h=2)[:, :, 0:nk]
                                ).then_inc(S["pt_taken"], 1)
            if u < 2 * KD:
                ada_step(2 * KD + u)
        dve.wait_ge(S["o_taken"], len(UNITS))
        for qb in range(TB):
            nm = neg_max[:, qb, 0:HEADS_A].rearrange("p (g h) -> p g h", g=3)
            f = fac[:, 2 * qb].rearrange("p (g h) -> p g h", g=3)
            w = fac[:, 2 * qb + 1].rearrange("p (g h) -> p g h", g=3)
            own.step(dve.tensor_tensor(w[:, 0], nm[:, 0], nm[:, 1], ALU.min))
            own.step(dve.tensor_tensor(w[:, 0], w[:, 0], nm[:, 2], ALU.min))
            for grp in range(3):
                own.inc(dve.tensor_tensor(f[:, grp], w[:, 0], nm[:, grp], ALU.subtract))
            own.wait()
            dve.nop().then_inc(S["coef_in"], 1)
        for qb in range(TB):
            f = fac[:, 2 * qb].rearrange("p (g h) -> p g h", g=3)
            w = fac[:, 2 * qb + 1].rearrange("p (g h) -> p g h", g=3)
            dve.wait_ge(S["coef_out"], qb + 1)
            own.step(dve.tensor_tensor(w, f, den[:, qb, 0:HEADS_A].rearrange("p (g h) -> p g h", g=3), ALU.mult))
            own.step(dve.tensor_tensor(w[:, 0], w[:, 0], w[:, 1], ALU.add))
            own.step(dve.tensor_tensor(w[:, 0], w[:, 0], w[:, 2], ALU.add))
            own.inc(dve.reciprocal(w[:, 1], w[:, 0]))
            own.step(dve.reciprocal(den[:, qb, HEADS_A:], den[:, qb, HEADS_A:]))
            for grp in range(3):
                own.inc(dve.tensor_tensor(f[:, grp], f[:, grp], w[:, 1], ALU.mult))
            own.wait()
            own.inc(dve.tensor_tensor(heads_o[:, qb, 0:HEADS_A], heads_o[:, qb, 0:HEADS_A],
                                      fac[:, 2 * qb, :, None].to_broadcast([P, HEADS_A, DH]), ALU.mult))
            yc = y_nat[:, qb, 4 * DH:].rearrange("p (h e) -> p h e", e=DH)
            own.inc(dve.tensor_tensor(yc, heads_o[:, qb, HEADS_A:], den[:, qb, HEADS_A:, None].to_broadcast(
                [P, HEADS_C, DH]), ALU.mult))
            own.wait()
            ya = y_nat[:, qb, 0:4 * DH].rearrange("p (h e) -> p h e", e=DH)
            own.step(dve.tensor_tensor(ya, heads_o[:, qb, 0:4], heads_o[:, qb, 4:8], ALU.add))
            dve.tensor_tensor(ya, ya, heads_o[:, qb, 8:12], ALU.add).then_inc(S["y_ready"], 1)
        take_sums(1, gate_ffn)

        for n in range(2 * TB):
            half, blk = n // TB, n % TB
            dve.wait_ge(S["branch_ready"], n + 1)
            for br in range(3):
                own.inc(dve.scalar_tensor_tensor(
                    scaled[:, br], tanh_g[:, blk, D * br + 512 * half:D * br + 512 * (half + 1)], 1.0,
                    bank[3 * (n % 2) + br][:], ALU.add, ALU.mult))
            own.wait()
            dve.nop().then_inc(S["branch_taken"], 1)
            own.step(dve.tensor_tensor(scaled[:, 0], scaled[:, 0], scaled[:, 1], ALU.add))
            dst = mix[:, blk, 512 * half:512 * (half + 1)]
            own.step(dve.tensor_tensor(dst, scaled[:, 0], scaled[:, 2], ALU.add))
        dve.nop().then_inc(S["mix_ready"], 1)

        for n in range(2 * TB):
            half, blk = n // TB, n % TB
            dve.wait_ge(S["res_ready"], n + 1)
            cut = slice(512 * half, 512 * (half + 1))
            own.step(dve.tensor_tensor(scaled[:, 0], gate_mix[:, cut], bank[n][:], ALU.mult))
            own.step(dve.tensor_tensor(x[:, blk, cut], x[:, blk, cut], scaled[:, 0], ALU.add))

    @block.tensor
    def _(pe):
        def sum_ada(which):
            pe.wait_ge(S["ada_used"], 2 * KD * (which + 1))
            for part in range(2):
                for k in range(KD):
                    pe.matmul(bank[0][:, part * KD + k:part * KD + k + 1],
                              ada_acc[:, part * D + k:(part + 1) * D:KD], ones[:, 0:1], start=True, stop=True)
            pe.wait_ge(S["consts_in"], 16 * N_SMALL)
            for half in range(2):
                cut = slice(512 * half, 512 * (half + 1))
                pe.matmul(bank[6 + half][:], ones[:, 0:P], ada_acc[:, 2 * D + 512 * half:2 * D + 512 * (half + 1)],
                          start=True, stop=False)
                mm = pe.matmul(bank[6 + half][:], ones[0:1, 0:P], gates_row[which][0:1, cut], start=False, stop=True)
            mm.then_inc(S["ada_summed"], 1)

        pe.wait_ge(S["norm_ready"], TB)
        g["turn_pe"](pe, xn, bank[2:6])
        sum_ada(0)
        pe.wait_ge(S["hT_ready"], 1)

        def project(n):
            kind, load, col, size, dst = projections[n]
            ps = bank[n % 2]
            pe.wait_ge(w_loaded[load % W_SLOTS], W_LANDED[load])
            if n >= 2:
                pe.wait_ge(S["proj_taken"], n - 1)
            if kind in ("T", "C"):
                w = w_view(load, KD, W_LOADS[load][2])
                for j in range(size):
                    for k in range(KD):
                        mm = pe.matmul(ps[:, j * T:(j + 1) * T], w[:, k, col + P * j:col + P * (j + 1)], hT[:, k],
                                       start=(k == 0), stop=(k == KD - 1))
            elif kind in ("N", "G"):
                w = w_view(load, KD, W_LOADS[load][2])
                blk, width = size
                for k in range(KD):
                    mm = pe.matmul(ps[:, 0:width], hT[:, k, blk * P:(blk + 1) * P], w[:, k, col:col + width],
                                   start=(k == 0), stop=(k == KD - 1))
            elif kind == "N2":
                w = w_view(load, KD, W_LOADS[load][2])
                for blk in range(TB):
                    for k in range(KD):
                        mm = pe.matmul(ps[:, blk * size:(blk + 1) * size], hT[:, k, blk * P:(blk + 1) * P],
                                       w[:, k, col:col + size], start=(k == 0), stop=(k == KD - 1))
            elif kind in ("Q", "Q2"):
                w = w_view(load, JQ, HEADS_C * QK)
                for blk, width, at in ([(size[0], size[1], 0)] if kind == "Q"
                                       else [(b, size, b * size) for b in range(TB)]):
                    for j in range(JQ):
                        mm = pe.matmul(ps[:, at:at + width], latent[:, j, blk * P:(blk + 1) * P],
                                       w[:, j, col:col + width], start=(j == 0), stop=(j == JQ - 1))
            elif kind == "K":
                w = w_view(load, JKV, HEADS_C * P)
                for h in range(size):
                    for j in range(JKV):
                        mm = pe.matmul(ps[0:NOPE, h * T:(h + 1) * T],
                                       w[:, j, (col + h) * P:(col + h) * P + NOPE], latent[:, JQ + j],
                                       start=(j == 0), stop=(j == JKV - 1))
            else:
                w = w_view(load, JKV, HEADS_C * P).rearrange("p j (h e) -> p j h e", e=P)
                for j in range(JKV):
                    mm = pe.matmul(ps[:], latent[:, JQ + j, size * P:(size + 1) * P], w[:, j, :, NOPE:P],
                                   start=(j == 0), stop=(j == JKV - 1))
            mm.then_inc(S["proj_ready"], 1)
            if last_of_load[load] == n:
                pe.wait_ge(S["proj_ready"], n + 1)
                pe.sem_inc(S["w_used"], 1)

        for n in range(len(first)):
            project(n)
        pe.wait_ge(S["proj_taken"], 5)
        for i, tiles in enumerate((range(JQ), range(JQ, 5))):
            for j in tiles:
                mm = pe.matmul(bank[2][:, i * T:(i + 1) * T], ones[:, 0:P], sq_c[:, j],
                               start=(j == tiles[0]), stop=(j == tiles[-1]))
        mm.then_inc(S["sums_ready"], 1)
        for n in range(len(first), len(first) + len(second)):
            if projections[n][0] == "Q":
                pe.wait_ge(S["latent_ready"], 1)
            project(n)
        pe.wait_ge(S["pooled_ready"], 1)
        pe.wait_ge(S["ada_bcast"], 1)
        for i in range(2):
            for j in range(2):
                mm = pe.matmul(bank[6 + i][:, j * T:(j + 1) * T], pool_w[:, 2 * i + j], pooled[:, 2 * i + j],
                               start=True, stop=True)
            mm.then_inc(S["mixed_ready"], 1)
        pe.wait_ge(S["rope_ready"], 1)
        for i in range(5):
            if i >= 2:
                pe.wait_ge(S["qt_taken"], i - 1)
            for j in range(2 if i < 4 else 1):
                for blk in range(TB):
                    slot = 2 * i + j
                    mm = pe.transpose(bank[2 + i % 2][0:QK, j * T + blk * P:j * T + (blk + 1) * P],
                                      q_y[:, blk, slot * QK:(slot + 1) * QK], ident[:])
            mm.then_inc(S["qt_ready"], 1)
        pe.wait_ge(S["qt_taken"], 5)
        pe.wait_ge(S["mixed_taken"], 2)
        gate_n = len(first) + len(second)
        pe.wait_ge(S["proj_taken"], gate_n)
        for u in range(len(UNITS) + 2):
            if u < len(UNITS):
                pair, qb = UNITS[u]
                nk = P * (qb + 1)
                if u >= 2:
                    pe.wait_ge(S["s_taken"], 2 * (u - 1))
                for h in range(2):
                    if pair < 6:
                        q = qkT[DH * h:DH * (h + 1), pair, qb * P:(qb + 1) * P]
                        k = qkT[DH * h:DH * (h + 1), 6 + pair, 0:nk]
                    else:
                        head = 2 * (pair - 6) + h
                        q, k = qcT[:, head, qb * P:(qb + 1) * P], kcT[:, head, 0:nk]
                    mm = pe.matmul(bank[2 + 2 * (u % 2) + h][:, 0:nk], q, k, start=True, stop=True)
                mm.then_inc(S["s_ready"], 1)
            for n in gates_at(u):
                project(gate_n + n)
            if 1 <= u <= len(UNITS):
                pair, qb = UNITS[u - 1]
                pe.wait_ge(S["p_ready"], u)
                if u >= 2:
                    pe.wait_ge(S["pt_taken"], u - 1)
                for h in range(2):
                    for kb in range(qb + 1):
                        cut = slice(h * T + kb * P, h * T + (kb + 1) * P)
                        mm = pe.transpose(bank[6][:, cut], p_sb[:, (u - 1) % 2, h, kb * P:(kb + 1) * P],
                                          ident[:])
                mm.then_inc(S["pt_ready"], 1)
            if u >= 2:
                pair, qb = UNITS[u - 2]
                pe.wait_ge(S["pt_taken"], u - 1)
                if u >= 3:
                    pe.wait_ge(S["o_taken"], u - 2)
                for h in range(2):
                    head = 2 * pair + h
                    for kb in range(qb + 1):
                        v = (va[:, kb, DH * head:DH * (head + 1)] if pair < 6
                             else vc[:, kb, DH * (head - HEADS_A):DH * (head - HEADS_A + 1)])
                        mm = pe.matmul(bank[7][:, h * DH:(h + 1) * DH], pt_sb[:, u % 2, h, kb * P:(kb + 1) * P],
                                       v, start=(kb == 0), stop=(kb == qb))
                mm.then_inc(S["o_ready"], 1)

        pe.wait_ge(S["y_ready"], TB)
        for i in range(3):
            for j in range(2):
                for blk in range(TB):
                    mm = pe.transpose(bank[2 + i][:, j * T + blk * P:j * T + (blk + 1) * P],
                                      y_nat[:, blk, (2 * i + j) * P:(2 * i + j + 1) * P], ident[:])
            mm.then_inc(S["yt_ready"], 1)
        pe.wait_ge(S["proj_taken"], len(projections))
        sum_ada(1)
        pe.wait_ge(S["yt_taken"], 3)
        pe.wait_ge(S["ada_bcast"], 2)
        for n in range(2 * TB):
            half, blk = n // TB, n % TB
            if n >= 2:
                pe.wait_ge(S["branch_taken"], n - 1)
            load = W_AT["w_o", 512 * half]
            pe.wait_ge(w_loaded[load % W_SLOTS], W_LANDED[load])
            w = w_view(load, 10, 512)
            for br, (src, at) in enumerate(((yT, 0), (ybT, 0), (yT, 2))):
                _, row, rows = W_BRANCH_ROWS[br]
                for j in range(rows):
                    mm = pe.matmul(bank[3 * (n % 2) + br][:], src[:, at + j, blk * P:(blk + 1) * P],
                                   w[:, row + j], start=(j == 0), stop=(j == rows - 1))
            mm.then_inc(S["branch_ready"], 1)
            if blk == TB - 1:
                pe.wait_ge(S["branch_ready"], n + 1)
                pe.sem_inc(S["w_used"], 1)
        pe.wait_ge(S["mix_ready"], 1)
        for i in range(4):
            if i >= 2:
                pe.wait_ge(S["mixt_taken"], i - 1)
            for j in range(2):
                for blk in range(TB):
                    mm = pe.transpose(bank[6 + i % 2][:, j * T + blk * P:j * T + (blk + 1) * P],
                                      mix[:, blk, 2 * i + j::KD], ident[:])
            mm.then_inc(S["mixt_ready"], 1)
        pe.wait_ge(S["mixt_taken"], 4)
        for n in range(2 * TB):
            half, blk = n // TB, n % TB
            load = W_AT["w_out", 512 * half]
            pe.wait_ge(w_loaded[load % W_SLOTS], W_LANDED[load])
            w = w_view(load, KD, 512)
            for k in range(KD):
                mm = pe.matmul(bank[n][:], mixT[:, k, blk * P:(blk + 1) * P], w[:, k], start=(k == 0),
                               stop=(k == KD - 1))
            mm.then_inc(S["res_ready"], 1)


def experts_block(nc, t, layer, g, sb, block):
    S, bank, x, ident, ones = g["S"], g["bank"], g["x"], g["ident"], g["ones"]
    gate_ffn, small, raw_loaded = g["gate_ffn"], g["small"], g["raw_loaded"]
    scratch = g["item_scratch"]
    acc = [bank[n] for n in range(4)]
    up_bank, y_bank, gather_bank = bank[4], bank[5:7], bank[7]

    xn_hi = sb("xn_hi", [P, TB, D], F32R)
    xn_lo = sb("xn_lo", [P, TB, D], F32R)
    hT = sb("e_hT", [P, KD, T])
    raw = sb("raw", [P, RAW, 2048])
    w_hi = sb("w_hi", [P, 3, 2048], F32R)
    w_lo = sb("w_lo", [P, 3, 2048], F32R)
    stage = sb("stage", [P, 2, KD, BATCH_ITEMS * SLOTS])
    xn = stage[:, 1].rearrange("p k (a s) -> p (k a s)", a=1).rearrange("p (b d) -> p b d", b=TB)
    squares = stage[:, 0].rearrange("p k s -> p (k s)")[:, 0:D]
    xg = sb("xg", [P, 2, KD, 2 * SLOTS], F32R)
    onehot = sb("onehot", [P, TB, BATCH_ITEMS, 2 * SLOTS], F32R)
    pos_rows = sb("pos_rows", [P, 2, BATCH_ITEMS, T], BF16)
    spread = sb("spread", [P, T], F32R)
    t_half = sb("t_half", [SLOTS, 512])
    up_sum = sb("up_sum", [SLOTS, 512])
    silu_sb = sb("silu_sb", [SLOTS, FF])
    g_sb = sb("g_sb", [SLOTS, FF])
    gT = sb("gT", [P, 2, 2 * SLOTS], F32R)
    y_h = sb("y_h", [P, D], F32R)
    y_l = sb("y_l", [P, D], F32R)
    w_slot = sb("w_slot", [P, 2, BATCH_ITEMS])
    router_w = sb("router_w_sb", [P, KD, NE])
    bias_row = sb("bias_row", [P, NE])
    scores = sb("scores", [P, TB, NE])
    sel = sb("sel", [P, TB, NE])
    chosen = sb("chosen", [P, TB, NE])
    weight = sb("weight", [P, TB, NE])
    top = sb("top", [P, TB, 8, GROUP])
    grp = sb("grp", [P, TB, 8])
    versus = sb("versus", [P, 2, 8, 8])
    earlier = sb("earlier", [P, 8, 8])
    earlier_e = sb("earlier_e", [NE, NE])
    iota_i = sb("iota_i", [P, 2, SLOTS], I32)
    slot_id = sb("slot_id", [P, 2 * SLOTS])
    slot_of_row = sb("slot_of_row", [P, 1])
    e_id = sb("e_id", [NE, 1])
    part_i = sb("part_i", [P, 2], I32)
    sums = sb("sums", [P, TB, 2])
    maskT_wT = sb("maskT_wT", [NE, 2, T])
    posT = sb("posT", [NE, T])
    extra = sb("extra", [NE, 8])
    pick = sb("pick", [NE, ITEMS])
    shift = sb("shift", [NE, ITEMS])
    sel_x = sb("sel_x", [NE, 2, MAX_EXTRA])
    item_pos = sb("item_pos", [P, TB, ITEMS])
    item_w = sb("item_w", [P, TB, ITEMS, 2], F32R)
    item_rows = sb("item_rows", [ITEMS, T], BF16)
    extra_e = sb("extra_e", [1, 2 + MAX_EXTRA], I32)
    extra_n = sb("extra_n", [1, 4])
    extra_b = sb("extra_b", [1, 4], I32)
    shared_g = sb("shared_g", [P, TB, FF])
    shared_gT = sb("shared_gT", [P, 2, T])
    scaled = sb("e_scaled", [P, 512])

    shared_at = [Item(None, 1).raw_slot(c) for c in range(3)]
    scratch_rows = scratch.rearrange("(b i) t -> b (i t)", i=BATCH_ITEMS)

    def piece(c, buf):
        if c < 2:
            return buf.rearrange("p (m k f) -> p m k f", m=2, k=4)
        return buf.rearrange("p (j n) -> p j n", j=2)

    @block.sync
    def _(sp):
        def load_piece(c, slot, w1, w3, w2):
            dst = piece(c, raw[:, slot])
            if c < 2:
                for m, w in enumerate((w1, w3)):
                    sp.dma_start(dst[:, m], w.rearrange("(p k) f -> p k f", k=KD)[:, 4 * c:4 * c + 4]
                                 ).then_inc(raw_loaded[slot], 16)
            else:
                for j in range(2):
                    sp.dma_start(dst[:, j], w2[j * P:(j + 1) * P, :]).then_inc(raw_loaded[slot], 16)

        w1s, w3s, w2s = (t[f"exp_w{i}"].rearrange("l e a b -> (l e) a b") for i in (1, 3, 2))

        def load(c, i, e):
            if not i.early:
                sp.wait_ge(S[LO[c]], i.val(2, -2))
            n = layer * NE + e
            load_piece(c, i.raw_slot(c), w1s[n], w3s[n], w2s[n])

        sp.dma_start(router_w[:], t["router_w"][layer].rearrange("(p k) e -> p k e", k=KD)
                     ).then_inc(S["router_in"], 16)
        sp.dma_start(bias_row[:], t["router_bias"][layer].rearrange("(a e) -> a e", a=1).to_broadcast([P, NE])
                     ).then_inc(S["router_in"], 16)
        for c in range(3):
            load_piece(c, shared_at[c], t["sh_w1"][layer], t["sh_w3"][layer], t["sh_w2"][layer])
        for c in range(3):
            load(c, Item(None, 0, early=True), 0)
        for c in range(3):
            sp.wait_ge(S["shared_used"], c + 1)
            load(c, Item(None, 1, early=True), 1)
        for n in (2, 3):
            if n == 3:
                sp.wait_ge(S["tables_ready"], 1)
                sp.dma_start(scratch, item_rows[:]).then_inc(S["scratch_written"], 16)
                sp.wait_ge(S["scratch_written"], 16)
                sp.dma_start(pos_rows[:, 0].rearrange("p i t -> p (i t)"), scratch_rows[0:1].to_broadcast(
                    [P, BATCH_ITEMS * T])).then_inc(S["pos_in"], 16)
            for c in range(2):
                load(c, Item(None, n), n)
        with sp.Fori(1, NE // BATCH_ITEMS) as b:
            for u in range(BATCH_ITEMS):
                i = Item(b, u)
                load(2, i.next(-2), b * BATCH_ITEMS + (u - 2))
                for c in range(2):
                    load(c, i, b * BATCH_ITEMS + u)
        sp.wait_ge(S["extra_in"], 1)
        batches = sp.value_load(extra_b[0:1, 0:1], min_val=0, max_val=8)

        def expert(n):
            return sp.value_load(extra_e[0:1, bass.ds(n, 1)], min_val=0, max_val=NE - 1)

        with sp.If(batches > 0):
            with sp.Fori(0, batches) as xb:
                for u in range(BATCH_ITEMS):
                    i = Item(xb, NE + u)
                    load(2, i.next(-2), expert(xb * BATCH_ITEMS + u))
                    e = expert(xb * BATCH_ITEMS + (u + 2))
                    for c in range(2):
                        load(c, i, e)
        for u in range(2):
            load(2, Item(batches, NE + u - 2), expert(batches * BATCH_ITEMS + u))

    def has(last, u, ahead):
        return not last or u + ahead < BATCH_ITEMS

    def stage_of(par, nxt, off):
        which, v = (par, nxt)[off // BATCH_ITEMS], off % BATCH_ITEMS
        return stage[:, bass.ds(which, 1), :, v * SLOTS:(v + 1) * SLOTS].rearrange("p a k s -> p (a k) s")

    def lo_half(eng, i, c, h):
        eng.wait_ge(S[HI[c]], i.val(2, h + 1))
        cut = slice(1024 * h, 1024 * (h + 1))
        eng.tensor_tensor(w_lo[:, c, cut], raw[:, i.raw_slot(c), cut], w_hi[:, c, cut].bitcast(F32),
                          ALU.subtract).then_inc(S[LO[c]], 1)

    @block.gpsimd
    def _(pool):
        own = Count(pool, S["pool_own"])
        own.inc(pool.iota(iota_i[:], [[0, 2], [1, SLOTS]], base=0, channel_multiplier=0))
        own.inc(pool.iota(part_i[:, 0:1], [[1, 1]], base=0, channel_multiplier=1))
        own.inc(pool.memset(earlier[:], 1.0))
        own.inc(pool.memset(earlier_e[:], 1.0))
        own.wait()
        own.inc(pool.affine_select(out=earlier[:], in_=earlier[:], compare_op=ALU.is_gt, fill=0.0, base=0,
                                   pattern=[[1, 8], [-1, 8]], channel_multiplier=0))
        own.inc(pool.affine_select(out=earlier_e[:], in_=earlier_e[:], compare_op=ALU.is_gt, fill=0.0, base=0,
                                   pattern=[[1, NE]], channel_multiplier=-1))
        own.wait()

        def xg_low(i, src):
            pool.wait_ge(S["xg_hi"], i.val(1, 1))
            pool.tensor_tensor(xg[:, i.parity, :, SLOTS:], src, xg[:, i.parity, :, 0:SLOTS].bitcast(F32),
                               ALU.subtract).then_inc(S["xg_lo"], 1)

        def batch(b, last=False):
            par = pool.snap(b % 2)
            nxt = pool.snap((b + 1) % 2)
            for u in range(BATCH_ITEMS):
                i = Item(b, u)
                if has(last, u, 2):
                    lo_half(pool, i.next(2), 1, 1)
                if has(last, u, 1):
                    lo_half(pool, i.next(), 2, 1)
                if has(last, u, 3):
                    xg_low(i.next(3), stage_of(par, nxt, u + 3))

        for n in range(3):
            xg_low(Item(None, n), stage[:, 0, :, n * SLOTS:(n + 1) * SLOTS])
        pool.wait_ge(S["extra_in"], 1)
        batches = pool.value_load(extra_b[0:1, 0:1], min_val=0, max_val=8)
        with pool.Fori(0, batches + (NE // BATCH_ITEMS - 1)) as b:
            batch(b)
        batch(pool.snap(batches + (NE // BATCH_ITEMS - 1)), last=True)
    @block.scalar
    def _(act):
        own = Count(act, S["act_own"])

        def hi_half(i, c, h):
            if h == 0:
                act.wait_ge(raw_loaded[i.raw_slot(c)], i.uses_val(32))
                if c == 2 and not i.first:
                    act.wait_ge(S["down_done"], i.val(2, 1))
                elif not i.first:
                    act.wait_ge(S[("a_free", "b_free")[c]], i.val(1, 0))
            cut = slice(1024 * h, 1024 * (h + 1))
            act.activation(w_hi[:, c, cut], raw[:, i.raw_slot(c), cut], ACT.Copy).then_inc(S[HI[c]], 1)

        def take_gather(ready, pair, to):
            act.wait_ge(S["gather_ready"], ready)
            waited_apart(act, S["sig_ready"])
            for j in range(2):
                k = 2 * pair + j
                ins = act.activation(to[:, k], gather_bank[:, j * 256:(j + 1) * 256].rearrange(
                    "p (a s) -> p a s", a=1), ACT.Identity, bias=g["mod_b"][:, 1, k:k + 1],
                    scale=g["mod_a"][:, 1, k:k + 1])
            ins.then_inc(S["gather_taken"], 1)

        def xg_high(i, src, batch_done):
            waited_apart(act, S["sig_ready"])
            act.wait_ge(S["gather_taken"], batch_done)
            if not i.early:
                act.wait_ge(S["b_free"], i.val(1, -1))
            act.activation(xg[:, i.parity, :, 0:SLOTS], src, ACT.Copy).then_inc(S["xg_hi"], 1)

        def t_and_silu(i, between=None):
            act.wait_ge(S["b_free"], i.val(1, 1))
            act.activation(t_half[:], up_bank[SLOTS:P, :], ACT.Copy).then_inc(S["t_done"], 1)
            if between:
                between()
            act.wait_ge(S["added"], i.val(1, 1))
            act.activation(silu_sb[:], up_sum[:, 0:FF], ACT.Silu).then_inc(S["silu_done"], 1)

        def gt_high(i):
            act.wait_ge(S["gt_ready"], i.val(1, 1))
            if not i.first:
                act.wait_ge(S["down_done"], i.val(2, 1))
            act.activation(gT[:, :, 0:SLOTS], y_bank[0][:, 0:2 * SLOTS].rearrange("p (j s) -> p j s", j=2),
                           ACT.Copy).then_inc(S["gt_hi"], 1)

        def batch(b, last=False):
            par = act.snap(b % 2)
            nxt = act.snap((b + 1) % 2)
            if not last:
                act.wait_ge(S["pos_in"], b * 16 + 16)
                act.wait_ge(S["s_made"], b * BATCH_ITEMS + 1)
                act.dma_start(pos_rows[:, bass.ds(nxt, 1)].rearrange("p a i t -> p (a i t)"),
                              scratch_rows[bass.ds(b + 1, 1)].to_broadcast([P, BATCH_ITEMS * T])
                              ).then_inc(S["pos_in"], 16)
            for u in range(BATCH_ITEMS):
                i = Item(b, u)
                if has(last, u, 2):
                    hi_half(i.next(2), 1, 1)
                act.wait_ge(S["wslot_moved"], b + 1)
                for half in range(2):
                    act.wait_ge(S["down_done"], i.val(2, half + 2))
                    if half == 0:
                        act.wait_ge(S["scatter_done"], i.val(1, 1))
                    cut = slice(512 * half, 512 * (half + 1))
                    act.activation(y_h[:, cut], y_bank[half][:], ACT.Copy, scale=w_slot[:, 0, u:u + 1]
                                   ).then_inc(S["y_hi"], 1)
                if has(last, u, 1):
                    hi_half(i.next(), 2, 0)
                    hi_half(i.next(), 2, 1)
                    gt_high(i.next())
                if has(last, u, 3):
                    hi_half(i.next(3), 0, 0)
                if u >= 2 and not last:
                    act.wait_ge(S["xg_lo"], b * BATCH_ITEMS + BATCH_ITEMS)
                    take_gather(b * 4 + (9 + 2 * (u - 2)), 2 * (u - 2),
                                stage[:, bass.ds(par, 1)].rearrange("p a k s -> p k a s"))
                if has(last, u, 2):
                    t_and_silu(i.next(2), (lambda: hi_half(i.next(3), 0, 1)) if has(last, u, 3) else None)
                if has(last, u, 3):
                    hi_half(i.next(3), 1, 0)
                if u >= 2 and not last:
                    take_gather(b * 4 + (10 + 2 * (u - 2)), 2 * (u - 2) + 1,
                                stage[:, bass.ds(par, 1)].rearrange("p a k s -> p k a s"))
                if has(last, u, 3):
                    xg_high(i.next(3), stage_of(par, nxt, u + 3), b * 4 + (8 if u else 4))

        g["norm_act"](act, own, squares)
        act.wait_ge(S["norm_ready"], TB)
        for blk in range(TB):
            act.activation(xn_hi[:, blk], xn[:, blk], ACT.Copy).then_inc(S["norm_act"], 1)
        g["modulate_act"](act, hT, bank[4:8], 1)
        items = [Item(None, n, early=n < 2) for n in range(3)]
        for c in range(3):
            for h in range(2):
                hi_half(items[0], c, h)
        act.wait_ge(S["logits_ready"], 1)
        act.activation(scores[:], gather_bank[:, 0:TB * NE].rearrange("p (b e) -> p b e", b=TB),
                       ACT.Sigmoid).then_inc(S["sig_ready"], 1)
        for blk in range(TB):
            act.wait_ge(S["shared_up"], blk + 1)
            act.activation(shared_g[:, blk], bank[4 + blk][:, 0:FF], ACT.Silu).then_inc(S["shared_act"], 1)
        act.wait_ge(S["shared_gt"], 1)
        act.activation(shared_gT[:], bank[6][:].rearrange("p (j t) -> p j t", j=2), ACT.Copy
                       ).then_inc(S["shared_gt_taken"], 1)
        for pair in range(4):
            take_gather(pair + 1, pair, stage[:, 0:1].rearrange("p a k s -> p k a s"))
        for n in range(2):
            xg_high(items[n], stage[:, 0, :, n * SLOTS:(n + 1) * SLOTS], 4)
        hi_half(items[1], 0, 0)
        hi_half(items[1], 0, 1)
        for pair in range(2):
            take_gather(pair + 5, pair, stage[:, 1:2].rearrange("p a k s -> p k a s"))
        t_and_silu(items[0])
        hi_half(items[1], 1, 0)
        hi_half(items[1], 1, 1)
        gt_high(items[0])
        for pair in range(2, 4):
            take_gather(pair + 5, pair, stage[:, 1:2].rearrange("p a k s -> p k a s"))
        xg_high(items[2], stage[:, 0, :, 2 * SLOTS:3 * SLOTS], 4)
        hi_half(items[2], 0, 0)
        t_and_silu(items[1])
        hi_half(items[2], 0, 1)
        hi_half(items[2], 1, 0)
        act.wait_ge(S["extra_in"], 1)
        batches = act.value_load(extra_b[0:1, 0:1], min_val=0, max_val=8)
        with act.Fori(0, batches + (NE // BATCH_ITEMS - 1)) as b:
            batch(b)
        batch(act.snap(batches + (NE // BATCH_ITEMS - 1)), last=True)

    @block.vector
    def _(dve):
        own = Count(dve, S["dve_own"])

        def add_halves(i):
            dve.wait_ge(S["t_done"], i.val(1, 1))
            if not i.first:
                dve.wait_ge(S["mul_done"], i.val(1, 0))
            dve.tensor_tensor(up_sum[:], up_bank[0:SLOTS, :], t_half[:], ALU.add).then_inc(S["added"], 1)

        def multiply(i):
            dve.wait_ge(S["silu_done"], i.val(1, 1))
            if not i.first:
                dve.wait_ge(S["gt_ready"], i.val(1, 0))
            dve.tensor_tensor(g_sb[:], silu_sb[:], up_sum[:, FF:], ALU.mult).then_inc(S["mul_done"], 1)

        def gt_low(i):
            dve.wait_ge(S["gt_hi"], i.val(1, 1))
            dve.tensor_tensor(gT[:, :, SLOTS:], y_bank[0][:, 0:2 * SLOTS].rearrange("p (j s) -> p j s", j=2),
                              gT[:, :, 0:SLOTS].bitcast(F32), ALU.subtract).then_inc(S["gt_lo"], 1)

        def make_onehots(column):
            for blk in range(TB):
                for it in range(BATCH_ITEMS):
                    ins = dve.tensor_scalar(onehot[:, blk, it], slot_id[:], item_pos[:, blk, column(it)], None,
                                            ALU.is_equal)
            ins.then_inc(S["onehot_made"], 1)

        def take_wslot(b1):
            dve.wait_ge(S["wslot_ready"], b1)
            dve.tensor_reduce(w_slot[:, 1], gather_bank[:, 0:2 * BATCH_ITEMS].rearrange("p (i c) -> p i c", c=2),
                              AX_X, ALU.add).then_inc(S["wslot_made"], 1)

        def move_wslot(b1):
            dve.wait_ge(S["wslot_made"], b1)
            dve.tensor_copy(w_slot[:, 0], w_slot[:, 1]).then_inc(S["wslot_moved"], 1)

        def batch(b, last=False):
            par = dve.snap(b % 2)
            for u in range(BATCH_ITEMS):
                i = Item(b, u)
                if u == 0:
                    dve.wait_ge(S["pos_in"], b * 16 + 16)
                dve.wait_ge(S["scatter_done"], i.val(1, 1))
                dve.tensor_scalar(spread[:], pos_rows[:, bass.ds(par, 1), u].rearrange("p a t -> p (a t)"),
                                  slot_of_row[:], None, ALU.is_equal).then_inc(S["s_made"], 1)
                for half in range(2):
                    cut = slice(512 * half, 512 * (half + 1))
                    dve.wait_ge(S["y_hi"], i.val(2, half + 1))
                    dve.scalar_tensor_tensor(y_l[:, cut], y_bank[half][:], w_slot[:, 0, u:u + 1],
                                             y_h[:, cut].bitcast(F32), ALU.mult, ALU.subtract
                                             ).then_inc(S["y_lo"], 1)
                if has(last, u, 1):
                    lo_half(dve, i.next(), 2, 0)
                    gt_low(i.next())
                if u == 0 and not last:
                    take_wslot(b + 2)
                if u == BATCH_ITEMS - 1 and not last:
                    dve.wait_ge(S["y_lo"], i.val(2, 4))
                    move_wslot(b + 2)
                if has(last, u, 3):
                    lo_half(dve, i.next(3), 0, 0)
                if has(last, u, 2):
                    add_halves(i.next(2))
                if has(last, u, 3):
                    lo_half(dve, i.next(3), 0, 1)
                if has(last, u, 2):
                    multiply(i.next(2))
                if has(last, u, 3):
                    lo_half(dve, i.next(3), 1, 0)
                if u == 1 and not last:
                    dve.wait_ge(S["wslot_ready"], b + 2)
                    make_onehots(lambda it: bass.ds(b * BATCH_ITEMS + (2 * BATCH_ITEMS + it), 1))

        dve.nop().then_inc(S["s_made"], 1)
        dve.nop().then_inc(S["y_lo"], 2)
        g["norm_dve"](dve, own)
        for blk in range(TB):
            dve.tensor_scalar(xn[:, blk], x[:, blk], small[:, 4 + blk:5 + blk], None,
                              ALU.mult).then_inc(S["norm_ready"], 1)
        for blk in range(TB):
            dve.wait_ge(S["norm_act"], 3 + blk)
            dve.tensor_tensor(xn_lo[:, blk], xn[:, blk], xn_hi[:, blk].bitcast(F32), ALU.subtract
                              ).then_inc(S["norm_dve"], 1)
        dve.wait_ge(S["pool_own"], 6)
        own.inc(dve.tensor_copy(slot_id[:], iota_i[:].rearrange("p a s -> p (a s)")))
        own.inc(dve.tensor_copy(e_id[:], part_i[0:NE, 0:1]))
        own.step(dve.tensor_scalar(part_i[:, 1:2], part_i[:, 0:1], SLOTS - 1, None, ALU.bitwise_and))
        own.step(dve.tensor_copy(slot_of_row[:], part_i[:, 1:2]))
        items = [Item(None, n) for n in range(3)]
        for c in range(3):
            for h in range(2):
                lo_half(dve, items[0], c, h)

        dve.wait_ge(S["router_in"], 32)
        dve.wait_ge(S["sig_ready"], 1)
        own.step(dve.tensor_tensor(sel[:], scores[:], bias_row[:, None, :].to_broadcast([P, TB, NE]), ALU.add))
        for blk in range(TB):
            for gr in range(8):
                own.inc(dve.max(top[:, blk, gr], sel[:, blk, gr * GROUP:(gr + 1) * GROUP]))
        own.wait()
        own.step(dve.tensor_tensor(grp[:], top[:, :, :, 0], top[:, :, :, 1], ALU.add))
        for blk in range(TB):
            other = grp[:, blk, None, :].to_broadcast([P, 8, 8])
            this = grp[:, blk, :, None].to_broadcast([P, 8, 8])
            own.inc(dve.tensor_tensor(versus[:, 0], other, this, ALU.is_gt))
            own.step(dve.tensor_tensor(versus[:, 1], other, this, ALU.is_equal))
            own.step(dve.tensor_tensor(versus[:, 1], versus[:, 1], earlier[:], ALU.mult))
            own.step(dve.tensor_tensor(versus[:, 0], versus[:, 0], versus[:, 1], ALU.add))
            own.step(dve.tensor_reduce(grp[:, blk], versus[:, 0], AX_X, ALU.add))
            own.step(dve.tensor_scalar(grp[:, blk], grp[:, blk], float(TOPK_GROUPS), NEG, ALU.is_ge, ALU.mult))
            own.step(dve.tensor_tensor(sel[:, blk].rearrange("p (g e) -> p g e", g=8),
                                       sel[:, blk].rearrange("p (g e) -> p g e", g=8),
                                       grp[:, blk, :, None].to_broadcast([P, 8, GROUP]), ALU.add))
            own.step(dve.max(top[:, blk, 0], sel[:, blk]))
            own.step(dve.match_replace(chosen[:, blk], top[:, blk, 0], sel[:, blk], TAKEN))
            own.step(dve.tensor_scalar(chosen[:, blk], chosen[:, blk], 0.5 * TAKEN, None, ALU.is_le))
            own.step(dve.tensor_tensor(weight[:, blk], chosen[:, blk], scores[:, blk], ALU.mult))
            own.step(dve.tensor_reduce(sums[:, blk, 0:1], weight[:, blk], AX_X, ALU.add))
            own.step(dve.reciprocal(sums[:, blk, 1:2], sums[:, blk, 0:1]))
            own.step(dve.tensor_scalar(weight[:, blk], weight[:, blk], sums[:, blk, 1:2], ROUTED_SCALE,
                                       ALU.mult, ALU.mult))
        dve.nop().then_inc(S["sel_ready"], 1)

        dve.wait_ge(S["selt_ready"], 1)
        own.step(dve.tensor_copy(maskT_wT[:], bank[7][0:NE, :].rearrange("p (m t) -> p m t", m=2)))
        own.step(dve.tensor_tensor_scan(posT[:], ones[0:NE, :], maskT_wT[:, 0], 0.0, ALU.mult, ALU.add))
        count = posT[:, T - 1:T]
        for n in range(3):
            own.inc(dve.tensor_scalar(extra[:, n:n + 1], count, float(SLOTS * (n + 1)), None, ALU.is_gt))
        own.wait()
        own.step(dve.tensor_tensor(extra[:, 0:1], extra[:, 0:1], extra[:, 1:2], ALU.add))
        own.step(dve.tensor_tensor(extra[:, 0:1], extra[:, 0:1], extra[:, 2:3], ALU.add))
        own.step(dve.scalar_tensor_tensor(posT[:], posT[:], -1.0 - NOT_HERE, maskT_wT[:, 0], ALU.add, ALU.mult))
        own.step(dve.tensor_scalar(posT[:], posT[:], NOT_HERE - NO_ITEM, None, ALU.add))
        own.inc(dve.tensor_copy(pick[:, 0:NE], ident[0:NE, 0:NE]))
        own.step(dve.memset(shift[:, 0:NE], 0.0))
        dve.nop().then_inc(S["small_psum"], 1)
        for blk in range(TB):
            dve.wait_ge(S["shared_act"], blk + 1)
            dve.tensor_tensor(shared_g[:, blk], shared_g[:, blk], bank[4 + blk][:, FF:], ALU.mult
                              ).then_inc(S["shared_g"], 1)
        dve.wait_ge(S["small_taken"], 1)
        own.step(dve.tensor_copy(extra[:, 3:4], bank[7][0:NE, 0:1]))
        own.inc(dve.tensor_copy(extra_n[0:1, 0:1], bank[7][0:1, 1:2]))
        own.step(dve.tensor_tensor(extra[:, 4:5], extra[:, 3:4], extra[:, 0:1], ALU.add))
        ids = slot_id[0:NE, 0:MAX_EXTRA]
        own.inc(dve.tensor_scalar(sel_x[:, 0], ids, extra[:, 3:4], None, ALU.is_ge))
        own.step(dve.tensor_scalar(sel_x[:, 1], ids, extra[:, 4:5], None, ALU.is_lt))
        own.step(dve.tensor_tensor(pick[:, NE:], sel_x[:, 0], sel_x[:, 1], ALU.mult))
        own.step(dve.tensor_scalar(sel_x[:, 0], ids, extra[:, 3:4], None, ALU.subtract))
        own.step(dve.tensor_scalar(sel_x[:, 0], sel_x[:, 0], -float(SLOTS), -float(SLOTS), ALU.mult, ALU.add))
        own.step(dve.tensor_tensor(shift[:, NE:], sel_x[:, 0], pick[:, NE:], ALU.mult))
        own.step(dve.tensor_scalar(extra_n[0:1, 0:1], extra_n[0:1, 0:1], float(BATCH_ITEMS - 1), None, ALU.add))
        own.step(dve.tensor_copy(extra_b[0:1, 1:2], extra_n[0:1, 0:1]))
        own.step(dve.tensor_scalar(extra_b[0:1, 0:1], extra_b[0:1, 1:2], 2, None, ALU.arith_shift_right))
        dve.nop().then_inc(S["small_psum"], 1)
        dve.wait_ge(S["table_psum"], 1)
        own.inc(dve.tensor_copy(extra_e[:, 2:], bank[7][0:1, 0:MAX_EXTRA]))
        for n in range(2):
            own.inc(dve.memset(extra_e[:, n:n + 1], NE - 2 + n))
        own.wait()
        dve.nop().then_inc(S["extra_in"], 1)
        pos = up_bank[:, 0:TB * P].rearrange("p (b i) -> p b i", b=TB)[:, :, 0:ITEMS]
        wts = up_bank[:, TB * P:2 * TB * P].rearrange("p (b i) -> p b i", b=TB)[:, :, 0:ITEMS]
        own.inc(dve.tensor_scalar(item_pos[:], pos, NO_ITEM, None, ALU.add))
        own.step(dve.tensor_copy(item_w[:, :, :, 0], wts))
        own.inc(dve.tensor_tensor(item_w[:, :, :, 1], wts, item_w[:, :, :, 0].bitcast(F32), ALU.subtract))
        own.step(dve.tensor_scalar(item_rows[:], y_bank[0][0:ITEMS, 0:T], NO_ITEM, 256.0, ALU.add, ALU.min))
        dve.nop().then_inc(S["tables_ready"], 1)

        make_onehots(lambda it: slice(it, it + 1))
        take_wslot(1)
        move_wslot(1)
        make_onehots(lambda it: slice(BATCH_ITEMS + it, BATCH_ITEMS + it + 1))
        for h in range(2):
            lo_half(dve, items[1], 0, h)
        add_halves(items[0])
        multiply(items[0])
        for h in range(2):
            lo_half(dve, items[1], 1, h)
        gt_low(items[0])
        lo_half(dve, items[2], 0, 0)
        add_halves(items[1])
        lo_half(dve, items[2], 0, 1)
        multiply(items[1])
        lo_half(dve, items[2], 1, 0)
        dve.wait_ge(own.sem, own.n)
        batches = dve.value_load(extra_b[0:1, 0:1], min_val=0, max_val=8)
        with dve.Fori(0, batches + (NE // BATCH_ITEMS - 1)) as b:
            batch(b)
        batch(dve.snap(batches + (NE // BATCH_ITEMS - 1)), last=True)
        dve.wait_ge(S["pos_in"], batches * 16 + NE // BATCH_ITEMS * 16)
        dve.wait_ge(S["acc_ready"], 1)
        for blk in range(TB):
            for half in range(2):
                cut = slice(512 * half, 512 * (half + 1))
                own.step(dve.tensor_tensor(scaled[:], gate_ffn[:, cut], acc[2 * blk + half][:], ALU.mult))
                own.step(dve.tensor_tensor(x[:, blk, cut], x[:, blk, cut], scaled[:], ALU.add))

    @block.tensor
    def _(pe):
        def up(i, c):
            pe.wait_ge(S[LO[c]], i.val(2, 2))
            if c == 0:
                pe.wait_ge(S["xg_lo"], i.val(1, 1))
                if not i.first:
                    pe.wait_ge(S["added"], i.val(1, 0))
            for kk in range(4):
                k = 4 * c + kk
                if c == 0 and kk == 3 and i.b is not None:
                    pe.wait_ge(S["y_lo"], i.val(2, -1))
                for w in (w_hi, w_lo):
                    mm = pe.matmul(up_bank[:], xg[:, i.parity, k], piece(c, w[:, c])[:, :, kk],
                                   start=(k == 0 and w is w_hi), stop=(k == KD - 1 and w is w_lo))
            mm.then_inc(S["a_free" if c == 0 else "b_free"], 1)

        def down(i):
            pe.wait_ge(S["gt_lo"], i.val(1, 1))
            pe.wait_ge(S["lo_c"], i.val(2, 2))
            for half in range(2):
                for j in range(2):
                    for w in (w_hi, w_lo):
                        mm = pe.matmul(y_bank[half][:], gT[:, j], piece(2, w[:, 2])[:, j, 512 * half:512 * half + 512],
                                       start=(j == 0 and w is w_hi), stop=(j == 1 and w is w_lo))
                mm.then_inc(S["down_done"], 1)

        def scatter(i):
            pe.wait_ge(S["s_made"], i.val(1, 2))
            pe.wait_ge(S["y_lo"], i.val(2, 4))
            for blk in range(TB):
                for half in range(2):
                    for y in (y_h, y_l):
                        mm = pe.matmul(acc[2 * blk + half][:], spread[:, blk * P:(blk + 1) * P],
                                       y[:, 512 * half:512 * half + 512], start=False, stop=False,
                                       skip_group_check=True)
            mm.then_inc(S["scatter_done"], 1)

        def turn_g(i):
            waited_apart(pe, S["logits_ready"])
            pe.wait_ge(S["mul_done"], i.val(1, 1))
            for j in range(2):
                mm = pe.transpose(y_bank[0][:, j * SLOTS:(j + 1) * SLOTS], g_sb[:, j * P:(j + 1) * P],
                                  ident[0:SLOTS, 0:SLOTS])
            mm.then_inc(S["gt_ready"], 1)

        def gather(pair):
            for j in range(2):
                k = 2 * pair + j
                for blk in range(TB):
                    for xs in (xn_hi, xn_lo):
                        mm = pe.matmul(gather_bank[:, 256 * j:256 * (j + 1)], xs[:, blk, k::KD],
                                       onehot[:, blk, :, 0:SLOTS],
                                       start=(blk == 0 and xs is xn_hi), stop=(blk == TB - 1 and xs is xn_lo))
            mm.then_inc(S["gather_ready"], 1)

        def slot_weights(taken, column):
            pe.wait_ge(S["gather_taken"], taken)
            for it in range(BATCH_ITEMS):
                for blk in range(TB):
                    mm = pe.matmul(gather_bank[:, 2 * it:2 * it + 2],
                                   onehot[:, blk, it], item_w[:, blk, column(it)],
                                   start=(blk == 0), stop=(blk == TB - 1))
            mm.then_inc(S["wslot_ready"], 1)

        def batch(b, last=False):
            for u in range(BATCH_ITEMS):
                i = Item(b, u)
                down(i)
                if has(last, u, 2):
                    up(i.next(2), 0)
                    turn_g(i.next())
                if u == 0 and not last:
                    slot_weights(b * 4 + 8, lambda it: pe.snap(b * 4 + (4 + it)))
                if u >= 2 and not last:
                    if u == 2:
                        pe.wait_ge(S["onehot_made"], b + 3)
                        pe.wait_ge(S["wslot_made"], b + 2)
                    pe.wait_ge(S["gather_taken"], b * 4 + (8 + 2 * (u - 2)))
                    gather(2 * (u - 2))
                if has(last, u, 2):
                    up(i.next(2), 1)
                scatter(i)
                if has(last, u, 1) and not has(last, u, 2):
                    turn_g(i.next())
                if u >= 2 and not last:
                    pe.wait_ge(S["gather_taken"], b * 4 + (9 + 2 * (u - 2)))
                    gather(2 * (u - 2) + 1)

        pe.nop().then_inc(S["down_done"], 1)
        pe.nop().then_inc(S["scatter_done"], 1)
        pe.wait_ge(S["norm_ready"], TB)
        g["turn_pe"](pe, xn, bank[4:8])
        pe.wait_ge(S["hT_ready"], 1)
        pe.wait_ge(S["router_in"], 32)
        for blk in range(TB):
            for k in range(KD):
                mm = pe.matmul(bank[7][:, blk * NE:(blk + 1) * NE], hT[:, k, blk * P:(blk + 1) * P], router_w[:, k],
                               start=(k == 0), stop=(k == KD - 1))
        mm.then_inc(S["logits_ready"], 1)
        for blk in range(TB):
            for c in range(2):
                pe.wait_ge(raw_loaded[shared_at[c]], 32)
                for kk in range(4):
                    k = 4 * c + kk
                    mm = pe.matmul(bank[4 + blk][:], hT[:, k, blk * P:(blk + 1) * P], piece(c, raw[:, shared_at[c]])[:, :, kk],
                                   start=(k == 0), stop=(k == KD - 1))
            mm.then_inc(S["shared_up"], 1)
        pe.wait_ge(S["shared_up"], 2)
        pe.sem_inc(S["shared_used"], 2)
        pe.wait_ge(S["sel_ready"], 1)
        for m, src in enumerate((chosen, weight)):
            for blk in range(TB):
                mm = pe.transpose(bank[7][0:NE, m * T + blk * P:m * T + (blk + 1) * P], src[:, blk], ident[:])
        mm.then_inc(S["selt_ready"], 1)
        for blk in range(TB):
            pe.wait_ge(S["shared_g"], blk + 1)
            for j in range(2):
                mm = pe.transpose(bank[6][:, j * T + blk * P:j * T + (blk + 1) * P], shared_g[:, blk, j * P:(j + 1) * P],
                                  ident[:])
        mm.then_inc(S["shared_gt"], 1)
        pe.wait_ge(S["small_psum"], 1)
        pe.matmul(bank[7][0:NE, 0:1], earlier_e[:], extra[:, 0:1], start=True, stop=True)
        pe.matmul(bank[7][:, 1:2], ones[0:NE, 0:P], extra[:, 0:1], start=True, stop=True).then_inc(S["small_taken"], 1)
        pe.wait_ge(S["shared_gt_taken"], 1)
        pe.wait_ge(raw_loaded[shared_at[2]], 32)
        for blk in range(TB):
            for half in range(2):
                for j in range(2):
                    mm = pe.matmul(acc[2 * blk + half][:], shared_gT[:, j, blk * P:(blk + 1) * P],
                                   piece(2, raw[:, shared_at[2]])[:, j, 512 * half:512 * half + 512], start=(j == 0), stop=False,
                                   skip_group_check=True)
        mm.then_inc(S["shared_used"], 1)
        pe.wait_ge(S["small_psum"], 2)
        for blk in range(TB):
            cut = slice(blk * P, blk * P + ITEMS)
            pe.matmul(up_bank[:, cut], posT[:, blk * P:(blk + 1) * P], pick[:], start=True, stop=False)
            pe.matmul(up_bank[:, cut], ones[0:NE, 0:P], shift[:], start=False, stop=True)
        for blk in range(TB):
            cut = slice((TB + blk) * P, (TB + blk) * P + ITEMS)
            pe.matmul(up_bank[:, cut], maskT_wT[:, 1, blk * P:(blk + 1) * P], pick[:], start=True, stop=True)
        pe.matmul(y_bank[0][0:ITEMS, 0:T], pick[:], posT[:], start=True, stop=False)
        pe.matmul(y_bank[0][0:ITEMS, 0:T], shift[:], ones[0:NE, :], start=False, stop=True)
        pe.matmul(bank[7][0:1, 0:MAX_EXTRA], e_id[:], pick[:, NE:], start=True, stop=True
                  ).then_inc(S["table_psum"], 1)
        pe.wait_ge(S["norm_dve"], 1 + TB)
        items = [Item(None, n) for n in range(2)]
        pe.wait_ge(S["onehot_made"], 1)
        for pair in range(4):
            if pair:
                pe.wait_ge(S["gather_taken"], pair)
            gather(pair)
        slot_weights(4, lambda it: it)
        up(items[0], 0)
        up(items[0], 1)
        pe.wait_ge(S["onehot_made"], 2)
        pe.wait_ge(S["wslot_made"], 1)
        for pair in range(4):
            if pair:
                pe.wait_ge(S["gather_taken"], pair + 4)
            gather(pair)
            if pair == 1:
                turn_g(items[0])
        up(items[1], 0)
        up(items[1], 1)
        pe.wait_ge(S["extra_in"], 1)
        batches = pe.value_load(extra_b[0:1, 0:1], min_val=0, max_val=8)
        with pe.Fori(0, batches + (NE // BATCH_ITEMS - 1)) as b:
            batch(b)
        batch(pe.snap(batches + (NE // BATCH_ITEMS - 1)), last=True)
        pe.wait_ge(S["scatter_done"], batches * 4 + (NE + 1))
        pe.nop().then_inc(S["acc_ready"], 1)


def waited_apart(eng, sem):
    eng.wait_ge(sem, 1)


class Item:

    def __init__(self, b, off, early=False):
        self.b, self.off, self.early = b, off, early
        self.first = b is None and off == 0

    def val(self, a, c):
        return a * self.off + c if self.b is None else self.b * (BATCH_ITEMS * a) + (a * self.off + c)

    def next(self, n=1):
        return Item(self.b, self.off + n)

    @property
    def parity(self):
        return self.off % 2

    def raw_slot(self, c):
        return 3 * self.parity + c if c < 2 else 5 - 3 * self.parity

    def uses_val(self, a):
        n = self.off // 2 + 1 + self.parity
        return a * n if self.b is None else self.b * (BATCH_ITEMS // 2 * a) + a * n


_INS = ["x", "c", "positions", "ada_mix_w", "ada_mix_b", "norm_mix_g", "w_in", "pool_w", "pool_scale",
        "cq_norm_g", "ckv_norm_g", "w_uq", "w_ukv", "w_oa", "w_ob", "w_oc", "w_out", "ada_ffn_w", "ada_ffn_b",
        "norm_ffn_g", "router_w", "router_bias", "exp_w1", "exp_w3", "exp_w2", "sh_w1", "sh_w3", "sh_w2",
        "final_g"]


def kernel(**inputs):
    import concourse.bacc as bacc
    from concourse.bass_utils import run_bass_kernel_spmd

    nc = bacc.Bacc("TRN2", target_bir_lowering=False, num_devices=1)
    arrays, tensors = {}, {}
    for name in _INS:
        a = np.ascontiguousarray(inputs[name])
        arrays[f"in_{name}"] = a
        tensors[name] = nc.dram_tensor(f"in_{name}", a.shape, mybir.dt.from_np(a.dtype), kind="ExternalInput").ap()
    out = nc.dram_tensor("out_y", (1, T, D), F32, kind="ExternalOutput").ap()
    hybrid_trunk(nc, tensors, out)
    r = run_bass_kernel_spmd(nc, [arrays], core_ids=[0])
    return r.results[0]["out_y"]
```

```python
from contextlib import ExitStack
import math

import numpy as np
import concourse.bass as bass
import concourse.mybir as mybir

F32 = mybir.dt.float32
F32R = mybir.dt.float32r
BF16 = mybir.dt.bfloat16
I32 = mybir.dt.int32
ALU = mybir.AluOpType
ACT = mybir.ActivationFunctionType
AX_X = mybir.AxisListType.X

P = 128
D = 1024
KD = D // P
T = 256
TB = T // P
DEPTH = 2
DH = 64
HEADS_A = 12
DILATIONS = (1, 4, 16)
N_BACK = 128
DA = HEADS_A * DH
DB = 512
WINDOWS = (2, 4, 8, 16)
HEADS_C = 8
NOPE, ROPE = 64, 32
QK = NOPE + ROPE
Q_LORA, KV_LORA = 384, 256
JQ, JKV = Q_LORA // P, KV_LORA // P
DC = HEADS_C * DH
HEADS = HEADS_A + HEADS_C
NE = 64
FF = 256
GROUP = 8
TOPK_GROUPS = 4
ROUTED_SCALE = 2.5
EPS = 1e-6
NEG = -1e30
TAKEN = -3e38
SLOTS = 64
BATCH_ITEMS = 4
MAX_EXTRA = 40
ITEMS = NE + MAX_EXTRA
NOT_HERE = 512.0
NO_ITEM = 1024.0
W_SLOTS = 2
ADA_SLOTS = 2
ADA0_SLOTS = 8
RAW = 6

HI = ("hi_a", "hi_b", "hi_c")
LO = ("lo_a", "lo_b", "lo_c")

COL_QK, COL_V = 0, 2 * DA
COL_U = 3 * DA
COL_C = COL_U + DB
COL_KR = COL_C + Q_LORA + KV_LORA
COL_G = COL_KR + ROPE

W_LOADS = [("w_in", COL_U, 512), ("w_in", COL_C, 512), ("w_in", COL_C + 512, 160)]
W_LOADS += [("w_in", COL_QK + 512 * i, 512) for i in range(3)]
W_LOADS += [("w_in", COL_V, 512), ("w_in", COL_V + 512, 256), ("w_uq", 0, 0), ("w_ukv", 0, 0)]
W_LOADS += [("w_in", COL_G + 512 * i, 512) for i in range(6)]
W_LOADS += [("w_o", 0, 512), ("w_o", 512, 512), ("w_out", 0, 512), ("w_out", 512, 512)]
W_BRANCH_ROWS = (("w_oa", 0, 2), ("w_ob", 2, 4), ("w_oc", 6, 4))
W_AT = {}
for _n, _load in enumerate(W_LOADS):
    W_AT.setdefault(_load[:2], _n)
W_LANDED = []
for _n, _load in enumerate(W_LOADS):
    W_LANDED.append((W_LANDED[_n - W_SLOTS] if _n >= W_SLOTS else 0) + (48 if _load[0] == "w_o" else 16))

UNITS = [(pair, qb) for pair in range(HEADS // 2) for qb in range(TB)]
GATE_GROUPS = [(c, blk) for c in range(6) for blk in range(TB)]


class Count:

    def __init__(self, eng, sem):
        self.eng, self.sem, self.n = eng, sem, 0

    def inc(self, ins):
        self.n += 1
        ins.then_inc(self.sem, 1)

    def wait(self):
        self.eng.wait_ge(self.sem, self.n)

    def step(self, ins):
        self.inc(ins)
        self.wait()


def hybrid_trunk(nc, t, out):
    stack = ExitStack()
    with stack:
        def sb(name, shape, dt=F32, where=stack):
            return where.enter_context(nc.sbuf_tensor(name, shape, dt))

        def sem(name):
            return stack.enter_context(nc.semaphore(name))

        bank = [stack.enter_context(nc.psum_tensor(f"bank{i}", [P, 512], F32)) for i in range(8)]

        x = sb("x", [P, TB, D])
        ident = sb("ident", [P, P])
        ones = sb("ones", [P, T])
        mask = sb("mask", [P, 3, TB, T], BF16)
        rcount = sb("rcount", [P, len(WINDOWS), 16])
        cos_sin = sb("cos_sin", [P, TB, 2, ROPE // 2])
        silu_c = sb("silu_c", [P, KD])
        mod_a = sb("mod_a", [P, 2, KD])
        mod_b = sb("mod_b", [P, 2, KD])
        gate_ffn = sb("gate_ffn", [P, D])
        small = sb("small", [P, 16])
        ada_acc = sb("ada_acc", [P, 3 * D])
        item_scratch = nc.dram_tensor("item_scratch", [ITEMS, T], BF16, kind="Internal").ap()

        s_first = sem("s_first")
        setup_dma = sem("setup_dma")
        pool_setup = sem("pool_setup")
        act_setup = sem("act_setup")
        dve_setup = sem("dve_setup")
        ada0_used = sem("ada0_used")
        ada0_loaded = [sem(f"ada0_loaded{i}") for i in range(ADA0_SLOTS)]

        def ada_source(w, n):
            return w.rearrange("(p k) n -> p k n", k=KD)[:, n // 2, 1536 * (n % 2):1536 * (n % 2 + 1)]

        def ada_step(dve, ring, n, loaded, used):
            k, half = (n // 2) % KD, n % 2
            slots = len(loaded)
            dve.wait_ge(loaded[n % slots], 16 * (n // slots + 1))
            acc = ada_acc[:, 1536 * half:1536 * (half + 1)]
            if k == 0:
                ins = dve.tensor_scalar(acc, ring[:, n % slots], silu_c[:, 0:1], None, ALU.mult)
            else:
                dve.wait_ge(used, n - 1)
                ins = dve.scalar_tensor_tensor(acc, ring[:, n % slots], silu_c[:, k:k + 1], acc,
                                               ALU.mult, ALU.add)
            ins.then_inc(used, 1)

        with ExitStack() as scope, nc.Block() as block:
            diff = sb("diff", [P, TB, T], I32, scope)
            low = sb("low", [P, len(DILATIONS), TB, T], I32, scope)
            ok = sb("ok", [P, TB, T], F32, scope)
            tok = sb("tok", [P, 16], I32, scope)
            tokf = sb("tokf", [P, 16], F32, scope)
            pos_i = sb("pos_i", [P, TB], I32, scope)
            pos_f = sb("pos_f", [P, TB], F32, scope)
            ang = sb("ang", [P, TB, 2, ROPE // 2], F32, scope)
            turns = sb("turns", [P, TB, 2, ROPE // 2], F32, scope)
            c_col = sb("c_col", [P, KD], F32, scope)
            ada0_ring = sb("ada0_ring", [P, ADA0_SLOTS, 1536], F32, scope)

            @block.sync
            def _(sp):
                sp.dma_start(c_col[:], t["c"][0].rearrange("(p k) -> p k", k=KD)).then_inc(setup_dma, 16)
                sp.dma_start(pos_i[:], t["positions"][0].rearrange("(b p) -> p b", p=P),
                             allow_slow_non_contiguous=True).then_inc(setup_dma, 16)
                for n in range(2 * KD):
                    if n >= ADA0_SLOTS:
                        sp.wait_ge(ada0_used, n - ADA0_SLOTS + 1)
                    sp.dma_start(ada0_ring[:, n % ADA0_SLOTS], ada_source(t["ada_mix_w"][0], n)
                                 ).then_inc(ada0_loaded[n % ADA0_SLOTS], 16)
                sp.dma_start(x[:], t["x"][0].rearrange("(b p) d -> p b d", p=P)).then_inc(setup_dma, 16)
                sp.wait_ge(setup_dma, 48)

            @block.gpsimd
            def _(pool):
                pool.memset(ident[:], 0.0).then_inc(pool_setup, 1)
                pool.memset(ones[:], 1.0).then_inc(pool_setup, 1)
                pool.iota(diff[:], [[P, TB], [-1, T]], base=0, channel_multiplier=1).then_inc(pool_setup, 1)
                pool.iota(tok[:], [[1, 16]], base=1, channel_multiplier=0).then_inc(pool_setup, 1)
                pool.wait_ge(pool_setup, 4)
                pool.affine_select(out=ident[:], in_=ident[:], compare_op=ALU.not_equal, fill=1.0, base=0,
                                   pattern=[[-1, P]], channel_multiplier=1).then_inc(pool_setup, 1)
                own = Count(pool, pool_setup)
                own.n = 5
                own.wait()
                pool.wait_ge(dve_setup, 1)
                for g, dil in enumerate(DILATIONS):
                    own.step(pool.tensor_copy(ok[:], low[:, g]))
                    own.step(pool.tensor_scalar(ok[:], ok[:], 0.0, NEG, ALU.is_gt, ALU.mult))
                    own.step(pool.affine_select(out=ok[:], in_=ok[:], compare_op=ALU.is_ge, fill=NEG, base=0,
                                                pattern=[[P, TB], [-1, T]], channel_multiplier=1))
                    own.step(pool.affine_select(out=mask[:, g], in_=ok[:], compare_op=ALU.is_ge, fill=NEG,
                                                base=N_BACK * dil, pattern=[[-P, TB], [1, T]],
                                                channel_multiplier=-1))

            @block.scalar
            def _(act):
                act.wait_ge(setup_dma, 32)
                act.activation(silu_c[:], c_col[:], ACT.Silu).then_inc(act_setup, 1)
                act.wait_ge(dve_setup, 2)
                act.activation(cos_sin[:], ang[:], ACT.Sin).then_inc(act_setup, 1)

            def angles(dve, own):
                dve.wait_ge(setup_dma, 32)
                own.step(dve.tensor_copy(pos_f[:], pos_i[:]))
                freqs = (np.float32(10000.0) ** (-np.arange(0, ROPE, 2, dtype=np.float32) / np.float32(ROPE)))
                for blk in range(TB):
                    for i, f in enumerate(freqs):
                        for part in range(2):
                            own.inc(dve.tensor_scalar(ang[:, blk, part, i:i + 1], pos_f[:, blk:blk + 1],
                                                      float(f), None, ALU.mult))
                own.wait()
                for part, quarter in ((0, 0.25), (1, 0.0)):
                    own.inc(dve.tensor_scalar(turns[:, :, part], ang[:, :, part], 1 / (2 * math.pi), quarter,
                                              ALU.mult, ALU.add))
                own.wait()
                magic = 1.5 * 2 ** 23
                own.step(dve.tensor_scalar(turns[:], turns[:], magic, None, ALU.add))
                own.step(dve.tensor_scalar(turns[:], turns[:], magic, None, ALU.subtract))
                first = 6.28125
                second = float(np.float32(math.floor((2 * math.pi - first) * 2 ** 20) / 2 ** 20))
                third = 2 * math.pi - first - second
                for piece in (first, second, third):
                    own.step(dve.scalar_tensor_tensor(ang[:], turns[:], -piece, ang[:], ALU.mult, ALU.add))
                own.step(dve.tensor_scalar(ang[:, :, 0], ang[:, :, 0], math.pi / 2, None, ALU.add))
                dve.tensor_scalar(ang[:], ang[:], 3.1415925, -3.1415925, ALU.min, ALU.max).then_inc(dve_setup, 1)

            @block.vector
            def _(dve):
                own = Count(dve, s_first)
                dve.wait_ge(pool_setup, 4)
                for g, dil in enumerate(DILATIONS):
                    own.inc(dve.tensor_scalar(low[:, g], diff[:], dil - 1, None, ALU.bitwise_and))
                own.wait()
                dve.nop().then_inc(dve_setup, 1)
                dve.wait_ge(act_setup, 1)
                for n in range(2 * KD):
                    ada_step(dve, ada0_ring, n, ada0_loaded, ada0_used)
                    if n == 1:
                        angles(dve, own)
                own.step(dve.tensor_copy(tokf[:], tok[:]))
                for g, w in enumerate(WINDOWS):
                    own.inc(dve.tensor_scalar(rcount[:, g], tokf[:], float(w), None, ALU.min))
                own.wait()
                own.step(dve.reciprocal(rcount[:], rcount[:]))

        nc.all_engine_barrier(sems_to_clear=range(s_first.num, ada0_loaded[-1].num + 1))

        names = """norm_act norm_dve norm_ready turned_ready act_own dve_own pool_own ada_used ada_summed
            gate_summed gate_bias_in ada_bcast mod_ready consts_in hT_ready proj_ready proj_taken
            sums_ready rstd_sq latent_ready rope_ready qt_ready qt_taken pooled_ready mixed_ready
            mixed_taken s_ready s_taken max_ready p_ready pt_ready pt_taken o_ready o_taken coef_in
            coef_out y_ready yt_ready yt_taken branch_ready branch_taken mix_ready mixt_ready mixt_taken
            res_ready router_in logits_ready sig_ready sel_ready selt_ready tables_ready tables_summed
            counts_made counts_summed scratch_written extra_in shared_up shared_act shared_g shared_gt
            shared_gt_taken shared_used hi_a hi_b hi_c lo_a lo_b lo_c a_free b_free added silu_done
            mul_done gt_ready gt_hi gt_lo down_done y_hi y_lo s_made gather_ready gather_taken
            onehot_made wslot_ready wslot_made wslot_moved xg_hi xg_lo scatter_done t_done pos_in
            acc_ready out_done final_in""".split()
        S = {}
        for n in names:
            S[n] = sem(n)
        w_loaded = [sem(f"w_loaded{i}") for i in range(W_SLOTS)]
        ada_loaded = [sem(f"ada_loaded{i}") for i in range(ADA_SLOTS)]
        raw_loaded = [sem(f"raw_loaded{i}") for i in range(RAW)]
        block_sems = range(S[names[0]].num, raw_loaded[-1].num + 1)

        def norm_act(act, own, squares):
            for blk in range(TB):
                own.inc(act.activation(squares, x[:, blk], ACT.Square, accum_out=small[:, blk:blk + 1]))
                own.wait()
            act.nop().then_inc(S["norm_act"], 1)
            act.wait_ge(S["norm_dve"], 1)
            act.activation(small[:, 4:6], small[:, 2:4], ACT.Sqrt).then_inc(S["norm_act"], 1)

        def norm_dve(dve, own):
            dve.wait_ge(S["norm_act"], 1)
            own.step(dve.tensor_scalar(small[:, 6:8], small[:, 0:2], 1.0 / D, EPS, ALU.mult, ALU.add))
            dve.reciprocal(small[:, 2:4], small[:, 6:8]).then_inc(S["norm_dve"], 1)
            dve.wait_ge(S["norm_act"], 2)
            own.step(dve.tensor_tensor(small[:, 8:10], small[:, 4:6], small[:, 4:6], ALU.mult))
            own.step(dve.tensor_tensor(small[:, 8:10], small[:, 8:10], small[:, 6:8], ALU.mult))
            own.step(dve.tensor_scalar(small[:, 8:10], small[:, 8:10], -0.5, 1.5, ALU.mult, ALU.add))
            own.step(dve.tensor_tensor(small[:, 4:6], small[:, 4:6], small[:, 8:10], ALU.mult))

        def turn_pe(pe, xn, banks):
            for k in range(KD):
                for blk in range(TB):
                    mm = pe.transpose(banks[k // 2][:, (k % 2) * T + blk * P:(k % 2) * T + blk * P + P],
                                      xn[:, blk, k::KD], ident[:])
                if k % 2:
                    mm.then_inc(S["turned_ready"], 1)

        def modulate_act(act, hT, banks, which):
            for k in range(KD):
                if k % 2 == 0:
                    act.wait_ge(S["turned_ready"], k // 2 + 1)
                mm = act.activation(hT[:, k], banks[k // 2][:, (k % 2) * T:(k % 2 + 1) * T], ACT.Identity,
                                    bias=mod_b[:, which, k:k + 1], scale=mod_a[:, which, k:k + 1])
            mm.then_inc(S["hT_ready"], 1)

        stages = dict(locals())
        with nc.Fori(0, DEPTH) as layer:
            with ExitStack() as scope, nc.Block() as block:
                mixer_block(nc, t, layer, stages, lambda n, s, d=F32: sb(n, s, d, scope), block)
            nc.all_engine_barrier(sems_to_clear=block_sems)
            with ExitStack() as scope, nc.Block() as block:
                experts_block(nc, t, layer, stages, lambda n, s, d=F32: sb(n, s, d, scope), block)
            nc.all_engine_barrier(sems_to_clear=block_sems)

        with ExitStack() as scope, nc.Block() as block:
            squares = sb("squares", [P, D], F32, scope)
            final_g = sb("final_g_row", [P, D], F32, scope)
            y = sb("y_out", [P, TB, D], F32, scope)

            @block.sync
            def _(sp):
                sp.dma_start(final_g[:], t["final_g"].rearrange("(a d) -> a d", a=1).to_broadcast([P, D])
                             ).then_inc(S["final_in"], 16)
                for blk in range(TB):
                    sp.wait_ge(S["norm_ready"], blk + 1)
                    sp.dma_start(out[0, blk * P:(blk + 1) * P, :], y[:, blk]).then_inc(S["out_done"], 16)
                sp.wait_ge(S["out_done"], 16 * TB)

            @block.scalar
            def _(act):
                norm_act(act, Count(act, S["act_own"]), squares[:])

            @block.vector
            def _(dve):
                norm_dve(dve, Count(dve, S["dve_own"]))
                dve.wait_ge(S["final_in"], 16)
                for blk in range(TB):
                    dve.scalar_tensor_tensor(y[:, blk], x[:, blk], small[:, 4 + blk:5 + blk], final_g[:],
                                             ALU.mult, ALU.mult).then_inc(S["norm_ready"], 1)


def mixer_block(nc, t, layer, g, sb, block):
    S, bank, x, ident, ones = g["S"], g["bank"], g["x"], g["ident"], g["ones"]
    mask, rcount, cos_sin, silu_c = g["mask"], g["rcount"], g["cos_sin"], g["silu_c"]
    mod_a, mod_b, gate_ffn, small = g["mod_a"], g["mod_b"], g["gate_ffn"], g["small"]
    w_loaded, ada_loaded, ada_acc = g["w_loaded"], g["ada_loaded"], g["ada_acc"]

    hT = sb("m_hT", [P, KD, T])
    xn_o = sb("xn_o", [P, TB * HEADS * DH])
    xn = xn_o[:, 0:TB * D].rearrange("p (b d) -> p b d", b=TB)
    heads_o = xn_o[:, :].rearrange("p (b h e) -> p b h e", b=TB, h=HEADS)
    qk_t = sb("qk_t", [P, 12 * T])
    qkT = qk_t[:, :].rearrange("p (j t) -> p j t", j=12)
    yT = qk_t[:, 0:6 * T].rearrange("p (j t) -> p j t", j=6)
    va = sb("va", [P, TB, DA])
    uT = sb("uT", [P, 4, T])
    ybT = uT
    latent = sb("latent", [P, 5, T])
    tanh_g = sb("tanh_g", [P, TB, 3 * D])
    q_y = sb("q_y", [P, TB, (HEADS_C + 1) * QK])
    y_nat = q_y[:, :, 0:768]
    qT_mix = sb("qT_mix", [P, 8 * T])
    qcT = qT_mix[0:QK, :].rearrange("p (h t) -> p h t", h=8)
    raw_c = qT_mix[:, 0:5 * T].rearrange("p (j t) -> p j t", j=5)
    mix = qT_mix[:, :].rearrange("p (b d) -> p b d", b=TB)
    kT_mixT = sb("kT_mixT", [P, 8 * T])
    kcT = kT_mixT[0:QK, :].rearrange("p (h t) -> p h t", h=8)
    sq_c = kT_mixT[:, 0:5 * T].rearrange("p (j t) -> p j t", j=5)
    mixT = kT_mixT[:, :].rearrange("p (k t) -> p k t", k=KD)
    vc = sb("vc", [P, TB, DC])
    att = sb("att", [P, 3, 2, 2, T])
    s_sb, p_sb, pt_sb = att[:, 0], att[:, 1], att[:, 2]
    flat = att[:, :, :, :, :].rearrange("p a b c t -> p (a b c t)")
    pooled = flat[:, 0:4 * T].rearrange("p (g t) -> p g t", g=4)
    cs = flat[:, 4 * T:4 * T + 4 * (16 + T)].rearrange("p (g t) -> p g t", g=4)
    squares = flat[:, 0:D]
    rope_t = sb("rope_t", [P, 4, HEADS_C + 1, ROPE // 2])
    neg_max = sb("neg_max", [P, TB, HEADS])
    den = sb("den", [P, TB, HEADS])
    fac = sb("fac", [P, 4, HEADS_A])
    gate_mix = sb("gate_mix", [P, D])
    scaled = sb("scaled", [P, 3, 512])
    rstd = scaled[:, 0:2].rearrange("p a (b t) -> p a b t", b=2)
    wring = sb("wring", [P, W_SLOTS, 5120])
    ada_ring = sb("ada_ring", [P, ADA_SLOTS, 1536])
    pool_w = sb("pool_w_sb", [P, 4, P])
    cols = sb("cols", [P, 64])
    g_col = [cols[:, 0:8], cols[:, 8:16]]
    shift_col = [cols[:, 16:24], cols[:, 24:32]]
    scale_col = [cols[:, 32:40], cols[:, 40:48]]
    pscale = cols[:, 48:52]
    lat_g = cols[:, 52:57]
    gates = (gate_mix, gate_ffn)
    N_SMALL = 10
    gate_bank = (6, 4)

    def w_view(n, rows, width):
        return wring[:, n % W_SLOTS, 0:rows * width].rearrange("p (r n) -> p r n", r=rows)

    first = [("T", W_AT["w_in", COL_U], 0, 2, uT[:, 0:2]), ("T", W_AT["w_in", COL_U], 256, 2, uT[:, 2:4]),
             ("C", W_AT["w_in", COL_C], 0, 2, 0), ("C", W_AT["w_in", COL_C], 256, 2, 2),
             ("C", W_AT["w_in", COL_C + 512], 0, 1, 4),
             ("N2", W_AT["w_in", COL_C + 512], 128, ROPE, q_y[:, :, HEADS_C * QK + NOPE:])]
    second = []
    for i in range(3):
        for half in range(2):
            second.append(("T", W_AT["w_in", COL_QK + 512 * i], 256 * half, 2,
                           qkT[:, 4 * i + 2 * half:4 * i + 2 * half + 2]))
    second += [("N", W_AT["w_in", COL_V], 0, (blk, 512), va[:, blk, 0:512]) for blk in range(TB)]
    second += [("N2", W_AT["w_in", COL_V + 512], 0, 256, va[:, :, 512:768])]
    second += [("Q", W_AT["w_uq", 0], 0, (blk, 512), q_y[:, blk, 0:512]) for blk in range(TB)]
    second += [("Q2", W_AT["w_uq", 0], 512, 256, q_y[:, :, 512:768])]
    second += [("K", W_AT["w_ukv", 0], 2 * h, 2, kcT[0:NOPE, 2 * h:2 * h + 2]) for h in range(4)]
    second += [("V", W_AT["w_ukv", 0], 0, blk, vc[:, blk]) for blk in range(TB)]
    gate_projections = [("G", W_AT["w_in", COL_G + 512 * c], 0, (blk, 512), tanh_g[:, blk, 512 * c:512 * c + 512])
             for c, blk in GATE_GROUPS]
    projections = first + second + gate_projections
    last_of_load = {p[1]: n for n, p in enumerate(projections)}

    def gates_at(u):
        n = len(GATE_GROUPS) - 1
        return range(u * n // 20, (u + 1) * n // 20) if u < 20 else range(0)

    def scales(pair):
        return DH ** -0.5 if pair < 6 else QK ** -0.5

    @block.sync
    def _(sp):
        loads = [(pool_w[:], t["pool_w"][layer].rearrange("g c d -> c g d")),
                 (pscale, t["pool_scale"][layer].rearrange("(g p) -> p g", p=P)),
                 (lat_g[:, 0:JQ], t["cq_norm_g"][layer].rearrange("(j p) -> p j", p=P)),
                 (lat_g[:, JQ:5], t["ckv_norm_g"][layer].rearrange("(j p) -> p j", p=P))]
        for i, kind in enumerate(("mix", "ffn")):
            bias = t[f"ada_{kind}_b"][layer]
            loads += [(g_col[i], t[f"norm_{kind}_g"][layer].rearrange("(p k) -> p k", k=KD)),
                      (shift_col[i], bias[0:D].rearrange("(p k) -> p k", k=KD)),
                      (scale_col[i], bias[D:2 * D].rearrange("(p k) -> p k", k=KD))]
        assert len(loads) == N_SMALL
        for dst, src in loads:
            sp.dma_start(dst, src, allow_slow_non_contiguous=True).then_inc(S["consts_in"], 16)
        for n, (src, col, width) in enumerate(W_LOADS):
            if n == 0:
                continue
            if n == 2:
                for i, kind in enumerate(("mix", "ffn")):
                    sp.dma_start(gates[i][:], t[f"ada_{kind}_b"][layer][2 * D:3 * D].rearrange("(a d) -> a d", a=1)
                                 .to_broadcast([P, D])).then_inc(S["gate_bias_in"], 16)
            if n >= W_SLOTS:
                held = n - W_SLOTS
                if held in last_of_load:
                    sp.wait_ge(S["proj_ready"], last_of_load[held] + 1)
                else:
                    sp.wait_ge(S["branch_ready"], TB * (held - W_AT["w_o", 0] + 1))
            if src == "w_o":
                for name, row, rows in W_BRANCH_ROWS:
                    sp.dma_start(w_view(n, 10, 512)[:, row:row + rows],
                                 t[name][layer][:, col:col + 512].rearrange("(j p) n -> p j n", p=P)
                                 ).then_inc(w_loaded[n % W_SLOTS], 16)
                continue
            w = t[src][layer]
            if src in ("w_in", "w_out"):
                dst = w_view(n, KD, width)
                sp.dma_start(dst, w[:, col:col + width].rearrange("(p k) n -> p k n", k=KD)
                             ).then_inc(w_loaded[n % W_SLOTS], 16)
            else:
                rows, width = w.shape[0] // P, w.shape[1]
                sp.dma_start(w_view(n, rows, width), w.rearrange("(j p) n -> p j n", p=P)
                             ).then_inc(w_loaded[n % W_SLOTS], 16)

    @block.scalar
    def _(act):
        own = Count(act, S["act_own"])
        def load_ada(n):
            src = t["ada_ffn_w"][layer] if n < 2 * KD else t["ada_mix_w"][next_layer]
            if n >= ADA_SLOTS:
                act.wait_ge(S["ada_used"], n - ADA_SLOTS + 1)
            act.dma_start(ada_ring[:, n % ADA_SLOTS], g["ada_source"](src, n % (2 * KD))
                          ).then_inc(ada_loaded[n % ADA_SLOTS], 16)

        next_layer = act.snap((layer + 1) % DEPTH)
        act.dma_start(w_view(0, KD, W_LOADS[0][2]), t["w_in"][layer][:, W_LOADS[0][1]:W_LOADS[0][1] + W_LOADS[0][2]]
                      .rearrange("(p k) n -> p k n", k=KD)).then_inc(w_loaded[0], 16)
        g["norm_act"](act, own, squares)
        act.wait_ge(S["mod_ready"], 1)
        g["modulate_act"](act, hT, bank[2:6], 0)
        for n in range(ADA_SLOTS):
            load_ada(n)

        def take_projection(n):
            kind, load, col, size, dst = projections[n]
            act.wait_ge(S["proj_ready"], n + 1)
            ps = bank[n % 2]
            if kind in ("T", "K"):
                rows = P if kind == "T" else NOPE
                ins = act.activation(dst, ps[0:rows, 0:size * T].rearrange("p (j t) -> p j t", j=size), ACT.Copy)
            elif kind == "C":
                src = ps[:, 0:size * T].rearrange("p (j t) -> p j t", j=size)
                act.activation(raw_c[:, dst:dst + size], src, ACT.Copy)
                ins = act.activation(sq_c[:, dst:dst + size], src, ACT.Square)
            elif kind in ("N2", "Q2"):
                ins = act.activation(dst, ps[:, 0:TB * size].rearrange("p (b n) -> p b n", b=TB), ACT.Copy)
            elif kind == "G":
                ins = act.activation(dst, ps[:], ACT.Tanh, scale=0.5)
            else:
                ins = act.activation(dst, ps[:], ACT.Copy)
            ins.then_inc(S["proj_taken"], 1)
            if n + ADA_SLOTS < 2 * KD:
                load_ada(n + ADA_SLOTS)

        for n in range(len(first)):
            take_projection(n)
        act.wait_ge(S["rstd_sq"], 1)
        act.activation(rstd[:, :, 0], rstd[:, :, 1], ACT.Sqrt).then_inc(S["rstd_sq"], 1)
        for n in range(len(first), len(first) + len(second)):
            if n == len(first) + 12:
                act.wait_ge(S["sums_ready"], 1)
            take_projection(n)
        for i in range(2):
            act.wait_ge(S["mixed_ready"], i + 1)
            for j in range(2):
                ins = act.activation(ybT[:, 2 * i + j], bank[6 + i][:, j * T:(j + 1) * T], ACT.Copy,
                                     scale=pscale[:, 2 * i + j:2 * i + j + 1])
            ins.then_inc(S["mixed_taken"], 1)
        for i in range(5):
            act.wait_ge(S["qt_ready"], i + 1)
            src = bank[2 + i % 2][0:QK, :].rearrange("p (j t) -> p j t", j=2)
            if i < 4:
                ins = act.activation(qcT[:, 2 * i:2 * i + 2], src, ACT.Copy)
            else:
                ins = act.activation(kcT[NOPE:QK], src[NOPE:QK, 0:1].to_broadcast([ROPE, HEADS_C, T]), ACT.Copy)
            ins.then_inc(S["qt_taken"], 1)

        for n in range(2 * KD, 2 * KD + ADA_SLOTS):
            load_ada(n)
        gate_n = len(first) + len(second)
        for u in range(len(UNITS) + 2):
            if u < len(UNITS):
                pair, qb = UNITS[u]
                act.wait_ge(S["max_ready"], u + 1)
                if u >= 2:
                    act.wait_ge(S["pt_ready"], u - 1)
                for h in range(2):
                    ins = act.activation(p_sb[:, u % 2, h, 0:P * (qb + 1)], s_sb[:, u % 2, h, 0:P * (qb + 1)],
                                         ACT.Exp, bias=neg_max[:, qb, 2 * pair + h:2 * pair + h + 1],
                                         accum_out=den[:, qb, 2 * pair + h:2 * pair + h + 1])
                ins.then_inc(S["p_ready"], 1)
            if 1 <= u and u + 1 < 2 * KD:
                load_ada(2 * KD + u + 1)
            for n in gates_at(u):
                take_projection(gate_n + n)
            if u >= 2:
                pair, qb = UNITS[u - 2]
                act.wait_ge(S["o_ready"], u - 1)
                act.activation(heads_o[:, qb, 2 * pair:2 * pair + 2],
                               bank[7][:, 0:2 * DH].rearrange("p (h e) -> p h e", h=2),
                               ACT.Copy).then_inc(S["o_taken"], 1)
        for qb in range(TB):
            act.wait_ge(S["coef_in"], qb + 1)
            act.activation(fac[:, 2 * qb], fac[:, 2 * qb], ACT.Exp).then_inc(S["coef_out"], 1)
        take_projection(len(projections) - 1)
        for i in range(3):
            act.wait_ge(S["yt_ready"], i + 1)
            act.activation(yT[:, 2 * i:2 * i + 2], bank[2 + i][:].rearrange("p (j t) -> p j t", j=2),
                           ACT.Copy).then_inc(S["yt_taken"], 1)
        for i in range(4):
            act.wait_ge(S["mixt_ready"], i + 1)
            act.activation(mixT[:, 2 * i:2 * i + 2], bank[6 + i % 2][:].rearrange("p (j t) -> p j t", j=2),
                           ACT.Copy, scale=0.5).then_inc(S["mixt_taken"], 1)

    @block.vector
    def _(dve):
        own = Count(dve, S["dve_own"])

        def ada_steps(a, b):
            for n in range(a, b):
                g["ada_step"](dve, ada_ring, n, ada_loaded, S["ada_used"])

        def take_sums(which):
            dve.wait_ge(S["ada_summed"], which + 1)
            dve.wait_ge(S["consts_in"], 16 * N_SMALL)
            own.inc(dve.tensor_tensor(mod_b[:, which], bank[0][:, 0:KD], shift_col[which], ALU.add))
            own.step(dve.tensor_tensor(mod_a[:, which], bank[0][:, KD:2 * KD], scale_col[which], ALU.add))
            dve.scalar_tensor_tensor(mod_a[:, which], mod_a[:, which], 1.0, g_col[which], ALU.add,
                                     ALU.mult).then_inc(S["mod_ready"], 1)
            dve.wait_ge(S["gate_summed"], which + 1)
            dve.wait_ge(S["gate_bias_in"], 32)
            for half in range(2):
                gate = gates[which][:, 512 * half:512 * (half + 1)]
                ins = dve.tensor_tensor(gate, bank[gate_bank[which] + half][:], gate, ALU.add)
            ins.then_inc(S["ada_bcast"], 1)

        g["norm_dve"](dve, own)
        for blk in range(TB):
            dve.tensor_scalar(xn[:, blk], x[:, blk], small[:, 4 + blk:5 + blk], None,
                              ALU.mult).then_inc(S["norm_ready"], 1)
        take_sums(0)
        ada_steps(0, 2)

        own.inc(dve.memset(cs[:, :, 0:16], 0.0))
        for grp in range(4):
            dve.wait_ge(S["proj_taken"], grp // 2 + 1)
            own.inc(dve.tensor_tensor_scan(cs[:, grp, 16:], ones[:], uT[:, grp], 0.0, ALU.mult, ALU.add))
        own.wait()
        for grp, w in enumerate(WINDOWS):
            own.inc(dve.tensor_tensor(pooled[:, grp], cs[:, grp, 16:], cs[:, grp, 16 - w:16 - w + T], ALU.subtract))
        own.wait()
        for grp, w in enumerate(WINDOWS):
            own.inc(dve.tensor_tensor(pooled[:, grp, 0:16], pooled[:, grp, 0:16], rcount[:, grp], ALU.mult))
        own.wait()
        for grp, w in enumerate(WINDOWS):
            own.inc(dve.tensor_tensor(pooled[:, grp, 0:16], pooled[:, grp, 0:16], uT[:, grp, 0:16], ALU.subtract))
            own.inc(dve.scalar_tensor_tensor(pooled[:, grp, 16:], pooled[:, grp, 16:], 1.0 / w, uT[:, grp, 16:],
                                             ALU.mult, ALU.subtract))
        own.wait()
        dve.nop().then_inc(S["pooled_ready"], 1)

        ada_steps(2, 6)
        dve.wait_ge(S["sums_ready"], 1)
        for i, n in enumerate((Q_LORA, KV_LORA)):
            own.inc(dve.tensor_scalar(cs[:, i, 0:T], bank[2][:, i * T:(i + 1) * T], 1.0 / n, EPS, ALU.mult, ALU.add))
        own.wait()
        ms = cs[:, 0:2, 0:T]
        dve.reciprocal(rstd[:, :, 1], ms).then_inc(S["rstd_sq"], 1)
        dve.wait_ge(S["rstd_sq"], 2)
        own.step(dve.tensor_tensor(rstd[:, :, 1], rstd[:, :, 0], rstd[:, :, 0], ALU.mult))
        own.step(dve.tensor_tensor(rstd[:, :, 1], rstd[:, :, 1], ms, ALU.mult))
        own.step(dve.tensor_scalar(rstd[:, :, 1], rstd[:, :, 1], -0.5, 1.5, ALU.mult, ALU.add))
        own.step(dve.tensor_tensor(rstd[:, :, 0], rstd[:, :, 0], rstd[:, :, 1], ALU.mult))
        for j in range(5):
            ins = dve.scalar_tensor_tensor(latent[:, j], raw_c[:, j], lat_g[:, j:j + 1],
                                           rstd[:, 0 if j < JQ else 1, 0], ALU.mult, ALU.mult)
        ins.then_inc(S["latent_ready"], 1)

        ada_steps(6, 2 * KD)
        own.inc(dve.memset(q_y[:, :, HEADS_C * QK:HEADS_C * QK + NOPE], 0.0))
        dve.wait_ge(S["proj_taken"], len(first) + 12)
        for blk in range(TB):
            heads = q_y[:, blk].rearrange("p (h e) -> p h e", e=QK)
            x1, x2 = heads[:, :, NOPE:NOPE + ROPE // 2], heads[:, :, NOPE + ROPE // 2:QK]
            cos, sin = (cos_sin[:, blk, i:i + 1].to_broadcast([P, HEADS_C + 1, ROPE // 2]) for i in range(2))
            own.inc(dve.tensor_tensor(rope_t[:, 0], x1, cos, ALU.mult))
            own.inc(dve.tensor_tensor(rope_t[:, 1], x2, sin, ALU.mult))
            own.inc(dve.tensor_tensor(rope_t[:, 2], x2, cos, ALU.mult))
            own.step(dve.tensor_tensor(rope_t[:, 3], x1, sin, ALU.mult))
            own.inc(dve.tensor_tensor(x1, rope_t[:, 0], rope_t[:, 1], ALU.subtract))
            own.step(dve.tensor_tensor(x2, rope_t[:, 2], rope_t[:, 3], ALU.add))
        dve.nop().then_inc(S["rope_ready"], 1)
        take_sums(1)

        for u in range(len(UNITS) + 1):
            if u < len(UNITS):
                pair, qb = UNITS[u]
                nk = P * (qb + 1)
                dve.wait_ge(S["s_ready"], u + 1)
                if u >= 2:
                    dve.wait_ge(S["p_ready"], u - 1)
                ps = [bank[2 + 2 * (u % 2) + h][:, 0:nk] for h in range(2)]
                grp = pair // 2 if pair < 6 else 0
                for h in range(2):
                    if pair < 6:
                        dve.scalar_tensor_tensor(s_sb[:, u % 2, h, 0:nk], ps[h], scales(pair),
                                                 mask[:, grp, qb, 0:nk], ALU.mult, ALU.add
                                                 ).then_inc(S["s_taken"], 1)
                    else:
                        if qb:
                            dve.tensor_scalar(s_sb[:, u % 2, h, 0:P], ps[h][:, 0:P], scales(pair), None, ALU.mult)
                        dve.scalar_tensor_tensor(s_sb[:, u % 2, h, nk - P:nk], ps[h][:, nk - P:nk], scales(pair),
                                                 mask[:, 0, 0, 0:P], ALU.mult, ALU.add).then_inc(S["s_taken"], 1)
                dve.wait_ge(S["s_taken"], 2 * u + 2)
                own.step(dve.tensor_reduce(neg_max[:, qb, 2 * pair:2 * pair + 2], s_sb[:, u % 2, :, 0:nk], AX_X,
                                           ALU.max))
                dve.tensor_scalar(neg_max[:, qb, 2 * pair:2 * pair + 2], neg_max[:, qb, 2 * pair:2 * pair + 2], -1.0,
                                  None, ALU.mult).then_inc(S["max_ready"], 1)
            if u >= 1:
                pair, qb = UNITS[u - 1]
                nk = P * (qb + 1)
                dve.wait_ge(S["pt_ready"], u)
                if u >= 3:
                    dve.wait_ge(S["o_ready"], u - 2)
                dve.tensor_copy(pt_sb[:, (u - 1) % 2, :, 0:nk],
                                bank[6][:].rearrange("p (h k) -> p h k", h=2)[:, :, 0:nk]
                                ).then_inc(S["pt_taken"], 1)
            if u < 2 * KD:
                ada_steps(2 * KD + u, 2 * KD + u + 1)
        dve.wait_ge(S["o_taken"], len(UNITS))
        for qb in range(TB):
            nm = neg_max[:, qb, 0:HEADS_A].rearrange("p (g h) -> p g h", g=3)
            f = fac[:, 2 * qb].rearrange("p (g h) -> p g h", g=3)
            w = fac[:, 2 * qb + 1].rearrange("p (g h) -> p g h", g=3)
            own.step(dve.tensor_tensor(w[:, 0], nm[:, 0], nm[:, 1], ALU.min))
            own.step(dve.tensor_tensor(w[:, 0], w[:, 0], nm[:, 2], ALU.min))
            for grp in range(3):
                own.inc(dve.tensor_tensor(f[:, grp], w[:, 0], nm[:, grp], ALU.subtract))
            own.wait()
            dve.nop().then_inc(S["coef_in"], 1)
        for qb in range(TB):
            f = fac[:, 2 * qb].rearrange("p (g h) -> p g h", g=3)
            w = fac[:, 2 * qb + 1].rearrange("p (g h) -> p g h", g=3)
            dve.wait_ge(S["coef_out"], qb + 1)
            own.step(dve.tensor_tensor(w, f, den[:, qb, 0:HEADS_A].rearrange("p (g h) -> p g h", g=3), ALU.mult))
            own.step(dve.tensor_tensor(w[:, 0], w[:, 0], w[:, 1], ALU.add))
            own.step(dve.tensor_tensor(w[:, 0], w[:, 0], w[:, 2], ALU.add))
            own.inc(dve.reciprocal(w[:, 1], w[:, 0]))
            own.step(dve.reciprocal(den[:, qb, HEADS_A:], den[:, qb, HEADS_A:]))
            for grp in range(3):
                own.inc(dve.tensor_tensor(f[:, grp], f[:, grp], w[:, 1], ALU.mult))
            own.wait()
            own.inc(dve.tensor_tensor(heads_o[:, qb, 0:HEADS_A], heads_o[:, qb, 0:HEADS_A],
                                      fac[:, 2 * qb, :, None].to_broadcast([P, HEADS_A, DH]), ALU.mult))
            yc = y_nat[:, qb, 4 * DH:].rearrange("p (h e) -> p h e", e=DH)
            own.inc(dve.tensor_tensor(yc, heads_o[:, qb, HEADS_A:], den[:, qb, HEADS_A:, None].to_broadcast(
                [P, HEADS_C, DH]), ALU.mult))
            own.wait()
            ya = y_nat[:, qb, 0:4 * DH].rearrange("p (h e) -> p h e", e=DH)
            own.step(dve.tensor_tensor(ya, heads_o[:, qb, 0:4], heads_o[:, qb, 4:8], ALU.add))
            dve.tensor_tensor(ya, ya, heads_o[:, qb, 8:12], ALU.add).then_inc(S["y_ready"], 1)

        for n in range(2 * TB):
            half, blk = n // TB, n % TB
            dve.wait_ge(S["branch_ready"], n + 1)
            for br in range(3):
                own.inc(dve.scalar_tensor_tensor(
                    scaled[:, br], tanh_g[:, blk, D * br + 512 * half:D * br + 512 * (half + 1)], 1.0,
                    bank[3 * (n % 2) + br][:], ALU.add, ALU.mult))
            own.wait()
            dve.nop().then_inc(S["branch_taken"], 1)
            own.step(dve.tensor_tensor(scaled[:, 0], scaled[:, 0], scaled[:, 1], ALU.add))
            dst = mix[:, blk, 512 * half:512 * (half + 1)]
            own.step(dve.tensor_tensor(dst, scaled[:, 0], scaled[:, 2], ALU.add))
        dve.nop().then_inc(S["mix_ready"], 1)

        for n in range(2 * TB):
            half, blk = n // TB, n % TB
            dve.wait_ge(S["res_ready"], n + 1)
            cut = slice(512 * half, 512 * (half + 1))
            own.step(dve.tensor_tensor(scaled[:, 0], gate_mix[:, cut], bank[n][:], ALU.mult))
            own.step(dve.tensor_tensor(x[:, blk, cut], x[:, blk, cut], scaled[:, 0], ALU.add))

    @block.tensor
    def _(pe):
        def sum_columns():
            for part in range(2):
                for k in range(KD):
                    mm = pe.matmul(bank[0][:, part * KD + k:part * KD + k + 1],
                                   ada_acc[:, part * D + k:(part + 1) * D:KD], ones[:, 0:1], start=True, stop=True)
            mm.then_inc(S["ada_summed"], 1)

        def sum_gate(which):
            for half in range(2):
                mm = pe.matmul(bank[gate_bank[which] + half][:], ones[:, 0:P],
                               ada_acc[:, 2 * D + 512 * half:2 * D + 512 * (half + 1)], start=True, stop=True)
            mm.then_inc(S["gate_summed"], 1)

        sum_columns()
        pe.wait_ge(S["norm_ready"], TB)
        g["turn_pe"](pe, xn, bank[2:6])
        pe.wait_ge(S["hT_ready"], 1)

        def project(n):
            kind, load, col, size, dst = projections[n]
            ps = bank[n % 2]
            pe.wait_ge(w_loaded[load % W_SLOTS], W_LANDED[load])
            if n >= 2:
                pe.wait_ge(S["proj_taken"], n - 1)
            if kind in ("T", "C"):
                w = w_view(load, KD, W_LOADS[load][2])
                for j in range(size):
                    for k in range(KD):
                        mm = pe.matmul(ps[:, j * T:(j + 1) * T], w[:, k, col + P * j:col + P * (j + 1)], hT[:, k],
                                       start=(k == 0), stop=(k == KD - 1))
            elif kind in ("N", "G"):
                w = w_view(load, KD, W_LOADS[load][2])
                blk, width = size
                for k in range(KD):
                    mm = pe.matmul(ps[:, 0:width], hT[:, k, blk * P:(blk + 1) * P], w[:, k, col:col + width],
                                   start=(k == 0), stop=(k == KD - 1))
            elif kind == "N2":
                w = w_view(load, KD, W_LOADS[load][2])
                for blk in range(TB):
                    for k in range(KD):
                        mm = pe.matmul(ps[:, blk * size:(blk + 1) * size], hT[:, k, blk * P:(blk + 1) * P],
                                       w[:, k, col:col + size], start=(k == 0), stop=(k == KD - 1))
            elif kind in ("Q", "Q2"):
                w = w_view(load, JQ, HEADS_C * QK)
                for blk, width, at in ([(size[0], size[1], 0)] if kind == "Q"
                                       else [(b, size, b * size) for b in range(TB)]):
                    for j in range(JQ):
                        mm = pe.matmul(ps[:, at:at + width], latent[:, j, blk * P:(blk + 1) * P],
                                       w[:, j, col:col + width], start=(j == 0), stop=(j == JQ - 1))
            elif kind == "K":
                w = w_view(load, JKV, HEADS_C * P)
                for h in range(size):
                    for j in range(JKV):
                        mm = pe.matmul(ps[0:NOPE, h * T:(h + 1) * T],
                                       w[:, j, (col + h) * P:(col + h) * P + NOPE], latent[:, JQ + j],
                                       start=(j == 0), stop=(j == JKV - 1))
            else:
                w = w_view(load, JKV, HEADS_C * P).rearrange("p j (h e) -> p j h e", e=P)
                for j in range(JKV):
                    mm = pe.matmul(ps[:], latent[:, JQ + j, size * P:(size + 1) * P], w[:, j, :, NOPE:P],
                                   start=(j == 0), stop=(j == JKV - 1))
            mm.then_inc(S["proj_ready"], 1)

        for n in range(len(first)):
            project(n)
            if n == 1:
                sum_gate(0)
        pe.wait_ge(S["proj_taken"], 5)
        for i, tiles in enumerate((range(JQ), range(JQ, 5))):
            for j in tiles:
                mm = pe.matmul(bank[2][:, i * T:(i + 1) * T], ones[:, 0:P], sq_c[:, j],
                               start=(j == tiles[0]), stop=(j == tiles[-1]))
        mm.then_inc(S["sums_ready"], 1)
        for n in range(len(first), len(first) + len(second)):
            if projections[n][0] == "Q":
                pe.wait_ge(S["latent_ready"], 1)
            project(n)
        pe.wait_ge(S["pooled_ready"], 1)
        pe.wait_ge(S["ada_bcast"], 1)
        for i in range(2):
            for j in range(2):
                mm = pe.matmul(bank[6 + i][:, j * T:(j + 1) * T], pool_w[:, 2 * i + j], pooled[:, 2 * i + j],
                               start=True, stop=True)
            mm.then_inc(S["mixed_ready"], 1)
        pe.wait_ge(S["ada_used"], 2 * KD)
        pe.wait_ge(S["proj_taken"], len(first) + len(second))
        sum_columns()
        sum_gate(1)
        pe.wait_ge(S["rope_ready"], 1)
        for i in range(5):
            if i >= 2:
                pe.wait_ge(S["qt_taken"], i - 1)
            for j in range(2 if i < 4 else 1):
                for blk in range(TB):
                    slot = 2 * i + j
                    mm = pe.transpose(bank[2 + i % 2][0:QK, j * T + blk * P:j * T + (blk + 1) * P],
                                      q_y[:, blk, slot * QK:(slot + 1) * QK], ident[:])
            mm.then_inc(S["qt_ready"], 1)
        pe.wait_ge(S["qt_taken"], 5)
        pe.wait_ge(S["mixed_taken"], 2)
        pe.wait_ge(S["ada_bcast"], 2)
        gate_n = len(first) + len(second)
        pe.wait_ge(S["proj_taken"], gate_n)
        for u in range(len(UNITS) + 2):
            if u < len(UNITS):
                pair, qb = UNITS[u]
                nk = P * (qb + 1)
                if u >= 2:
                    pe.wait_ge(S["s_taken"], 2 * (u - 1))
                for h in range(2):
                    if pair < 6:
                        q = qkT[DH * h:DH * (h + 1), pair, qb * P:(qb + 1) * P]
                        k = qkT[DH * h:DH * (h + 1), 6 + pair, 0:nk]
                    else:
                        head = 2 * (pair - 6) + h
                        q, k = qcT[:, head, qb * P:(qb + 1) * P], kcT[:, head, 0:nk]
                    mm = pe.matmul(bank[2 + 2 * (u % 2) + h][:, 0:nk], q, k, start=True, stop=True)
                mm.then_inc(S["s_ready"], 1)
            for n in gates_at(u):
                project(gate_n + n)
            if 1 <= u <= len(UNITS):
                pair, qb = UNITS[u - 1]
                pe.wait_ge(S["p_ready"], u)
                if u >= 2:
                    pe.wait_ge(S["pt_taken"], u - 1)
                for h in range(2):
                    for kb in range(qb + 1):
                        cut = slice(h * T + kb * P, h * T + (kb + 1) * P)
                        mm = pe.transpose(bank[6][:, cut], p_sb[:, (u - 1) % 2, h, kb * P:(kb + 1) * P],
                                          ident[:])
                mm.then_inc(S["pt_ready"], 1)
            if u >= 2:
                pair, qb = UNITS[u - 2]
                pe.wait_ge(S["pt_taken"], u - 1)
                if u >= 3:
                    pe.wait_ge(S["o_taken"], u - 2)
                for h in range(2):
                    head = 2 * pair + h
                    for kb in range(qb + 1):
                        v = (va[:, kb, DH * head:DH * (head + 1)] if pair < 6
                             else vc[:, kb, DH * (head - HEADS_A):DH * (head - HEADS_A + 1)])
                        mm = pe.matmul(bank[7][:, h * DH:(h + 1) * DH], pt_sb[:, u % 2, h, kb * P:(kb + 1) * P],
                                       v, start=(kb == 0), stop=(kb == qb))
                mm.then_inc(S["o_ready"], 1)

        project(len(projections) - 1)
        pe.wait_ge(S["y_ready"], TB)
        for i in range(3):
            for j in range(2):
                for blk in range(TB):
                    mm = pe.transpose(bank[2 + i][:, j * T + blk * P:j * T + (blk + 1) * P],
                                      y_nat[:, blk, (2 * i + j) * P:(2 * i + j + 1) * P], ident[:])
            mm.then_inc(S["yt_ready"], 1)
        pe.wait_ge(S["proj_taken"], len(projections))
        pe.wait_ge(S["yt_taken"], 3)
        for n in range(2 * TB):
            half, blk = n // TB, n % TB
            if n >= 2:
                pe.wait_ge(S["branch_taken"], n - 1)
            load = W_AT["w_o", 512 * half]
            pe.wait_ge(w_loaded[load % W_SLOTS], W_LANDED[load])
            w = w_view(load, 10, 512)
            for br, (src, at) in enumerate(((yT, 0), (ybT, 0), (yT, 2))):
                _, row, rows = W_BRANCH_ROWS[br]
                for j in range(rows):
                    mm = pe.matmul(bank[3 * (n % 2) + br][:], src[:, at + j, blk * P:(blk + 1) * P],
                                   w[:, row + j], start=(j == 0), stop=(j == rows - 1))
            mm.then_inc(S["branch_ready"], 1)
        pe.wait_ge(S["mix_ready"], 1)
        for i in range(4):
            if i >= 2:
                pe.wait_ge(S["mixt_taken"], i - 1)
            for j in range(2):
                for blk in range(TB):
                    mm = pe.transpose(bank[6 + i % 2][:, j * T + blk * P:j * T + (blk + 1) * P],
                                      mix[:, blk, 2 * i + j::KD], ident[:])
            mm.then_inc(S["mixt_ready"], 1)
        pe.wait_ge(S["mixt_taken"], 4)
        for n in range(2 * TB):
            half, blk = n // TB, n % TB
            load = W_AT["w_out", 512 * half]
            pe.wait_ge(w_loaded[load % W_SLOTS], W_LANDED[load])
            w = w_view(load, KD, 512)
            for k in range(KD):
                mm = pe.matmul(bank[n][:], mixT[:, k, blk * P:(blk + 1) * P], w[:, k], start=(k == 0),
                               stop=(k == KD - 1))
            mm.then_inc(S["res_ready"], 1)


def experts_block(nc, t, layer, g, sb, block):
    S, bank, x, ident, ones = g["S"], g["bank"], g["x"], g["ident"], g["ones"]
    gate_ffn, small, raw_loaded = g["gate_ffn"], g["small"], g["raw_loaded"]
    scratch = g["item_scratch"]
    acc = [bank[n] for n in range(4)]
    up_bank, y_bank, gather_bank = bank[4], bank[5:7], bank[7]

    xn_hi = sb("xn_hi", [P, TB, D], F32R)
    xn_lo = sb("xn_lo", [P, TB, D], F32R)
    raw = sb("raw", [P, RAW, 2048])
    w_hi = sb("w_hi", [P, 3, 2048], F32R)
    w_lo = sb("w_lo", [P, 3, 2048], F32R)
    stage = sb("stage", [P, 2, KD, BATCH_ITEMS * SLOTS])
    xn = stage[:, 1].rearrange("p k (a s) -> p (k a s)", a=1).rearrange("p (b d) -> p b d", b=TB)
    hT = stage[:, 0]
    squares = hT.rearrange("p k s -> p (k s)")[:, 0:D]
    xg = sb("xg", [P, 2, KD, 2 * SLOTS], F32R)
    onehot = sb("onehot", [P, TB, BATCH_ITEMS, 2 * SLOTS], F32R)
    pos_rows = sb("pos_rows", [P, 2, BATCH_ITEMS, T], BF16)
    spread = sb("spread", [P, T], F32R)
    t_half = sb("t_half", [SLOTS, 512])
    up_sum = sb("up_sum", [SLOTS, 512])
    silu_sb = sb("silu_sb", [SLOTS, FF])
    g_sb = sb("g_sb", [SLOTS, FF])
    gT = sb("gT", [P, 2, 2 * SLOTS], F32R)
    y_h = sb("y_h", [P, D], F32R)
    y_l = sb("y_l", [P, D], F32R)
    w_slot = sb("w_slot", [P, 2, BATCH_ITEMS])
    router_w = sb("router_w_sb", [P, KD, NE])
    bias_row = sb("bias_row", [P, NE])
    scores = sb("scores", [P, TB, NE])
    sel = sb("sel", [P, TB, NE])
    chosen = sb("chosen", [P, TB, NE])
    weight = sb("weight", [P, TB, NE])
    top = sb("top", [P, TB, 8, GROUP])
    grp = sb("grp", [P, TB, 8])
    versus = sb("versus", [P, 2, 8, 8])
    earlier = sb("earlier", [P, 8, 8])
    earlier_e = sb("earlier_e", [NE, NE])
    iota_i = sb("iota_i", [P, 2, SLOTS], I32)
    slot_id = sb("slot_id", [P, 2 * SLOTS])
    slot_of_row = sb("slot_of_row", [P, 1])
    e_id = sb("e_id", [NE, 1])
    part_i = sb("part_i", [P, 2], I32)
    sums = sb("sums", [P, TB, 2])
    maskT_wT = sb("maskT_wT", [NE, 2, T])
    posT = sb("posT", [NE, T])
    extra = sb("extra", [NE, 8])
    pick = sb("pick", [NE, ITEMS])
    shift = sb("shift", [NE, ITEMS])
    sel_x = sb("sel_x", [NE, 2, MAX_EXTRA])
    item_pos = sb("item_pos", [P, TB, ITEMS])
    item_w = sb("item_w", [P, TB, ITEMS, 2], F32R)
    item_rows = sb("item_rows", [ITEMS, T], BF16)
    extra_e = sb("extra_e", [1, 2 + MAX_EXTRA], I32)
    extra_n = sb("extra_n", [1, 4])
    extra_b = sb("extra_b", [1, 4], I32)
    shared_g = sb("shared_g", [P, TB, FF])
    shared_gT = sb("shared_gT", [P, 2, T])
    scaled = shared_g[:].rearrange("p b f -> p (b f)")

    gather_at = ((bank[7], bank[4], bank[5], bank[6]), (bank[7], bank[6], bank[7]))
    shared_at = [Item(None, 1).raw_slot(c) for c in range(3)]
    scratch_rows = scratch.rearrange("(b i) t -> b (i t)", i=BATCH_ITEMS)

    def piece(c, buf):
        if c < 2:
            return buf.rearrange("p (m k f) -> p m k f", m=2, k=4)
        return buf.rearrange("p (j n) -> p j n", j=2)

    @block.sync
    def _(sp):
        def load_piece(c, slot, w1, w3, w2):
            dst = piece(c, raw[:, slot])
            if c < 2:
                for m, w in enumerate((w1, w3)):
                    sp.dma_start(dst[:, m], w.rearrange("(p k) f -> p k f", k=KD)[:, 4 * c:4 * c + 4]
                                 ).then_inc(raw_loaded[slot], 16)
            else:
                for j in range(2):
                    sp.dma_start(dst[:, j], w2[j * P:(j + 1) * P, :]).then_inc(raw_loaded[slot], 16)

        w1s, w3s, w2s = (t[f"exp_w{i}"].rearrange("l e a b -> (l e) a b") for i in (1, 3, 2))

        def load(c, i, e):
            if not i.early:
                sp.wait_ge(S[LO[c]], i.val(2, -2))
            n = layer * NE + e
            load_piece(c, i.raw_slot(c), w1s[n], w3s[n], w2s[n])

        sp.dma_start(router_w[:], t["router_w"][layer].rearrange("(p k) e -> p k e", k=KD)
                     ).then_inc(S["router_in"], 16)
        sp.dma_start(bias_row[:], t["router_bias"][layer].rearrange("(a e) -> a e", a=1).to_broadcast([P, NE])
                     ).then_inc(S["router_in"], 16)
        for c in range(3):
            load_piece(c, shared_at[c], t["sh_w1"][layer], t["sh_w3"][layer], t["sh_w2"][layer])
        for c in range(3):
            load(c, Item(None, 0, early=True), 0)
        for c in range(2):
            sp.wait_ge(S["shared_used"], c + 1)
            load(c, Item(None, 1, early=True), 1)
        sp.wait_ge(S["tables_ready"], 1)
        sp.dma_start(scratch, item_rows[:]).then_inc(S["scratch_written"], 16)
        for c in range(2):
            load(c, Item(None, 2), 2)
        sp.wait_ge(S["shared_used"], 3)
        load(2, Item(None, 1, early=True), 1)
        sp.wait_ge(S["scratch_written"], 16)
        sp.dma_start(pos_rows[:, 0].rearrange("p i t -> p (i t)"), scratch_rows[0:1].to_broadcast(
            [P, BATCH_ITEMS * T])).then_inc(S["pos_in"], 16)
        for c in range(2):
            load(c, Item(None, 3), 3)
        with sp.Fori(1, NE // BATCH_ITEMS) as b:
            for u in range(BATCH_ITEMS):
                i = Item(b, u)
                load(2, i.next(-2), b * BATCH_ITEMS + (u - 2))
                for c in range(2):
                    load(c, i, b * BATCH_ITEMS + u)
        sp.wait_ge(S["extra_in"], 1)
        batches = sp.value_load(extra_b[0:1, 0:1], min_val=0, max_val=8)

        def expert(n):
            return sp.value_load(extra_e[0:1, bass.ds(n, 1)], min_val=0, max_val=NE - 1)

        with sp.If(batches > 0):
            with sp.Fori(0, batches) as xb:
                for u in range(BATCH_ITEMS):
                    i = Item(xb, NE + u)
                    load(2, i.next(-2), expert(xb * BATCH_ITEMS + u))
                    e = expert(xb * BATCH_ITEMS + (u + 2))
                    for c in range(2):
                        load(c, i, e)
        for u in range(2):
            load(2, Item(batches, NE + u - 2), expert(batches * BATCH_ITEMS + u))

    def has(last, u, ahead):
        return not last or u + ahead < BATCH_ITEMS

    def stage_of(par, nxt, off):
        which, v = (par, nxt)[off // BATCH_ITEMS], off % BATCH_ITEMS
        return stage[:, bass.ds(which, 1), :, v * SLOTS:(v + 1) * SLOTS].rearrange("p a k s -> p (a k) s")

    def lo_half(eng, i, c, h):
        eng.wait_ge(S[HI[c]], i.val(2, h + 1))
        cut = slice(1024 * h, 1024 * (h + 1))
        eng.tensor_tensor(w_lo[:, c, cut], raw[:, i.raw_slot(c), cut], w_hi[:, c, cut].bitcast(F32),
                          ALU.subtract).then_inc(S[LO[c]], 1)

    @block.gpsimd
    def _(pool):
        own = Count(pool, S["pool_own"])
        own.inc(pool.iota(iota_i[:], [[0, 2], [1, SLOTS]], base=0, channel_multiplier=0))
        own.inc(pool.iota(part_i[:, 0:1], [[1, 1]], base=0, channel_multiplier=1))
        own.inc(pool.memset(earlier[:], 1.0))
        own.inc(pool.memset(earlier_e[:], 1.0))
        own.wait()
        own.inc(pool.affine_select(out=earlier[:], in_=earlier[:], compare_op=ALU.is_gt, fill=0.0, base=0,
                                   pattern=[[1, 8], [-1, 8]], channel_multiplier=0))
        own.inc(pool.affine_select(out=earlier_e[:], in_=earlier_e[:], compare_op=ALU.is_gt, fill=0.0, base=0,
                                   pattern=[[1, NE]], channel_multiplier=-1))
        own.wait()

        def xg_high(i, src, batch_done):
            waited_apart(pool, S["pool_own"])
            pool.wait_ge(S["gather_taken"], batch_done)
            if not i.early:
                pool.wait_ge(S["b_free"], i.val(1, -1))
            pool.tensor_copy(xg[:, i.parity, :, 0:SLOTS], src).then_inc(S["xg_hi"], 1)
            pool.wait_ge(S["xg_hi"], i.val(1, 1))

        def xg_low(i, src):
            pool.tensor_tensor(xg[:, i.parity, :, SLOTS:], src, xg[:, i.parity, :, 0:SLOTS].bitcast(F32),
                               ALU.subtract).then_inc(S["xg_lo"], 1)

        def batch(b, last=False):
            par = pool.snap(b % 2)
            nxt = pool.snap((b + 1) % 2)
            for u in range(BATCH_ITEMS):
                i = Item(b, u)
                if has(last, u, 2):
                    lo_half(pool, i.next(2), 1, 1)
                if has(last, u, 3):
                    xg_high(i.next(3), stage_of(par, nxt, u + 3), b * 4 + (8 if u else 4))
                if has(last, u, 1):
                    lo_half(pool, i.next(), 2, 1)
                if has(last, u, 3):
                    xg_low(i.next(3), stage_of(par, nxt, u + 3))

        for n in range(3):
            tokens = stage[:, 0, :, n * SLOTS:(n + 1) * SLOTS]
            xg_high(Item(None, n, early=n < 2), tokens, 4)
            xg_low(Item(None, n), tokens)
        pool.wait_ge(S["extra_in"], 1)
        batches = pool.value_load(extra_b[0:1, 0:1], min_val=0, max_val=8)
        with pool.Fori(0, batches + (NE // BATCH_ITEMS - 1)) as b:
            batch(b)
        batch(pool.snap(batches + (NE // BATCH_ITEMS - 1)), last=True)
    @block.scalar
    def _(act):
        own = Count(act, S["act_own"])

        def hi_half(i, c, h):
            if h == 0:
                act.wait_ge(raw_loaded[i.raw_slot(c)], i.uses_val(32))
                if c == 2 and not i.first:
                    act.wait_ge(S["down_done"], i.val(2, 1))
                elif not i.first:
                    act.wait_ge(S[("a_free", "b_free")[c]], i.val(1, 0))
            cut = slice(1024 * h, 1024 * (h + 1))
            act.activation(w_hi[:, c, cut], raw[:, i.raw_slot(c), cut], ACT.Copy).then_inc(S[HI[c]], 1)

        def take_gather(ready, pair, to, at=gather_bank):
            act.wait_ge(S["gather_ready"], ready)
            waited_apart(act, S["sig_ready"])
            for j in range(2):
                k = 2 * pair + j
                ins = act.activation(to[:, k], at[:, j * 256:(j + 1) * 256].rearrange(
                    "p (a s) -> p a s", a=1), ACT.Identity, bias=g["mod_b"][:, 1, k:k + 1],
                    scale=g["mod_a"][:, 1, k:k + 1])
            ins.then_inc(S["gather_taken"], 1)

        def t_and_silu(i, between=None):
            act.wait_ge(S["b_free"], i.val(1, 1))
            act.activation(t_half[:], up_bank[SLOTS:P, :], ACT.Copy).then_inc(S["t_done"], 1)
            if between:
                between()
            act.wait_ge(S["added"], i.val(1, 1))
            act.activation(silu_sb[:], up_sum[:, 0:FF], ACT.Silu).then_inc(S["silu_done"], 1)

        def take_pair(b, u, par, nxt, last):
            if last:
                return
            if u == 1:
                act.wait_ge(S["xg_lo"], b * BATCH_ITEMS + BATCH_ITEMS)
            to = stage[:, bass.ds(par if u else nxt, 1)].rearrange("p a k s -> p k a s")
            take_gather(b * 4 + (8 + u), (u + 3) % 4, to)

        def gt_high(i):
            act.wait_ge(S["gt_ready"], i.val(1, 1))
            if not i.first:
                act.wait_ge(S["down_done"], i.val(2, 1))
            act.activation(gT[:, :, 0:SLOTS], y_bank[0][:, 0:2 * SLOTS].rearrange("p (j s) -> p j s", j=2),
                           ACT.Copy).then_inc(S["gt_hi"], 1)

        def batch(b, last=False):
            par = act.snap(b % 2)
            nxt = act.snap((b + 1) % 2)
            if not last:
                act.wait_ge(S["pos_in"], b * 16 + 16)
                act.wait_ge(S["s_made"], b * BATCH_ITEMS + 1)
                act.dma_start(pos_rows[:, bass.ds(nxt, 1)].rearrange("p a i t -> p (a i t)"),
                              scratch_rows[bass.ds(b + 1, 1)].to_broadcast([P, BATCH_ITEMS * T])
                              ).then_inc(S["pos_in"], 16)
            for u in range(BATCH_ITEMS):
                i = Item(b, u)
                if has(last, u, 2):
                    hi_half(i.next(2), 1, 1)
                act.wait_ge(S["wslot_moved"], b + 1)
                act.wait_ge(S["down_done"], i.val(2, 2))
                act.wait_ge(S["scatter_done"], i.val(1, 1))
                act.activation(y_h[:, 0:512], y_bank[0][:], ACT.Copy, scale=w_slot[:, 0, u:u + 1]
                               ).then_inc(S["y_hi"], 1)
                if has(last, u, 1):
                    hi_half(i.next(), 2, 0)
                    hi_half(i.next(), 2, 1)
                    gt_high(i.next())
                if has(last, u, 3):
                    hi_half(i.next(3), 0, 0)
                if u != 1:
                    take_pair(b, u, par, nxt, last)
                if has(last, u, 2):
                    t_and_silu(i.next(2), (lambda: hi_half(i.next(3), 0, 1)) if has(last, u, 3) else None)
                if has(last, u, 3):
                    hi_half(i.next(3), 1, 0)
                if u == 1:
                    take_pair(b, u, par, nxt, last)

        g["norm_act"](act, own, squares)
        act.wait_ge(S["norm_ready"], TB)
        for blk in range(TB):
            act.activation(xn_hi[:, blk], xn[:, blk], ACT.Copy).then_inc(S["norm_act"], 1)
        g["modulate_act"](act, hT, bank[4:8], 1)
        items = [Item(None, n) for n in range(3)]
        act.wait_ge(S["logits_ready"], 1)
        act.activation(scores[:], gather_bank[:, 0:TB * NE].rearrange("p (b e) -> p b e", b=TB),
                       ACT.Sigmoid).then_inc(S["sig_ready"], 1)
        for blk in range(TB):
            hi_half(items[0], blk, 0)
            hi_half(items[0], blk, 1)
            act.wait_ge(S["shared_up"], blk + 1)
            act.activation(shared_g[:, blk], bank[4 + blk][:, 0:FF], ACT.Silu).then_inc(S["shared_act"], 1)
        hi_half(items[0], 2, 0)
        hi_half(items[0], 2, 1)
        act.wait_ge(S["shared_gt"], 1)
        act.activation(shared_gT[:], bank[6][:].rearrange("p (j t) -> p j t", j=2), ACT.Copy
                       ).then_inc(S["shared_gt_taken"], 1)
        for pair in range(4):
            take_gather(pair + 1, pair, stage[:, 0:1].rearrange("p a k s -> p k a s"), gather_at[0][pair])
        hi_half(items[1], 0, 0)
        hi_half(items[1], 0, 1)
        for pair in range(2):
            take_gather(pair + 5, pair, stage[:, 1:2].rearrange("p a k s -> p k a s"), gather_at[1][pair])
        t_and_silu(items[0])
        hi_half(items[1], 1, 0)
        hi_half(items[1], 1, 1)
        gt_high(items[0])
        for pair in range(2, 3):
            take_gather(pair + 5, pair, stage[:, 1:2].rearrange("p a k s -> p k a s"), gather_at[1][pair])
        hi_half(items[2], 0, 0)
        t_and_silu(items[1])
        hi_half(items[2], 0, 1)
        hi_half(items[2], 1, 0)
        act.wait_ge(S["extra_in"], 1)
        batches = act.value_load(extra_b[0:1, 0:1], min_val=0, max_val=8)
        with act.Fori(0, batches + (NE // BATCH_ITEMS - 1)) as b:
            batch(b)
        batch(act.snap(batches + (NE // BATCH_ITEMS - 1)), last=True)

    @block.vector
    def _(dve):
        own = Count(dve, S["dve_own"])

        def add_halves(i):
            dve.wait_ge(S["t_done"], i.val(1, 1))
            if not i.first:
                dve.wait_ge(S["mul_done"], i.val(1, 0))
            dve.tensor_tensor(up_sum[:], up_bank[0:SLOTS, :], t_half[:], ALU.add).then_inc(S["added"], 1)

        def multiply(i):
            dve.wait_ge(S["silu_done"], i.val(1, 1))
            if not i.first:
                dve.wait_ge(S["gt_ready"], i.val(1, 0))
            dve.tensor_tensor(g_sb[:], silu_sb[:], up_sum[:, FF:], ALU.mult).then_inc(S["mul_done"], 1)

        def gt_low(i):
            dve.wait_ge(S["gt_hi"], i.val(1, 1))
            dve.tensor_tensor(gT[:, :, SLOTS:], y_bank[0][:, 0:2 * SLOTS].rearrange("p (j s) -> p j s", j=2),
                              gT[:, :, 0:SLOTS].bitcast(F32), ALU.subtract).then_inc(S["gt_lo"], 1)

        def make_onehots(columns):
            for blk in range(TB):
                ins = dve.tensor_tensor(onehot[:, blk], slot_id[:, None, :].to_broadcast([P, BATCH_ITEMS, 2 * SLOTS]),
                                        item_pos[:, blk, columns, None].to_broadcast([P, BATCH_ITEMS, 2 * SLOTS]),
                                        ALU.is_equal)
            ins.then_inc(S["onehot_made"], 1)

        def take_wslot(b1):
            dve.wait_ge(S["wslot_ready"], b1)
            dve.tensor_reduce(w_slot[:, 1], gather_bank[:, 0:2 * BATCH_ITEMS].rearrange("p (i c) -> p i c", c=2),
                              AX_X, ALU.add).then_inc(S["wslot_made"], 1)

        def move_wslot(b1):
            dve.wait_ge(S["wslot_made"], b1)
            dve.tensor_copy(w_slot[:, 0], w_slot[:, 1]).then_inc(S["wslot_moved"], 1)

        def batch(b, last=False):
            par = dve.snap(b % 2)
            for u in range(BATCH_ITEMS):
                i = Item(b, u)
                if u == 0:
                    dve.wait_ge(S["pos_in"], b * 16 + 16)
                dve.wait_ge(S["scatter_done"], i.val(1, 1))
                dve.tensor_scalar(spread[:], pos_rows[:, bass.ds(par, 1), u].rearrange("p a t -> p (a t)"),
                                  slot_of_row[:], None, ALU.is_equal).then_inc(S["s_made"], 1)
                for half in range(2):
                    cut = slice(512 * half, 512 * (half + 1))
                    if half == 1:
                        dve.wait_ge(S["down_done"], i.val(2, 3))
                        dve.tensor_scalar(y_h[:, cut], y_bank[1][:], w_slot[:, 0, u:u + 1], None, ALU.mult
                                          ).then_inc(S["y_hi"], 1)
                    dve.wait_ge(S["y_hi"], i.val(2, half + 1))
                    dve.scalar_tensor_tensor(y_l[:, cut], y_bank[half][:], w_slot[:, 0, u:u + 1],
                                             y_h[:, cut].bitcast(F32), ALU.mult, ALU.subtract
                                             ).then_inc(S["y_lo"], 1)
                if has(last, u, 1):
                    lo_half(dve, i.next(), 2, 0)
                    gt_low(i.next())
                if u == 1 and not last:
                    take_wslot(b + 2)
                    make_onehots(bass.ds(b * BATCH_ITEMS + 2 * BATCH_ITEMS, BATCH_ITEMS))
                if u == BATCH_ITEMS - 1 and not last:
                    dve.wait_ge(S["y_lo"], i.val(2, 4))
                    move_wslot(b + 2)
                if has(last, u, 3):
                    lo_half(dve, i.next(3), 0, 0)
                if has(last, u, 2):
                    add_halves(i.next(2))
                if has(last, u, 3):
                    lo_half(dve, i.next(3), 0, 1)
                if has(last, u, 2):
                    multiply(i.next(2))
                if has(last, u, 3):
                    lo_half(dve, i.next(3), 1, 0)

        dve.nop().then_inc(S["s_made"], 1)
        dve.nop().then_inc(S["y_lo"], 2)
        g["norm_dve"](dve, own)
        for blk in range(TB):
            dve.tensor_scalar(xn[:, blk], x[:, blk], small[:, 4 + blk:5 + blk], None,
                              ALU.mult).then_inc(S["norm_ready"], 1)
        for blk in range(TB):
            dve.wait_ge(S["norm_act"], 3 + blk)
            dve.tensor_tensor(xn_lo[:, blk], xn[:, blk], xn_hi[:, blk].bitcast(F32), ALU.subtract
                              ).then_inc(S["norm_dve"], 1)
        dve.wait_ge(S["pool_own"], 6)
        own.inc(dve.tensor_copy(slot_id[:], iota_i[:].rearrange("p a s -> p (a s)")))
        own.inc(dve.tensor_copy(e_id[:], part_i[0:NE, 0:1]))
        own.step(dve.tensor_scalar(part_i[:, 1:2], part_i[:, 0:1], SLOTS - 1, None, ALU.bitwise_and))
        own.step(dve.tensor_copy(slot_of_row[:], part_i[:, 1:2]))
        items = [Item(None, n) for n in range(3)]

        dve.wait_ge(S["router_in"], 32)
        dve.wait_ge(S["sig_ready"], 1)
        own.step(dve.tensor_tensor(sel[:], scores[:], bias_row[:, None, :].to_broadcast([P, TB, NE]), ALU.add))
        for blk in range(TB):
            for gr in range(8):
                own.inc(dve.max(top[:, blk, gr], sel[:, blk, gr * GROUP:(gr + 1) * GROUP]))
        own.wait()
        own.step(dve.tensor_tensor(grp[:], top[:, :, :, 0], top[:, :, :, 1], ALU.add))
        for blk in range(TB):
            other = grp[:, blk, None, :].to_broadcast([P, 8, 8])
            this = grp[:, blk, :, None].to_broadcast([P, 8, 8])
            own.inc(dve.tensor_tensor(versus[:, 0], other, this, ALU.is_gt))
            own.step(dve.tensor_tensor(versus[:, 1], other, this, ALU.is_equal))
            own.step(dve.tensor_tensor(versus[:, 1], versus[:, 1], earlier[:], ALU.mult))
            own.step(dve.tensor_tensor(versus[:, 0], versus[:, 0], versus[:, 1], ALU.add))
            own.step(dve.tensor_reduce(grp[:, blk], versus[:, 0], AX_X, ALU.add))
            own.step(dve.tensor_scalar(grp[:, blk], grp[:, blk], float(TOPK_GROUPS), NEG, ALU.is_ge, ALU.mult))
            own.step(dve.tensor_tensor(sel[:, blk].rearrange("p (g e) -> p g e", g=8),
                                       sel[:, blk].rearrange("p (g e) -> p g e", g=8),
                                       grp[:, blk, :, None].to_broadcast([P, 8, GROUP]), ALU.add))
            own.step(dve.max(top[:, blk, 0], sel[:, blk]))
            own.step(dve.match_replace(chosen[:, blk], top[:, blk, 0], sel[:, blk], TAKEN))
            own.step(dve.tensor_scalar(chosen[:, blk], chosen[:, blk], 0.5 * TAKEN, None, ALU.is_le))
            own.step(dve.tensor_tensor(weight[:, blk], chosen[:, blk], scores[:, blk], ALU.mult))
            own.step(dve.tensor_reduce(sums[:, blk, 0:1], weight[:, blk], AX_X, ALU.add))
            own.step(dve.reciprocal(sums[:, blk, 1:2], sums[:, blk, 0:1]))
            own.step(dve.tensor_scalar(weight[:, blk], weight[:, blk], sums[:, blk, 1:2], ROUTED_SCALE,
                                       ALU.mult, ALU.mult))
        dve.nop().then_inc(S["sel_ready"], 1)

        dve.wait_ge(S["selt_ready"], 1)
        own.step(dve.tensor_copy(maskT_wT[:], bank[7][0:NE, :].rearrange("p (m t) -> p m t", m=2)))
        own.step(dve.tensor_tensor_scan(posT[:], ones[0:NE, :], maskT_wT[:, 0], 0.0, ALU.mult, ALU.add))
        count = posT[:, T - 1:T]
        for n in range(3):
            own.inc(dve.tensor_scalar(extra[:, n:n + 1], count, float(SLOTS * (n + 1)), None, ALU.is_gt))
        own.wait()
        own.step(dve.tensor_tensor(extra[:, 0:1], extra[:, 0:1], extra[:, 1:2], ALU.add))
        own.step(dve.tensor_tensor(extra[:, 0:1], extra[:, 0:1], extra[:, 2:3], ALU.add))
        own.step(dve.scalar_tensor_tensor(posT[:], posT[:], -1.0 - NOT_HERE, maskT_wT[:, 0], ALU.add, ALU.mult))
        own.step(dve.tensor_scalar(posT[:], posT[:], NOT_HERE - NO_ITEM, None, ALU.add))
        own.inc(dve.tensor_copy(pick[:, 0:NE], ident[0:NE, 0:NE]))
        own.step(dve.memset(shift[:, 0:NE], 0.0))
        dve.nop().then_inc(S["counts_made"], 1)
        dve.wait_ge(S["counts_summed"], 1)
        own.step(dve.tensor_copy(extra[:, 3:4], bank[7][0:NE, 0:1]))
        own.inc(dve.tensor_copy(extra_n[0:1, 0:1], bank[7][0:1, 1:2]))
        own.step(dve.tensor_tensor(extra[:, 4:5], extra[:, 3:4], extra[:, 0:1], ALU.add))
        ids = slot_id[0:NE, 0:MAX_EXTRA]
        own.inc(dve.tensor_scalar(sel_x[:, 0], ids, extra[:, 3:4], None, ALU.is_ge))
        own.step(dve.tensor_scalar(sel_x[:, 1], ids, extra[:, 4:5], None, ALU.is_lt))
        own.step(dve.tensor_tensor(pick[:, NE:], sel_x[:, 0], sel_x[:, 1], ALU.mult))
        own.step(dve.tensor_scalar(sel_x[:, 0], ids, extra[:, 3:4], None, ALU.subtract))
        own.step(dve.tensor_scalar(sel_x[:, 0], sel_x[:, 0], -float(SLOTS), -float(SLOTS), ALU.mult, ALU.add))
        own.step(dve.tensor_tensor(shift[:, NE:], sel_x[:, 0], pick[:, NE:], ALU.mult))
        own.step(dve.tensor_scalar(extra_n[0:1, 0:1], extra_n[0:1, 0:1], float(BATCH_ITEMS - 1), None, ALU.add))
        own.step(dve.tensor_copy(extra_b[0:1, 1:2], extra_n[0:1, 0:1]))
        own.step(dve.tensor_scalar(extra_b[0:1, 0:1], extra_b[0:1, 1:2], 2, None, ALU.arith_shift_right))
        dve.nop().then_inc(S["counts_made"], 1)
        for blk in range(TB):
            dve.wait_ge(S["shared_act"], blk + 1)
            dve.tensor_tensor(shared_g[:, blk], shared_g[:, blk], bank[4 + blk][:, FF:], ALU.mult
                              ).then_inc(S["shared_g"], 1)
        dve.wait_ge(S["tables_summed"], 1)
        own.inc(dve.tensor_copy(extra_e[:, 2:], bank[7][0:1, 0:MAX_EXTRA]))
        for n in range(2):
            own.inc(dve.memset(extra_e[:, n:n + 1], NE - 2 + n))
        own.wait()
        dve.nop().then_inc(S["extra_in"], 1)
        pos = up_bank[:, 0:TB * P].rearrange("p (b i) -> p b i", b=TB)[:, :, 0:ITEMS]
        wts = up_bank[:, TB * P:2 * TB * P].rearrange("p (b i) -> p b i", b=TB)[:, :, 0:ITEMS]
        own.inc(dve.tensor_scalar(item_pos[:], pos, NO_ITEM, None, ALU.add))
        own.step(dve.tensor_copy(item_w[:, :, :, 0], wts))
        own.inc(dve.tensor_tensor(item_w[:, :, :, 1], wts, item_w[:, :, :, 0].bitcast(F32), ALU.subtract))
        own.step(dve.tensor_scalar(item_rows[:], y_bank[0][0:ITEMS, 0:T], NO_ITEM, 256.0, ALU.add, ALU.min))
        dve.nop().then_inc(S["tables_ready"], 1)

        make_onehots(slice(0, BATCH_ITEMS))
        for c in range(3):
            for h in range(2):
                lo_half(dve, items[0], c, h)
        take_wslot(1)
        move_wslot(1)
        make_onehots(slice(BATCH_ITEMS, 2 * BATCH_ITEMS))
        for h in range(2):
            lo_half(dve, items[1], 0, h)
        add_halves(items[0])
        multiply(items[0])
        for h in range(2):
            lo_half(dve, items[1], 1, h)
        gt_low(items[0])
        lo_half(dve, items[2], 0, 0)
        add_halves(items[1])
        lo_half(dve, items[2], 0, 1)
        multiply(items[1])
        lo_half(dve, items[2], 1, 0)
        dve.wait_ge(own.sem, own.n)
        batches = dve.value_load(extra_b[0:1, 0:1], min_val=0, max_val=8)
        with dve.Fori(0, batches + (NE // BATCH_ITEMS - 1)) as b:
            batch(b)
        batch(dve.snap(batches + (NE // BATCH_ITEMS - 1)), last=True)
        dve.wait_ge(S["pos_in"], batches * 16 + NE // BATCH_ITEMS * 16)
        dve.wait_ge(S["acc_ready"], 1)
        for blk in range(TB):
            for half in range(2):
                cut = slice(512 * half, 512 * (half + 1))
                own.step(dve.tensor_tensor(scaled[:], gate_ffn[:, cut], acc[2 * blk + half][:], ALU.mult))
                own.step(dve.tensor_tensor(x[:, blk, cut], x[:, blk, cut], scaled[:], ALU.add))

    @block.tensor
    def _(pe):
        def up(i, c):
            pe.wait_ge(S[LO[c]], i.val(2, 2))
            if c == 0:
                pe.wait_ge(S["xg_lo"], i.val(1, 1))
                if not i.first:
                    pe.wait_ge(S["added"], i.val(1, 0))
            for kk in range(4):
                k = 4 * c + kk
                if c == 0 and kk == 3 and i.b is not None:
                    pe.wait_ge(S["y_lo"], i.val(2, -1))
                for w in (w_hi, w_lo):
                    mm = pe.matmul(up_bank[:], xg[:, i.parity, k], piece(c, w[:, c])[:, :, kk],
                                   start=(k == 0 and w is w_hi), stop=(k == KD - 1 and w is w_lo))
            mm.then_inc(S["a_free" if c == 0 else "b_free"], 1)

        def down(i):
            pe.wait_ge(S["gt_lo"], i.val(1, 1))
            pe.wait_ge(S["lo_c"], i.val(2, 2))
            for half in range(2):
                for j in range(2):
                    for w in (w_hi, w_lo):
                        mm = pe.matmul(y_bank[half][:], gT[:, j], piece(2, w[:, 2])[:, j, 512 * half:512 * half + 512],
                                       start=(j == 0 and w is w_hi), stop=(j == 1 and w is w_lo))
                mm.then_inc(S["down_done"], 1)

        def scatter(i):
            pe.wait_ge(S["s_made"], i.val(1, 2))
            pe.wait_ge(S["y_lo"], i.val(2, 4))
            for blk in range(TB):
                for half in range(2):
                    for y in (y_h, y_l):
                        mm = pe.matmul(acc[2 * blk + half][:], spread[:, blk * P:(blk + 1) * P],
                                       y[:, 512 * half:512 * half + 512], start=False, stop=False,
                                       skip_group_check=True)
            mm.then_inc(S["scatter_done"], 1)

        def turn_g(i):
            waited_apart(pe, S["logits_ready"])
            pe.wait_ge(S["mul_done"], i.val(1, 1))
            for j in range(2):
                mm = pe.transpose(y_bank[0][:, j * SLOTS:(j + 1) * SLOTS], g_sb[:, j * P:(j + 1) * P],
                                  ident[0:SLOTS, 0:SLOTS])
            mm.then_inc(S["gt_ready"], 1)

        def shared_down(blk):
            for half in range(2):
                for j in range(2):
                    mm = pe.matmul(acc[2 * blk + half][:], shared_gT[:, j, blk * P:(blk + 1) * P],
                                   piece(2, raw[:, shared_at[2]])[:, j, 512 * half:512 * half + 512], start=(j == 0),
                                   stop=False, skip_group_check=True)
            return mm

        def gather(pair, to=gather_bank):
            for j in range(2):
                k = 2 * pair + j
                for blk in range(TB):
                    for xs in (xn_hi, xn_lo):
                        mm = pe.matmul(to[:, 256 * j:256 * (j + 1)], xs[:, blk, k::KD],
                                       onehot[:, blk, :, 0:SLOTS],
                                       start=(blk == 0 and xs is xn_hi), stop=(blk == TB - 1 and xs is xn_lo))
            mm.then_inc(S["gather_ready"], 1)

        def slot_weights(taken, column):
            pe.wait_ge(S["gather_taken"], taken)
            for it in range(BATCH_ITEMS):
                for blk in range(TB):
                    mm = pe.matmul(gather_bank[:, 2 * it:2 * it + 2],
                                   onehot[:, blk, it], item_w[:, blk, column(it)],
                                   start=(blk == 0), stop=(blk == TB - 1))
            mm.then_inc(S["wslot_ready"], 1)

        def batch(b, last=False):
            for u in range(BATCH_ITEMS):
                i = Item(b, u)
                down(i)
                if has(last, u, 2):
                    up(i.next(2), 0)
                    turn_g(i.next())
                if u != 1 and not last:
                    pe.wait_ge(S["gather_taken"], b * 4 + (7 + u))
                    gather((u + 3) % 4)
                if has(last, u, 2):
                    up(i.next(2), 1)
                scatter(i)
                if has(last, u, 1) and not has(last, u, 2):
                    turn_g(i.next())
                if u == 0 and not last:
                    slot_weights(b * 4 + 8, lambda it: pe.snap(b * 4 + (4 + it)))
                if u == 1 and not last:
                    pe.wait_ge(S["onehot_made"], b + 3)
                    pe.wait_ge(S["wslot_made"], b + 2)
                    gather(0)

        pe.nop().then_inc(S["down_done"], 1)
        pe.nop().then_inc(S["scatter_done"], 1)
        pe.wait_ge(S["norm_ready"], TB)
        g["turn_pe"](pe, xn, bank[4:8])
        pe.wait_ge(S["hT_ready"], 1)
        pe.wait_ge(S["router_in"], 32)
        for blk in range(TB):
            for k in range(KD):
                mm = pe.matmul(bank[7][:, blk * NE:(blk + 1) * NE], hT[:, k, blk * P:(blk + 1) * P], router_w[:, k],
                               start=(k == 0), stop=(k == KD - 1))
        mm.then_inc(S["logits_ready"], 1)
        def shared_up(blk, c):
            pe.wait_ge(raw_loaded[shared_at[c]], 32)
            for kk in range(4):
                k = 4 * c + kk
                mm = pe.matmul(bank[4 + blk][:], hT[:, k, blk * P:(blk + 1) * P],
                               piece(c, raw[:, shared_at[c]])[:, :, kk], start=(k == 0), stop=(k == KD - 1))
            return mm

        shared_up(0, 0)
        shared_up(0, 1).then_inc(S["shared_up"], 1)
        pe.wait_ge(S["sel_ready"], 1)
        for m, src in enumerate((chosen, weight)):
            for blk in range(TB):
                mm = pe.transpose(bank[7][0:NE, m * T + blk * P:m * T + (blk + 1) * P], src[:, blk], ident[:])
        mm.then_inc(S["selt_ready"], 1)
        shared_up(1, 0)
        pe.wait_ge(S["counts_made"], 1)
        pe.matmul(bank[7][0:NE, 0:1], earlier_e[:], extra[:, 0:1], start=True, stop=True)
        pe.matmul(bank[7][:, 1:2], ones[0:NE, 0:P], extra[:, 0:1], start=True, stop=True
                  ).then_inc(S["counts_summed"], 1)
        shared_up(1, 1).then_inc(S["shared_up"], 1)
        pe.wait_ge(S["shared_up"], 2)
        pe.sem_inc(S["shared_used"], 2)
        pe.wait_ge(S["shared_g"], 2)
        pe.wait_ge(S["counts_made"], 2)
        for blk in range(TB):
            cut = slice(blk * P, blk * P + ITEMS)
            pe.matmul(up_bank[:, cut], posT[:, blk * P:(blk + 1) * P], pick[:], start=True, stop=False)
            pe.matmul(up_bank[:, cut], ones[0:NE, 0:P], shift[:], start=False, stop=True)
        for blk in range(TB):
            cut = slice((TB + blk) * P, (TB + blk) * P + ITEMS)
            pe.matmul(up_bank[:, cut], maskT_wT[:, 1, blk * P:(blk + 1) * P], pick[:], start=True, stop=True)
        pe.matmul(y_bank[0][0:ITEMS, 0:T], pick[:], posT[:], start=True, stop=False)
        pe.matmul(y_bank[0][0:ITEMS, 0:T], shift[:], ones[0:NE, :], start=False, stop=True)
        pe.matmul(bank[7][0:1, 0:MAX_EXTRA], e_id[:], pick[:, NE:], start=True, stop=True
                  ).then_inc(S["tables_summed"], 1)
        pe.wait_ge(S["norm_dve"], 1 + TB)
        items = [Item(None, n) for n in range(2)]
        for blk in range(TB):
            for j in range(2):
                mm = pe.transpose(bank[6][:, j * T + blk * P:j * T + (blk + 1) * P],
                                  shared_g[:, blk, j * P:(j + 1) * P], ident[:])
        mm.then_inc(S["shared_gt"], 1)
        pe.wait_ge(S["shared_gt_taken"], 1)
        pe.wait_ge(raw_loaded[shared_at[2]], 32)
        shared_down(0)
        pe.wait_ge(S["onehot_made"], 1)
        for pair in range(4):
            gather(pair, gather_at[0][pair])
        slot_weights(1, lambda it: it)
        shared_down(1).then_inc(S["shared_used"], 1)
        pe.wait_ge(S["gather_taken"], 4)
        up(items[0], 0)
        up(items[0], 1)
        pe.wait_ge(S["onehot_made"], 2)
        pe.wait_ge(S["wslot_made"], 1)
        for pair in range(3):
            if pair >= 2:
                pe.wait_ge(S["gather_taken"], pair + 3)
            gather(pair, gather_at[1][pair])
            if pair == 1:
                turn_g(items[0])
        up(items[1], 0)
        up(items[1], 1)
        pe.wait_ge(S["gather_taken"], 6)
        pe.wait_ge(S["extra_in"], 1)
        batches = pe.value_load(extra_b[0:1, 0:1], min_val=0, max_val=8)
        with pe.Fori(0, batches + (NE // BATCH_ITEMS - 1)) as b:
            batch(b)
        batch(pe.snap(batches + (NE // BATCH_ITEMS - 1)), last=True)
        pe.wait_ge(S["scatter_done"], batches * 4 + (NE + 1))
        pe.nop().then_inc(S["acc_ready"], 1)


def waited_apart(eng, sem):
    eng.wait_ge(sem, 1)


class Item:

    def __init__(self, b, off, early=False):
        self.b, self.off = b, off
        self.early = early
        self.first = b is None and off == 0

    def val(self, a, c):
        return a * self.off + c if self.b is None else self.b * (BATCH_ITEMS * a) + (a * self.off + c)

    def next(self, n=1):
        return Item(self.b, self.off + n)

    @property
    def parity(self):
        return self.off % 2

    def raw_slot(self, c):
        return 3 * self.parity + c if c < 2 else 5 - 3 * self.parity

    def uses_val(self, a):
        n = self.off // 2 + 1 + self.parity
        return a * n if self.b is None else self.b * (BATCH_ITEMS // 2 * a) + a * n


_INS = ["x", "c", "positions", "ada_mix_w", "ada_mix_b", "norm_mix_g", "w_in", "pool_w", "pool_scale",
        "cq_norm_g", "ckv_norm_g", "w_uq", "w_ukv", "w_oa", "w_ob", "w_oc", "w_out", "ada_ffn_w", "ada_ffn_b",
        "norm_ffn_g", "router_w", "router_bias", "exp_w1", "exp_w3", "exp_w2", "sh_w1", "sh_w3", "sh_w2",
        "final_g"]


def kernel(**inputs):
    import concourse.bacc as bacc
    from concourse.bass_utils import run_bass_kernel_spmd

    nc = bacc.Bacc("TRN2", target_bir_lowering=False, num_devices=1)
    arrays, tensors = {}, {}
    for name in _INS:
        a = np.ascontiguousarray(inputs[name])
        arrays[f"in_{name}"] = a
        tensors[name] = nc.dram_tensor(f"in_{name}", a.shape, mybir.dt.from_np(a.dtype), kind="ExternalInput").ap()
    out = nc.dram_tensor("out_y", (1, T, D), F32, kind="ExternalOutput").ap()
    hybrid_trunk(nc, tensors, out)
    r = run_bass_kernel_spmd(nc, [arrays], core_ids=[0])
    return r.results[0]["out_y"]
```
